# Optimizing a Trainium2 kernel written in Bass

```python
import math
import jax, jax.numpy as jnp
from jax import lax
import numpy as np

D_MODEL = 1024
BATCH = 1
SEQ = 256
DEPTH = 2

GRID_W = 64
Q_BLOCK = 128
EPS = 1e-6

A_HEADS = 8
A_KV_HEADS = 2
A_GROUP = A_HEADS // A_KV_HEADS
A_HEAD_DIM = 64
AXIAL_THETA = 10000.0

B_HEADS = 8
B_QK_DIM = 32
B_V_DIM = 2 * B_QK_DIM
B_ROT_DIM = B_QK_DIM // 4
ROPE_THETA = 500000.0

C_HEADS = 8
C_Q_RANK = 384
C_KV_RANK = 256
C_NOPE_DIM = 64
C_ROPE_DIM = 32
C_V_DIM = 64
MLA_THETA = 10000.0

N_BRANCH = 3
BRANCH_W = 512
D_FF = 4 * D_MODEL

A_Q_W = A_HEADS * A_HEAD_DIM
A_KV_W = A_KV_HEADS * A_HEAD_DIM
B_QK_W = B_HEADS * 2 * B_QK_DIM
B_V_W = B_HEADS * B_V_DIM
GATE_W = N_BRANCH * D_MODEL
IN_SIZES = (A_Q_W, A_KV_W, A_KV_W, B_QK_W, B_QK_W, B_V_W, C_Q_RANK, C_KV_RANK, C_ROPE_DIM, GATE_W)
IN_COLS = A_Q_W + 2 * A_KV_W + 2 * B_QK_W + B_V_W + C_Q_RANK + C_KV_RANK + C_ROPE_DIM + GATE_W


def _rms_norm(x, g):
    xf = x.astype(jnp.float32)
    y = xf * lax.rsqrt(jnp.mean(xf * xf, axis=-1, keepdims=True) + EPS)
    return (y * g.astype(jnp.float32)).astype(x.dtype)

def _angles(pos, dim, theta):
    inv_freq = theta ** (-jnp.arange(0, dim, 2, dtype=jnp.float32) / dim)
    return pos.astype(jnp.float32)[:, None] * inv_freq[None, :]

def _rotate(x, ang):
    cos = jnp.cos(ang)[:, None, :].astype(x.dtype)
    sin = jnp.sin(ang)[:, None, :].astype(x.dtype)
    x1, x2 = jnp.split(x, 2, axis=-1)
    return jnp.concatenate([x1 * cos - x2 * sin, x2 * cos + x1 * sin], axis=-1)

def _softmax_f32(s):
    return jax.nn.softmax(s.astype(jnp.float32), axis=-1)

def _sweep_query_blocks(block_fn, *qs):
    b, s = qs[0].shape[:2]
    nb = s // Q_BLOCK
    blocked = tuple(jnp.swapaxes(q.reshape((b, nb, Q_BLOCK) + q.shape[2:]), 0, 1) for q in qs)
    out = lax.map(lambda qb: block_fn(*qb), blocked)
    out = jnp.swapaxes(out, 0, 1)
    return out.reshape((b, s) + out.shape[3:])

def _split_columns(p):
    out, start = [], 0
    for n in IN_SIZES:
        out.append(p[..., start:start + n])
        start += n
    return out

def _gqa_axial(q, k, v, q_g, k_g, row_ang, col_ang):
    b, s = q.shape[:2]
    half = A_HEAD_DIM // 2

    def axial(t):
        return jnp.concatenate([_rotate(t[..., :half], row_ang), _rotate(t[..., half:], col_ang)], axis=-1)

    q = axial(_rms_norm(q, q_g)) * (A_HEAD_DIM ** -0.5)
    k = axial(_rms_norm(k, k_g))
    q = q.reshape(b, s, A_KV_HEADS, A_GROUP, A_HEAD_DIM)

    def block(qb):
        sc = jnp.einsum('bqkgd,bskd->bkgqs', qb, k)
        p = _softmax_f32(sc).astype(v.dtype)
        return jnp.einsum('bkgqs,bskd->bqkgd', p, v)

    o = _sweep_query_blocks(block, q)
    return o.reshape(b, s, A_HEADS * A_HEAD_DIM)

def _diff_attention(q, k, v, lam_p, sub_g, lambda_init, rot_ang):
    b, s = q.shape[:2]

    def partial_rot(t):
        t = t.reshape(b, s, B_HEADS * 2, B_QK_DIM)
        t = jnp.concatenate([_rotate(t[..., :B_ROT_DIM], rot_ang), t[..., B_ROT_DIM:]], axis=-1)
        return t.reshape(b, s, B_HEADS, 2, B_QK_DIM)

    q = partial_rot(q) * (B_QK_DIM ** -0.5)
    k = partial_rot(k)
    v = v.reshape(b, s, B_HEADS, B_V_DIM)
    lf = lam_p.astype(jnp.float32)
    lam = jnp.exp(jnp.sum(lf[0] * lf[1])) - jnp.exp(jnp.sum(lf[2] * lf[3])) + lambda_init

    def block(qb):
        sc = jnp.einsum('bqhcd,bshcd->bhcqs', qb, k)
        p = _softmax_f32(sc)
        p = (p[:, :, 0] - lam * p[:, :, 1]).astype(v.dtype)
        return jnp.einsum('bhqs,bshe->bqhe', p, v)

    o = _sweep_query_blocks(block, q)
    o = _rms_norm(o, sub_g) * (1.0 - lambda_init)
    return o.reshape(b, s, B_HEADS * B_V_DIM)

def _mla(c_q, c_kv, k_r, q_g, kv_g, w_uq, w_ukv, ang):
    b, s = c_q.shape[:2]
    q = jnp.einsum('bsr,rn->bsn', _rms_norm(c_q, q_g), w_uq).reshape(b, s, C_HEADS, C_NOPE_DIM + C_ROPE_DIM)
    kv = jnp.einsum('bsr,rn->bsn', _rms_norm(c_kv, kv_g), w_ukv).reshape(b, s, C_HEADS, C_NOPE_DIM + C_V_DIM)
    scale = (C_NOPE_DIM + C_ROPE_DIM) ** -0.5
    q_nope = q[..., :C_NOPE_DIM] * scale
    q_rope = _rotate(q[..., C_NOPE_DIM:], ang) * scale
    k_nope, v = kv[..., :C_NOPE_DIM], kv[..., C_NOPE_DIM:]
    k_rope = _rotate(k_r[:, :, None, :], ang)[:, :, 0]

    def block(qn, qr):
        sc = jnp.einsum('bqhd,bshd->bhqs', qn, k_nope) + jnp.einsum('bqhr,bsr->bhqs', qr, k_rope)
        p = _softmax_f32(sc).astype(v.dtype)
        return jnp.einsum('bhqs,bshe->bqhe', p, v)

    o = _sweep_query_blocks(block, q_nope, q_rope)
    return o.reshape(b, s, C_HEADS * C_V_DIM)

def first_inputs(seed: int = 0) -> dict:
    key = jax.random.key(seed)
    ks = jax.random.split(key, 20)
    f32 = jnp.float32

    def nrm(k, shape, scale):
        return jax.random.normal(k, shape, f32) * scale

    def gain(k, shape):
        return 1.0 + 0.02 * jax.random.normal(k, shape, f32)

    return {
        'x': jax.random.normal(ks[0], (BATCH, SEQ, D_MODEL), f32),
        'ln1_g': gain(ks[1], (DEPTH, D_MODEL)),
        'w_in': nrm(ks[2], (DEPTH, D_MODEL, IN_COLS), D_MODEL ** -0.5),
        'a_q_norm': gain(ks[3], (DEPTH, A_HEAD_DIM)),
        'a_k_norm': gain(ks[4], (DEPTH, A_HEAD_DIM)),
        'b_lambda': nrm(ks[5], (DEPTH, 4, B_QK_DIM), 0.1),
        'b_subln': gain(ks[6], (DEPTH, B_V_DIM)),
        'c_q_norm': gain(ks[7], (DEPTH, C_Q_RANK)),
        'c_kv_norm': gain(ks[8], (DEPTH, C_KV_RANK)),
        'c_w_uq': nrm(ks[9], (DEPTH, C_Q_RANK, C_HEADS * (C_NOPE_DIM + C_ROPE_DIM)), C_Q_RANK ** -0.5),
        'c_w_ukv': nrm(ks[10], (DEPTH, C_KV_RANK, C_HEADS * (C_NOPE_DIM + C_V_DIM)), C_KV_RANK ** -0.5),
        'w_branch': nrm(ks[11], (DEPTH, N_BRANCH, BRANCH_W, D_MODEL), BRANCH_W ** -0.5),
        'w_out': nrm(ks[12], (DEPTH, D_MODEL, D_MODEL), D_MODEL ** -0.5),
        'ln2_g': gain(ks[13], (DEPTH, D_MODEL)),
        'w_ff1': nrm(ks[14], (DEPTH, D_MODEL, D_FF), D_MODEL ** -0.5),
        'w_ff2': nrm(ks[15], (DEPTH, D_FF, D_MODEL), D_FF ** -0.5),
        'final_g': gain(ks[16], (D_MODEL,)),
    }

def first_block(x, ln1_g, w_in, a_q_norm, a_k_norm, b_lambda, b_subln, c_q_norm, c_kv_norm,
              c_w_uq, c_w_ukv, w_branch, w_out, ln2_g, w_ff1, w_ff2, final_g):
    b, s, d = x.shape
    n_rows = s // GRID_W
    t = jnp.arange(s)
    row_idx = jnp.repeat(jnp.arange(n_rows), GRID_W)
    col_idx = jnp.tile(jnp.arange(GRID_W), n_rows)
    half = A_HEAD_DIM // 2
    row_ang = _angles(row_idx, half, AXIAL_THETA)
    col_ang = _angles(col_idx, half, AXIAL_THETA)
    b_ang = _angles(t, B_ROT_DIM, ROPE_THETA)
    c_ang = _angles(t, C_ROPE_DIM, MLA_THETA)

    for l in range(DEPTH):
        h = _rms_norm(x, ln1_g[l])
        proj = jnp.einsum('bsd,dn->bsn', h, w_in[l])
        (a_q, a_k, a_v, b_q, b_k, b_v, c_cq, c_ckv, c_kr, gate_logits) = _split_columns(proj)

        y_a = _gqa_axial(a_q.reshape(b, s, A_HEADS, A_HEAD_DIM),
                         a_k.reshape(b, s, A_KV_HEADS, A_HEAD_DIM),
                         a_v.reshape(b, s, A_KV_HEADS, A_HEAD_DIM),
                         a_q_norm[l], a_k_norm[l], row_ang, col_ang)
        lambda_init = 0.8 - 0.6 * math.exp(-0.3 * l)
        y_b = _diff_attention(b_q, b_k, b_v, b_lambda[l], b_subln[l], lambda_init, b_ang)
        y_c = _mla(c_cq, c_ckv, c_kr, c_q_norm[l], c_kv_norm[l], c_w_uq[l], c_w_ukv[l], c_ang)

        y = jnp.stack([y_a, y_b, y_c], axis=2)
        gates = jax.nn.sigmoid(gate_logits.reshape(b, s, N_BRANCH, d))
        merged = jnp.sum(gates * jnp.einsum('bsne,ned->bsnd', y, w_branch[l]), axis=2)
        x = x + jnp.einsum('bsd,de->bse', merged, w_out[l])

        h2 = _rms_norm(x, ln2_g[l])
        ff = jnp.square(jax.nn.relu(jnp.einsum('bsd,df->bsf', h2, w_ff1[l])))
        x = x + jnp.einsum('bsf,fd->bsd', ff, w_ff2[l])

    return _rms_norm(x, final_g)


D_POOL = D_MODEL // 2
POOL_WINDOWS = (2, 4, 8, 16)
N_POOL_GROUPS = len(POOL_WINDOWS)
POOL_GROUP = D_POOL // N_POOL_GROUPS
D_ATTN = D_MODEL // 2
HEAD_DIM = 64
N_HEADS = D_ATTN // HEAD_DIM
DILATED_PATTERNS = ((128, 1), (512, 4), (2048, 16))
D_IN = D_POOL + 3 * D_ATTN
D_FF_2 = 2816
N_EXPERTS = 8
TOP_K = 2
D_FF_EXPERT = 3584
N_DENSE = (DEPTH + 1) // 2
N_MOE = DEPTH // 2


def rmsnorm(x, g):
    xf = x.astype(jnp.float32)
    y = xf * lax.rsqrt(jnp.mean(xf * xf, axis=-1, keepdims=True) + EPS)
    return (y * g.astype(jnp.float32)).astype(x.dtype)

def pool_mixer(u, w_pool, pool_scale):
    B, S, _ = u.shape
    uf = u.astype(jnp.float32)
    c = jnp.concatenate([jnp.zeros((B, 1, D_POOL), jnp.float32), jnp.cumsum(uf, axis=1)], axis=1)
    t = jnp.arange(S)
    diffs = []
    for gi, w in enumerate(POOL_WINDOWS):
        sl = slice(gi * POOL_GROUP, (gi + 1) * POOL_GROUP)
        cg = c[..., sl]
        lo = jnp.maximum(t + 1 - w, 0)
        win_sum = cg[:, 1:] - cg[:, lo]
        cnt = (t + 1 - lo).astype(jnp.float32)[None, :, None]
        diffs.append(win_sum / cnt - uf[..., sl])
    d = jnp.stack(diffs, axis=2).astype(u.dtype)
    z = jnp.einsum('bsgc,gce->bsge', d, w_pool).reshape(B, S, D_POOL)
    return rmsnorm(z, pool_scale)

def dilated_attention(q, k, v):
    B, H, S, Dh = q.shape
    nb = S // Q_BLOCK
    scale = HEAD_DIM ** -0.5
    qb = q.reshape(B, H, nb, Q_BLOCK, Dh).transpose(2, 0, 1, 3, 4)

    def block(args):
        bi, qblk = args
        pos = bi * Q_BLOCK + jnp.arange(Q_BLOCK)
        outs, lses = [], []
        for window, dil in DILATED_PATTERNS:
            n_keys = window // dil + 1
            kidx = pos[:, None] - dil * jnp.arange(n_keys)[None, :]
            valid = kidx >= 0
            kidx = jnp.maximum(kidx, 0)
            kg = k[:, :, kidx]
            vg = v[:, :, kidx]
            s = jnp.einsum('bhqd,bhqjd->bhqj', qblk, kg).astype(jnp.float32) * scale
            s = jnp.where(valid[None, None], s, -jnp.inf)
            m = jnp.max(s, axis=-1, keepdims=True)
            p = jnp.exp(s - m)
            den = jnp.sum(p, axis=-1, keepdims=True)
            o = jnp.einsum('bhqj,bhqjd->bhqd', p, vg.astype(jnp.float32)) / den
            outs.append(o)
            lses.append(m + jnp.log(den))
        wts = jax.nn.softmax(jnp.concatenate(lses, axis=-1), axis=-1)
        o = jnp.einsum('bhqp,pbhqd->bhqd', wts, jnp.stack(outs, axis=0))
        return o.astype(q.dtype)

    ob = lax.map(block, (jnp.arange(nb), qb))
    return ob.transpose(1, 2, 0, 3, 4).reshape(B, H, S, Dh)

def hybrid_mixer(h, w_in, w_pool, pool_scale, attn_gain, w_out):
    B, S, _ = h.shape
    proj = h @ w_in
    u = proj[..., :D_POOL]
    q, k, v = jnp.split(proj[..., D_POOL:], 3, axis=-1)
    to_heads = lambda t: t.reshape(B, S, N_HEADS, HEAD_DIM).transpose(0, 2, 1, 3)
    y_a = pool_mixer(u, w_pool, pool_scale)
    o = dilated_attention(to_heads(q), to_heads(k), to_heads(v))
    y_b = rmsnorm(o.transpose(0, 2, 1, 3).reshape(B, S, D_ATTN), attn_gain)
    return jnp.concatenate([y_a, y_b], axis=-1) @ w_out

def swiglu(h, wg, wu, wd):
    return (jax.nn.silu(h @ wg) * (h @ wu)) @ wd

def moe_swiglu(h, w_router, wg, wu, wd):
    B, S, D = h.shape
    xt = h.reshape(-1, D)
    logits = (xt @ w_router).astype(jnp.float32)
    top_v, top_i = lax.top_k(logits, TOP_K)
    gates = jax.nn.softmax(top_v, axis=-1)
    gate = jnp.sum(jax.nn.one_hot(top_i, N_EXPERTS, dtype=jnp.float32) * gates[..., None], axis=1)
    y = jnp.zeros_like(xt)
    for e in range(N_EXPERTS):
        y = y + gate[:, e:e + 1].astype(xt.dtype) * swiglu(xt, wg[e], wu[e], wd[e])
    return y.reshape(B, S, D)

def second_inputs(seed: int = 0) -> dict:
    key = jax.random.key(seed)
    ks = jax.random.split(key, 20)
    f32 = jnp.float32
    nrm = lambda k, shape, fan_in: jax.random.normal(k, shape, f32) * (fan_in ** -0.5)
    gain = lambda k, shape: 1.0 + 0.05 * jax.random.normal(k, shape, f32)
    return {
        "x": jax.random.normal(ks[0], (BATCH, SEQ, D_MODEL), f32),
        "norm_mix": gain(ks[1], (DEPTH, D_MODEL)),
        "w_in": nrm(ks[2], (DEPTH, D_MODEL, D_IN), D_MODEL),
        "w_pool": nrm(ks[3], (DEPTH, N_POOL_GROUPS, POOL_GROUP, POOL_GROUP), POOL_GROUP),
        "pool_scale": gain(ks[4], (DEPTH, D_POOL)),
        "attn_gain": gain(ks[5], (DEPTH, D_ATTN)),
        "w_out": nrm(ks[6], (DEPTH, D_MODEL, D_MODEL), D_MODEL),
        "norm_ffn": gain(ks[7], (DEPTH, D_MODEL)),
        "ffn_wg": nrm(ks[8], (N_DENSE, D_MODEL, D_FF_2), D_MODEL),
        "ffn_wu": nrm(ks[9], (N_DENSE, D_MODEL, D_FF_2), D_MODEL),
        "ffn_wd": nrm(ks[10], (N_DENSE, D_FF_2, D_MODEL), D_FF_2),
        "w_router": nrm(ks[11], (N_MOE, D_MODEL, N_EXPERTS), D_MODEL),
        "moe_wg": nrm(ks[12], (N_MOE, N_EXPERTS, D_MODEL, D_FF_EXPERT), D_MODEL),
        "moe_wu": nrm(ks[13], (N_MOE, N_EXPERTS, D_MODEL, D_FF_EXPERT), D_MODEL),
        "moe_wd": nrm(ks[14], (N_MOE, N_EXPERTS, D_FF_EXPERT, D_MODEL), D_FF_EXPERT),
        "final_norm": gain(ks[15], (D_MODEL,)),
    }

def second_block(x, norm_mix, w_in, w_pool, pool_scale, attn_gain, w_out, norm_ffn,
              ffn_wg, ffn_wu, ffn_wd, w_router, moe_wg, moe_wu, moe_wd, final_norm):
    for l in range(DEPTH):
        h = rmsnorm(x, norm_mix[l])
        x = x + hybrid_mixer(h, w_in[l], w_pool[l], pool_scale[l], attn_gain[l], w_out[l])
        h = rmsnorm(x, norm_ffn[l])
        if l % 2 == 0:
            i = l // 2
            x = x + swiglu(h, ffn_wg[i], ffn_wu[i], ffn_wd[i])
        else:
            i = l // 2
            x = x + moe_swiglu(h, w_router[i], moe_wg[i], moe_wu[i], moe_wd[i])
    return rmsnorm(x, final_norm)


def setup_inputs(seed=0):
    out = dict(first_inputs(seed))
    for name, value in second_inputs(seed + 1).items():
        if name != "x":
            out[name + "_2"] = value
    return out


def reference(
    x, ln1_g, w_in, a_q_norm, a_k_norm, b_lambda, b_subln, c_q_norm, c_kv_norm, c_w_uq, c_w_ukv,
    w_branch, w_out, ln2_g, w_ff1, w_ff2, final_g, norm_mix_2, w_in_2, w_pool_2, pool_scale_2,
    attn_gain_2, w_out_2, norm_ffn_2, ffn_wg_2, ffn_wu_2, ffn_wd_2, w_router_2, moe_wg_2,
    moe_wu_2, moe_wd_2, final_norm_2,
):
    x = first_block(
        x, ln1_g, w_in, a_q_norm, a_k_norm, b_lambda, b_subln, c_q_norm, c_kv_norm, c_w_uq,
        c_w_ukv, w_branch, w_out, ln2_g, w_ff1, w_ff2, final_g,
    )
    return second_block(
        x, norm_mix_2, w_in_2, w_pool_2, pool_scale_2, attn_gain_2, w_out_2, norm_ffn_2,
        ffn_wg_2, ffn_wu_2, ffn_wd_2, w_router_2, moe_wg_2, moe_wu_2, moe_wd_2, final_norm_2,
    )


_drawn_inputs = setup_inputs


def setup_inputs(seed=0):
    import zlib

    import numpy as np

    out = dict(_drawn_inputs(seed))
    spreads = {}
    factors = {'a_q_norm': 8.0, 'a_k_norm': 8.0, 'b_subln': 3.457, 'c_q_norm': 8.0, 'c_kv_norm': 8.0}
    for name, (base, spread) in spreads.items():
        noise = np.random.default_rng([zlib.crc32(name.encode()), seed]).standard_normal(out[name].shape)
        drawn = base * np.exp(spread * noise) if base else spread * noise
        out[name] = __import__('jax').numpy.asarray(drawn.astype(out[name].dtype))
    for name, factor in factors.items():
        out[name] = (out[name] * factor).astype(out[name].dtype)
    return out
```

```python
import math
from contextlib import ExitStack

import concourse.bass as bass
import numpy as np
from concourse import mybir

F32 = mybir.dt.float32
F32R = mybir.dt.float32r
U32 = mybir.dt.uint32
ALU = mybir.AluOpType
ACT = mybir.ActivationFunctionType
AX = mybir.AxisListType

D, S, DEPTH, GRID_W, EPS = 1024, 256, 2, 64, 1e-6
P = 128
NTOK = S // P
KD = D // P
A_HEADS, A_KV, A_DIM = 8, 2, 64
B_HEADS, B_QK, B_ROT = 8, 32, 8
C_HEADS, C_QRANK, C_KVRANK, C_NOPE, C_ROPE, C_V = 8, 384, 256, 64, 32, 64
C_DIM = C_NOPE + C_ROPE
HV = 64
HEADS = 8
YW = HEADS * HV
NBR = 3
D_FF, D_FF2, D_FFE, NEXP = 4096, 2816, 3584, 8
POOL_WINDOWS = (2, 4, 8, 16)
PATTERNS = ((128, 1), (512, 4), (2048, 16))
W = 512

OA_Q, OA_K, OA_V = 0, 512, 640
OB_Q, OB_K, OB_V = 768, 1280, 1792
OC_Q, OC_KV, OC_KR = 2304, 2688, 2944
MIX_W = 2976
GATE_W = NBR * D

G1 = {}
_at = 0
for _n, _w in (("ln1", D), ("ln2", D), ("aq", A_DIM), ("ak", A_DIM), ("sub", HV), ("cq", C_QRANK),
               ("ckv", C_KVRANK), ("lam", 4 * B_QK), ("linit", 2)):
    G1[_n] = (_at, _at + _w)
    _at += _w
G1_W = _at
G2 = {"mix": (0, D), "pool": (D, D + 512), "attn": (D + 512, 2 * D), "ffn": (2 * D, 3 * D)}
G2_W = 3 * D

ROPE_W = 2 * (64 + B_ROT + C_ROPE)
TAB_W = P + NTOK * ROPE_W + 8
BIG_W = 2 * NTOK * S + NTOK * len(POOL_WINDOWS) * S


def rope_rows(pos, dim, theta):
    inv = np.float32(theta) ** (-np.arange(0, dim, 2, dtype=np.float32) / np.float32(dim))
    ang = pos.astype(np.float32)[:, None] * inv[None, :].astype(np.float32)
    c, s = np.cos(ang), np.sin(ang)
    return np.concatenate([c, c], 1), np.concatenate([-s, s], 1)


def make_tables():
    t = np.arange(S)
    row, col = rope_rows(t // GRID_W, 32, 10000.0), rope_rows(t % GRID_W, 32, 10000.0)
    b, c = rope_rows(t, B_ROT, 500000.0), rope_rows(t, C_ROPE, 10000.0)
    rope = np.concatenate([row[0], col[0], row[1], col[1], b[0], b[1], c[0], c[1]], 1)
    rope = rope.reshape(NTOK, P, ROPE_W).transpose(1, 0, 2).reshape(P, -1)
    iota = np.tile(np.arange(8), (P, 1))
    small = np.concatenate([np.eye(P), rope, iota], 1).astype(np.float32)
    d = t[:, None] - t[None, :]
    count = sum(((d >= 0) & (d % dil == 0) & (d <= win)).astype(np.float32) for win, dil in PATTERNS)
    mask = np.where(count > 0, 0.0, -1e30)
    pool = []
    for w in POOL_WINDOWS:
        n = np.minimum(t + 1, w).astype(np.float32)
        pool.append((((d >= 0) & (d < w)) / n[:, None] - np.eye(S)).T)
    pool = np.stack(pool, 1)
    tiles = lambda a: a.reshape(NTOK, P, -1).transpose(1, 0, 2).reshape(P, -1)
    big = np.concatenate([tiles(count), tiles(mask), tiles(pool)], 1).astype(np.float32)
    return small, big


def columns(w, rows, c0, width, k0=0, per=4):
    for k in range(0, rows, per * P):
        n = min(per * P, rows - k) // P
        yield (lambda r, k=k, n=n: w(r, k0 + k, n * P, c0, width).rearrange("(c p) n -> p c n", p=P), n, width)


def at_layer(w, rows):
    flat = w.rearrange("l r n -> (l r) n")

    def get(layer, k, n, c0, width):
        if isinstance(layer, int):
            return flat[layer * rows + k:layer * rows + k + n, c0:c0 + width]
        return flat[bass.ds(layer * rows + k, n), c0:c0 + width]
    return get


def ffn_steps(groups, gated):
    up = ("gate", "up") if gated else ("up",)
    for g in range(groups + 1):
        for n, kind in enumerate(up):
            if g < groups:
                yield kind, g, 0
                if n == 0 and g:
                    yield "turn", g - 1, 0
                yield kind, g, 1
                yield "act_" + kind, g, 0
            elif n == 0:
                yield "turn", g - 1, 0
            if g:
                if gated:
                    yield "down", g - 1, n
                else:
                    yield "down", g - 1, 0
                    yield "down", g - 1, 1


FF1_STEPS = list(ffn_steps(D_FF // W, False))
FF2_STEPS = list(ffn_steps(-(-D_FF2 // W), True))
FFE_STEPS = list(ffn_steps(D_FFE // W, True))
TILE_STEPS = ("gate", "up", "down")


def ffn_tiles(steps, gate, up, down, hidden):
    for kind, g, k in steps:
        w = min(W, hidden - g * W)
        if kind in ("gate", "up"):
            yield from columns(gate if kind == "gate" else up, D // 2, g * W, w, k0=k * D // 2)
        elif kind == "down":
            yield from columns(down, w, k * W, W, k0=g * W)


RAW, SPLIT = 3, 2
CREDIT = {"lo": RAW, "used": SPLIT, "fA": NTOK, "fB": NTOK, "fC": NTOK, "xn": 1}

TURNS1 = [("ln1", 4), ("cc", 4), ("qa", 2), ("ka", 2), ("qb", 2), ("kb", 2), ("pa", 8), ("pb", 8),
          ("qc", 4), ("kc", 4), ("pc", 8), ("y", 6), ("mrg", 4), ("ln2", 4), ("ff", 16)]
TURNS2 = [("mix", 4), ("dt", 2), ("q2", 2), ("k2", 2), ("p2", 8), ("y2", 4), ("ffn", 4), ("ff", 12)]
TURNS3 = TURNS2[:-1] + [("rt", 1)]
TURNSE = [("ff", 14)]


def starts(turns):
    out, at = {}, 0
    for name, n in turns:
        out[name] = at
        at += n
    return out, at


STEP_LAYER1 = 68
STEP_EXPERT = 1
PLAIN = ("qa", "ka", "qb", "kb", "pa", "pb", "qc", "kc", "pc", "q2", "k2", "p2", "rt")

def rises(tiles, turns, a, b, c, norms, powers, banks, branches, preps=0, relu=0):
    return dict(lo=tiles, used=tiles, hi=tiles, tp=starts(turns)[1],
                th=sum(n for name, n in turns if name not in PLAIN), fA=NTOK * a, fB=NTOK * b, fC=NTOK * c, xn=NTOK * norms, pw=powers, sb=banks, br=branches, prep=preps, relu=relu)


R1 = rises(72, TURNS1, 20, 13, 1, 2, 10, 32, 3, 4, 16)
RF = rises(0, [], 0, 0, 0, 1, 2, 0, 0)
R2 = rises(49, TURNS2, 16, 4, 1, 2, 8, 8, 1)
R3 = rises(13, TURNS3, 4, 3, 0, 2, 8, 8, 1)
RE = rises(42, TURNSE, 14, 1, 1, 0, 0, 0, 0)


class Span:

    def __init__(self, turns, rise, base, turn=0, tiles=()):
        self.start, self.turn, self.rise, self.base = starts(turns)[0], turn, rise, base
        self.tiles = tiles

    def value(self, fixed, rise):
        return self.turn * rise + fixed if rise else fixed

    def at(self, name, k):
        return self.value(self.base[name] + CREDIT.get(name, 0) + k, self.rise[name])

    def bank(self, k):
        return (self.base["tp"] + k) % 2

    def empty(self, k):
        return self.value((self.base["tp"] + k) // 2 + 1, self.rise["tp"] // 2)

    def turned(self, k):
        return self.value((self.base["tp"] + k) // 2 + 2, self.rise["tp"] // 2)

    def landed(self, j):
        return self.value(16 * ((self.base["lo"] + j) // RAW + 1), 16 * (self.rise["lo"] // RAW))

    def tile(self, j):
        return self.base["lo"] + j


def after(base, rise, rounds=1):
    return {k: base[k] + rise[k] * rounds for k in rise}


BASE1 = {k: 0 for k in R1}
BASEF = after(BASE1, R1, DEPTH)
BASE2 = after(BASEF, RF)
BASE3 = after(BASE2, R2)
BASEE = after(BASE3, R3)
BASEG = after(BASEE, RE, NEXP)


def build(nc, a, out):
    ctx = ExitStack()
    with ctx:
        def sb(name, shape, dt=F32):
            return ctx.enter_context(nc.sbuf_tensor(name, shape, dt))

        def sem(name):
            return ctx.enter_context(nc.semaphore(name))

        x_sb = sb("x_res", [P, NTOK, D])
        hT = sb("hT", [P, 2, 16, S], F32R)
        work = sb("work", [P, 20288])
        raw = sb("raw", [P, RAW, 4 * W])
        whi = sb("w_high", [P, SPLIT, 4 * W], F32R)
        wlo = sb("w_low", [P, SPLIT, 4 * W], F32R)
        gains = sb("gains", [P, G2_W])
        tab = sb("tables", [P, TAB_W])
        probs = sb("probs", [P, 4, NTOK, S])
        probsT = sb("probsT", [P, 2, NTOK, S])
        scr = sb("scratch", [P, W])
        negmax = sb("negmax", [P, 32, NTOK])
        rowsum = sb("rowsum", [P, 32, NTOK])
        rinv = sb("rinv", [P, 32, NTOK])
        meansq = sb("meansq", [P, 2, 16])
        rstd = sb("rstd", [P, 2, 16])
        neghalf = sb("neghalf", [P, 16])
        lam = sb("lam", [P, 8])
        route = sb("route", [P, 96])
        route_i = sb("route_i", [P, 8], U32)
        gate_e = sb("gate_e", [P, NEXP, NTOK])
        gate_c = sb("gate_c", [P, NTOK])
        w_route = sb("w_route", [P, KD, NEXP])
        psum = ctx.enter_context(nc.psum_tensor("acc", [P, 8, W], F32))
        SETS = {"A": (0, 1), "B": (2, 3), "C": (4, 5)}
        TB = (6, 7)

        def region(at, *shape):
            n = int(np.prod(shape))
            v = work[:, at:at + n]
            return v if len(shape) == 1 else v.rearrange("p (a b) -> p a b", a=shape[0])

        mix = region(0, NTOK, MIX_W)
        gts = region(5952, NTOK, GATE_W)
        qT_a, kT_a = region(12096, 4, S), region(13120, 1, S)
        qT_b, kT_b = region(13376, 4, S), region(14400, 4, S)
        qT_c, kT_c = region(12096, HEADS, S), region(14144, HEADS, S)
        q_c = region(16192, NTOK, C_HEADS * C_DIM)
        v_c = region(17728, NTOK, YW)
        k_c = region(18752, NTOK, C_HEADS * C_DIM)
        ropeU, ropeV = region(16192, 640), region(16832, 640)
        merged = region(0, NTOK, D)
        xn = region(12096, NTOK, D)
        ff_s, ff_a = region(14144, NTOK, W), region(15168, NTOK, W)
        mix2 = region(0, NTOK, 4 * W)
        qT_2, kT_2 = region(4096, 4, S), region(5120, 4, S)
        big = region(6144, BIG_W)
        count = big[:, 0:NTOK * S].rearrange("p (a b) -> p a b", a=NTOK)
        mask = big[:, NTOK * S:2 * NTOK * S].rearrange("p (a b) -> p a b", a=NTOK)
        poolT = big[:, 2 * NTOK * S:].rearrange("p (a g t) -> p a g t", a=NTOK, g=4)
        z_2, o_2 = region(9216, NTOK, W), region(10240, NTOK, W)

        ident = tab[:, 0:P]
        rope = tab[:, P:P + NTOK * ROPE_W].rearrange("p (a b) -> p a b", a=NTOK)
        iota = tab[:, P + NTOK * ROPE_W:TAB_W]

        s_raw = [sem(f"raw_landed{i}") for i in range(RAW)]
        s_in, s_gain, s_gain2, s_big, s_wr, s_out = (sem(n) for n in (
            "inputs_landed", "gains_landed", "gains2_landed", "big_landed", "router_landed", "out_landed"))
        s_hi, s_lo, s_used = sem("w_high_ready"), sem("w_low_ready"), sem("w_tile_used")
        s_free = {k: sem(f"acc{k}_emptied") for k in "ABC"}
        s_tp = sem("turned")
        s_tf = [sem("turn_bank0_emptied"), sem("turn_bank1_emptied")]
        s_thi = sem("turned_high_ready")
        s_xn = sem("normed_ready")
        s_pow_in, s_pow = sem("meansq_ready"), sem("rstd_ready")
        s_step = sem("vector_step")
        s_prep = sem("qk_prepared")
        s_sc, s_nm, s_pr = sem("scores_ready"), sem("negmax_ready"), sem("probs_ready")
        s_pw = sem("probs_weighted")
        s_o, s_y = sem("heads_done"), sem("branch_ready")
        s_mrg = sem("merged_ready")
        s_lam, s_lame = sem("lambda_sums"), sem("lambda_exp")
        s_relu = sem("relu_ready")
        s_rt, s_rte = sem("route_diff"), sem("route_exp")
        s_const = sem("constants_set")

        w_in = at_layer(a["w_in"], D)
        uq, ukv = at_layer(a["c_w_uq"], C_QRANK), at_layer(a["c_w_ukv"], C_KVRANK)
        w_br = at_layer(a["w_branch"].rearrange("l n r c -> l (n r) c"), NBR * YW)
        w_o, ff1, ff2 = at_layer(a["w_out"], D), at_layer(a["w_ff1"], D), at_layer(a["w_ff2"], D_FF)
        WIN_W = [W] * 5 + [MIX_W - 5 * W] + [W] * 6
        WIN_0 = [sum(WIN_W[:g]) for g in range(12)]
        tiles1 = []
        for g in range(12):
            tiles1 += columns(w_in, D, WIN_0[g], WIN_W[g])
        T_UQ = len(tiles1)
        UQ_W = (W, 256)
        for g in range(2):
            tiles1 += columns(uq, C_QRANK, g * W, UQ_W[g])
        T_UKV = len(tiles1)
        for g in range(2):
            tiles1 += columns(ukv, C_KVRANK, g * W, W, per=1)
        T_BR = len(tiles1)
        for n in range(NBR):
            for h in range(2):
                tiles1 += columns(w_br, YW, h * W, W, k0=n * YW)
        T_OUT = len(tiles1)
        for h in range(2):
            tiles1 += columns(w_o, D, h * W, W)
        T_FF = len(tiles1)
        tiles1 += ffn_tiles(FF1_STEPS, None, ff1, ff2, D_FF)
        assert len(tiles1) == R1["lo"]

        w_in2, w_o2 = at_layer(a["w_in_2"], D), at_layer(a["w_out_2"], D)
        w_pl = at_layer(a["w_pool_2"].rearrange("l g r c -> l (g r) c"), W)
        wg2, wu2, wd2 = at_layer(a["ffn_wg_2"], D), at_layer(a["ffn_wu_2"], D), at_layer(a["ffn_wd_2"], D_FF2)
        mixer2 = []
        for g in range(4):
            mixer2 += columns(w_in2, D, g * W, W)
        T_POOL = len(mixer2)
        mixer2 += columns(w_pl, W, 0, P)
        T_OUT2 = len(mixer2)
        for h in range(2):
            mixer2 += columns(w_o2, D, h * W, W)
        T_FF2 = len(mixer2)
        fix = lambda ts, r: [(lambda _, f=f: f(r), n, w) for f, n, w in ts]
        tiles2 = fix(mixer2, 0) + list(ffn_tiles(FF2_STEPS, wg2, wu2, wd2, D_FF2))
        tiles3 = fix(mixer2, 1)
        assert len(tiles2) == R2["lo"] and len(tiles3) == R3["lo"], (len(tiles2), len(tiles3))
        wge, wue, wde = (at_layer(a[n].rearrange("m e r c -> (m e) r c"), r) for n, r in (
            ("moe_wg_2", D), ("moe_wu_2", D), ("moe_wd_2", D_FFE)))
        tilese = list(ffn_tiles(FFE_STEPS, wge, wue, wde, D_FFE))
        assert len(tilese) == RE["lo"]

        span1 = lambda r: Span(TURNS1, R1, BASE1, r, tiles1)
        spanf = Span([], RF, BASEF)
        span2 = Span(TURNS2, R2, BASE2, 0, tiles2)
        span3 = Span(TURNS3, R3, BASE3, 0, tiles3)
        spane = lambda r: Span(TURNSE, RE, BASEE, r, tilese)
        spang = Span([], RF, BASEG)

        block = ctx.enter_context(nc.Block())

        @block.sync
        def _(sp):
            sp.sem_inc(s_lo, RAW)
            sp.sem_inc(s_xn, 1)
            sp.dma_start(x_sb[:], a["x"][0].rearrange("(i p) d -> p i d", p=P)).then_inc(s_in, 16)
            sp.dma_start(tab[:], a["tables"]).then_inc(s_in, 16)
            sp.dma_start(w_route[:], a["w_router_2"][0].rearrange("(c p) e -> p c e", p=P)).then_inc(s_wr, 16)

            def load(m, r, j0, j1):
                for j in range(j0, j1):
                    src, n, w = m.tiles[j]
                    b = m.tile(j) % RAW
                    sp.wait_ge(s_lo, m.at("lo", j + 1 - RAW))
                    sp.dma_start(raw[:, b, 0:n * w].rearrange("p (c n) -> p c n", c=n), src(r))\
                      .then_inc(s_raw[b], 16)

            def gain(cols, src, done):
                sp.dma_start(gains[:, cols[0]:cols[1]], src.partition_broadcast(P)).then_inc(done, 16)

            with sp.Fori(0, DEPTH) as r:
                m = span1(r)
                sp.wait_ge(s_xn, m.at("xn", 0))
                gain((0, G1_W), a["gains1"][bass.ds(r, 1), :].rearrange("a n -> (a n)"), s_gain)
                load(m, r, 0, len(tiles1))
            sp.wait_ge(s_xn, spanf.at("xn", 0))
            gain((2 * D, 3 * D), a["final_g"], s_gain2)
            gain((0, 2 * D), a["gains2"][0, 0:2 * D], s_gain2)
            sp.dma_start(big, a["big"]).then_inc(s_big, 16)
            load(span2, 0, 0, RAW)
            sp.wait_ge(s_xn, span2.at("xn", 0))
            gain((2 * D, 3 * D), a["gains2"][0, 2 * D:3 * D], s_gain2)
            load(span2, 0, RAW, T_FF2 + RAW)
            sp.wait_ge(s_xn, span3.at("xn", 0))
            gain((0, 3 * D), a["gains2"][1, :], s_gain2)
            load(span2, 0, T_FF2 + RAW, len(tiles2))
            load(span3, 0, 0, len(tiles3))
            with sp.Fori(0, NEXP) as e:
                load(spane(e), e, 0, len(tilese))
            sp.wait_ge(s_xn, spang.at("xn", 0))
            gain((0, D), a["final_norm_2"], s_gain2)
            sp.wait_ge(s_xn, spang.at("xn", NTOK))
            sp.dma_start(out[0].rearrange("(i p) d -> p i d", p=P), xn).then_inc(s_out, 16)
            sp.wait_ge(s_out, 16)

        @block.gpsimd
        def _(pool):
            nc.gpsimd.memset(neghalf[:], -0.5).then_inc(s_const, 1)
            nc.gpsimd.memset(meansq[:], 1.0).then_inc(s_const, 1)
            pool.wait_ge(s_const, 2)
            with pool.Fori(0, (BASEG["pw"] + RF["pw"]) // 2) as r:
                for b in range(2):
                    pool.wait_ge(s_pow_in, 2 * r + (b + 1))
                    nc.gpsimd.tensor_tensor(rstd[:, b], meansq[:, b], neghalf[:], ALU.pow).then_inc(s_pow, 1)

        @block.scalar
        def _(act):
            def high(m, j):
                t = m.tile(j)
                n, w = m.tiles[j][1:]
                act.wait_ge(s_raw[t % RAW], m.landed(j))
                act.wait_ge(s_used, m.at("used", j + 1 - SPLIT))
                nc.scalar.activation(whi[:, t % SPLIT, 0:n * w], raw[:, t % RAW, 0:n * w], ACT.Copy)\
                  .then_inc(s_hi, 1)

            def ahead(m, j):
                if j + 1 < len(m.tiles):
                    high(m, j + 1)

            def turned_high(m, k, view, blocks, cols):
                b = m.bank(k)
                act.wait_ge(s_tp, m.at("tp", k + 1))
                src = psum[:, TB[b], 0:blocks * cols].rearrange("p (c t) -> p c t", c=blocks)
                nc.scalar.activation(view, src, ACT.Copy).then_inc(s_thi, 1)

            def normed_high(m, stage):
                for n in range(4):
                    i, c = n // 2, n % 2
                    turned_high(m, m.start[stage] + n, hT[:, 0, 4 * c:4 * c + 4, i * P:(i + 1) * P], 4, P)

            def plain_turn(m, k, dst, parts, blocks, cols, scale):
                b = m.bank(k)
                act.wait_ge(s_tp, m.at("tp", k + 1))
                src = psum[0:parts, TB[b], 0:blocks * cols].rearrange("p (c t) -> p c t", c=blocks)
                nc.scalar.activation(dst, src, ACT.Copy, scale=scale).then_inc(s_tf[b], 1)

            def softmax_exp(m, n):
                act.wait_ge(s_nm, m.at("sb", n + 1))
                for i in range(NTOK):
                    ins = nc.scalar.activation(probs[:, n % 4, i], psum[:, n % 4, i * S:(i + 1) * S], ACT.Exp,
                                               bias=negmax[:, n, i:i + 1], accum_out=rowsum[:, n, i:i + 1])
                ins.then_inc(s_pr, 1)

            def evac(m, key, j, dst, w, func=ACT.Copy):
                act.wait_ge(s_used, m.at("used", j + 1))
                for i in range(NTOK):
                    ins = nc.scalar.activation(dst(i), psum[:, SETS[key][i], 0:w], func)
                    ins.then_inc(s_free[key], 1)

            def ffn(m, steps, j, hidden, a0):
                use, turn, gated = a0, m.start["ff"], steps is not FF1_STEPS
                for kind, g, k in steps:
                    w = min(W, hidden - g * W)
                    if kind in TILE_STEPS:
                        ahead(m, j)
                        j += 1
                    elif kind in ("act_up", "act_gate"):
                        if kind == "act_gate":
                            evac(m, "A", j - 1, lambda i: ff_s[:, i, 0:w], w, ACT.Silu)
                        elif not gated:
                            act.wait_ge(s_used, m.at("used", j))
                            for i in range(NTOK):
                                nc.scalar.activation(ff_s[:, i, 0:w], psum[:, SETS["A"][i], 0:w], ACT.Relu)\
                                  .then_inc(s_relu, 1)
                        use += 1
                    elif kind == "turn":
                        c = 8 + 4 * (g % 2)
                        for i in range(NTOK):
                            turned_high(m, turn, hT[:, 0, c:c + w // P, i * P:(i + 1) * P], w // P, P)
                            turn += 1

            act.sem_inc(s_used, SPLIT)

            with act.Fori(0, DEPTH) as r:
                m = span1(r)
                high(m, 0)
                normed_high(m, "ln1")
                act.wait_ge(s_lam, r + 1)
                nc.scalar.activation(lam[:, 2:4], lam[:, 0:2], ACT.Exp).then_inc(s_lame, 1)
                for g in range(12):
                    ahead(m, 2 * g)
                    ahead(m, 2 * g + 1)
                    key, w = "AB"[g % 2], WIN_W[g]
                    if g < 6:
                        evac(m, key, 2 * g + 1, lambda i: mix[:, i, WIN_0[g]:WIN_0[g] + w], w)
                    else:
                        evac(m, key, 2 * g + 1, lambda i: gts[:, i, (g - 6) * W:(g - 5) * W], w, ACT.Sigmoid)
                for i in range(NTOK):
                    turned_high(m, m.start["cc"] + 2 * i, hT[:, 0, 0:3, i * P:(i + 1) * P], 3, P)
                    turned_high(m, m.start["cc"] + 2 * i + 1, hT[:, 0, 3:5, i * P:(i + 1) * P], 2, P)
                for g in range(2):
                    ahead(m, T_UQ + g)
                    evac(m, "AB"[g], T_UQ + g, lambda i: q_c[:, i, g * W:g * W + UQ_W[g]], UQ_W[g])
                for g in range(2):
                    ahead(m, T_UKV + 2 * g)
                    ahead(m, T_UKV + 2 * g + 1)
                    key = "AB"[g]
                    act.wait_ge(s_used, m.at("used", T_UKV + 2 * g + 2))
                    for i in range(NTOK):
                        src = psum[:, SETS[key][i], :].rearrange("p (h e) -> p h e", h=4)
                        kd = k_c[:, i].rearrange("p (h e) -> p h e", h=8)[:, 4 * g:4 * g + 4, 0:C_NOPE]
                        vd = v_c[:, i].rearrange("p (h e) -> p h e", h=8)[:, 4 * g:4 * g + 4, :]
                        nc.scalar.activation(kd, src[:, :, 0:C_NOPE], ACT.Copy)
                        nc.scalar.activation(vd, src[:, :, C_NOPE:], ACT.Copy).then_inc(s_free[key], 1)
                for i in range(NTOK):
                    plain_turn(m, m.start["qa"] + i, qT_a[:, :, i * P:(i + 1) * P], P, 4, P, A_DIM ** -0.5)
                for i in range(NTOK):
                    plain_turn(m, m.start["ka"] + i, kT_a[:, :, i * P:(i + 1) * P], P, 1, P, 1.0)
                for i in range(NTOK):
                    plain_turn(m, m.start["qb"] + i, qT_b[:, :, i * P:(i + 1) * P], P, 4, P, B_QK ** -0.5)
                for i in range(NTOK):
                    plain_turn(m, m.start["kb"] + i, kT_b[:, :, i * P:(i + 1) * P], P, 4, P, 1.0)
                for n in range(8):
                    softmax_exp(m, n)
                for h in range(B_HEADS + 1):
                    if h < B_HEADS:
                        softmax_exp(m, 8 + 2 * h)
                        softmax_exp(m, 9 + 2 * h)
                    if h:
                        b = m.bank(m.start["pb"] + h - 1)
                        act.wait_ge(s_tp, m.at("tp", m.start["pb"] + h))
                        nc.scalar.activation(probsT[:, (h - 1) % 2], psum[:, TB[b]].rearrange(
                            "p (c t) -> p c t", c=2), ACT.Copy).then_inc(s_tf[b], 1)
                for stage, dst, scale in (("qc", qT_c, C_DIM ** -0.5), ("kc", kT_c, 1.0)):
                    for n in range(4):
                        i, c = n // 2, n % 2
                        plain_turn(m, m.start[stage] + n, dst[0:C_DIM, 4 * c:4 * c + 4, i * P:(i + 1) * P],
                                   C_DIM, 4, P, scale)
                for n in range(24, 32):
                    softmax_exp(m, n)
                for n in range(NBR):
                    for i in range(NTOK):
                        turned_high(m, m.start["y"] + 2 * n + i, hT[:, 0, 4 * n:4 * n + 4, i * P:(i + 1) * P], 4, P)
                for j in range(T_BR, T_OUT):
                    ahead(m, j)
                normed_high(m, "mrg")
                for j in range(T_OUT, T_FF):
                    ahead(m, j)
                normed_high(m, "ln2")
                ffn(m, FF1_STEPS, T_FF, D_FF, 12)

            def mixer2_act(m):
                high(m, 0)
                normed_high(m, "mix")
                for g in range(4):
                    ahead(m, 2 * g)
                    ahead(m, 2 * g + 1)
                    evac(m, "AB"[g % 2], 2 * g + 1, lambda i: mix2[:, i, g * W:(g + 1) * W], W)
                for n in range(2):
                    turned_high(m, m.start["dt"] + n, hT[:, 0, 8 + 2 * n:10 + 2 * n, :], 2, S)
                ahead(m, T_POOL)
                evac(m, "A", T_POOL, lambda i: z_2[:, i], W)
                for stage, dst, scale in (("q2", qT_2, HV ** -0.5), ("k2", kT_2, 1.0)):
                    for i in range(NTOK):
                        plain_turn(m, m.start[stage] + i, dst[:, :, i * P:(i + 1) * P], P, 4, P, scale)
                for n in range(8):
                    act.wait_ge(s_nm, m.at("sb", n + 1))
                    for i in range(NTOK):
                        ins = nc.scalar.activation(probs[:, n % 4, i], probs[:, n % 4, i], ACT.Exp,
                                                   bias=negmax[:, n, i:i + 1])
                    ins.then_inc(s_pr, 1)
                for n in range(4):
                    i, c = n // 2, n % 2
                    turned_high(m, m.start["y2"] + n, hT[:, 0, 4 * c:4 * c + 4, i * P:(i + 1) * P], 4, P)
                for j in range(T_OUT2, T_FF2):
                    ahead(m, j)
                normed_high(m, "ffn")

            mixer2_act(span2)
            ffn(span2, FF2_STEPS, T_FF2, D_FF2, 4)
            mixer2_act(span3)
            act.wait_ge(s_rt, 1)
            nc.scalar.activation(route[:, 24:26], route[:, 16:18], ACT.Exp).then_inc(s_rte, 1)
            with act.Fori(0, NEXP) as e:
                m = spane(e)
                high(m, 0)
                ffn(m, FFE_STEPS, 0, D_FFE, 0)

        @block.vector
        def _(dve):
            chain = {"base": 0, "n": 0, "rise": 0}
            powers = [0]

            def link(m, ins):
                chain["n"] += 1
                ins.then_inc(s_step, 1)
                fixed = chain["base"] + chain["n"]
                dve.wait_ge(s_step, m.turn * chain["rise"] + fixed if chain["rise"] else fixed)

            def low(m, j):
                t = m.tile(j)
                n, w = m.tiles[j][1:]
                hi = whi[:, t % SPLIT, 0:n * w].bitcast(F32)
                dve.wait_ge(s_hi, m.at("hi", j + 1))
                nc.vector.tensor_tensor(wlo[:, t % SPLIT, 0:n * w], raw[:, t % RAW, 0:n * w], hi, ALU.subtract)\
                  .then_inc(s_lo, 1)

            def ahead(m, j):
                if j + 1 < len(m.tiles):
                    low(m, j + 1)

            split_turns = [0]

            def turned_low(m, k, chunks, cols, blocks, width):
                b = m.bank(k)
                split_turns[0] += 1
                dve.wait_ge(s_thi, m.at("th", split_turns[0]))
                src = psum[:, TB[b], 0:blocks * width].rearrange("p (c t) -> p c t", c=blocks)
                nc.vector.tensor_tensor(hT[:, 1, chunks, cols], src, hT[:, 0, chunks, cols].bitcast(F32),
                                        ALU.subtract).then_inc(s_tf[b], 1)

            def quarter_low(m, stage):
                for n in range(4):
                    i, c = n // 2, n % 2
                    turned_low(m, m.start[stage] + n, slice(4 * c, 4 * c + 4), slice(i * P, (i + 1) * P), 4, P)

            def slot(m):
                return meansq[:, (m.base["pw"] + powers[0]) % 2]

            def power(m, ins):
                r = rstd[:, (m.base["pw"] + powers[0]) % 2]
                powers[0] += 1
                ins.then_inc(s_pow_in, 1)
                dve.wait_ge(s_pow, m.at("pw", powers[0]))
                return r

            def rms(m, src, gain, dst, junk, n, part=None):
                r = power(m, nc.vector.tensor_tensor_reduce(out=junk, in0=src, in1=src, scale=1.0 / n, scalar=EPS,
                                                            op0=ALU.mult, op1=ALU.add, accum_out=slot(m)[:, 0:1]))
                return nc.vector.scalar_tensor_tensor(out=dst, in0=src, scalar=r[:, 0:1], in1=gain,
                                                      op0=ALU.mult, op1=ALU.mult)

            def norm(m, g0, dst):
                for i in range(NTOK):
                    rms(m, x_sb[:, i], gains[:, g0:g0 + D], dst[:, i], xn[:, i], D).then_inc(s_xn, 1)

            def over(v, h):
                return v.unsqueeze(1).broadcast_to([P, h, v.shape[-1]])

            def each(v, n):
                return v.unsqueeze(2).broadcast_to([P, v.shape[-1], n])

            def heads(v, h):
                return v.rearrange("p (h e) -> p h e", h=h)

            def rotate(m, src, dst, cos, sin, axes, u, v):
                h, w = src.shape[1], src.shape[2]
                half = w // axes // 2
                u, v = (heads(t[:, 0:h * w], h) for t in (u, v))
                nc.vector.tensor_tensor(u, src, over(cos, h), ALU.mult)
                ax = lambda t: t.rearrange("p h (a d) -> p h a d", a=axes)
                sb_ = over(sin, h)
                for o in (0, half):
                    s0 = half - o
                    if axes == 1:
                        ins = nc.vector.tensor_tensor(v[:, :, o:o + half], src[:, :, s0:s0 + half],
                                                      sb_[:, :, o:o + half], ALU.mult)
                    else:
                        ins = nc.vector.tensor_tensor(ax(v)[:, :, :, o:o + half], ax(src)[:, :, :, s0:s0 + half],
                                                      ax(sb_)[:, :, :, o:o + half], ALU.mult)
                link(m, ins)
                return u, v

            def accumulate(m, key, use, half, j):
                dve.wait_ge(s_used, m.at("used", j + 1))
                for i in range(NTOK):
                    xs = x_sb[:, i, half * W:(half + 1) * W]
                    nc.vector.tensor_tensor(xs, psum[:, SETS[key][i]], xs, ALU.add).then_inc(s_free[key], 1)
                dve.wait_ge(s_free[key], m.at("f" + key, NTOK * (use + 1)))

            def ffn(m, steps, j, hidden, a0):
                use, turn, gated = a0, m.start["ff"], steps is not FF1_STEPS
                relu = 0
                for kind, g, k in steps:
                    w = min(W, hidden - g * W)
                    if kind in TILE_STEPS:
                        ahead(m, j)
                        j += 1
                    elif kind == "act_gate":
                        use += 1
                    elif kind == "act_up":
                        dve.wait_ge(s_used, m.at("used", j))
                        for i in range(NTOK):
                            ps = psum[:, SETS["A"][i], 0:w]
                            if gated:
                                ins = nc.vector.tensor_tensor(ff_a[:, i, 0:w], ps, ff_s[:, i, 0:w], ALU.mult)
                            else:
                                relu += 1
                                dve.wait_ge(s_relu, m.at("relu", relu))
                                ins = nc.vector.scalar_tensor_tensor(out=ff_a[:, i, 0:w], in0=ps, scalar=0.0,
                                                                     in1=ff_s[:, i, 0:w], op0=ALU.max, op1=ALU.mult)
                            ins.then_inc(s_free["A"], 1)
                        use += 1
                    elif kind == "turn":
                        c = 8 + 4 * (g % 2)
                        for i in range(NTOK):
                            turned_low(m, turn, slice(c, c + w // P), slice(i * P, (i + 1) * P), w // P, P)
                            turn += 1

            def row_max(m, n):
                dve.wait_ge(s_sc, m.at("sb", n + 1))
                nc.vector.tensor_reduce(negmax[:, n], psum[:, n % 4].rearrange("p (i k) -> p i k", i=NTOK),
                                        AX.X, ALU.max, negate=True).then_inc(s_nm, 1)

            def turned_probs(m, k, h):
                b = m.bank(k)
                dve.wait_ge(s_tp, m.at("tp", k + 1))
                nc.vector.tensor_copy(probsT[:, h % 2], psum[:, TB[b]].rearrange("p (c t) -> p c t", c=2))\
                  .then_inc(s_tf[b], 1)

            def softmax_heads(m, n0, stage):
                for h in range(3):
                    row_max(m, n0 + h)
                for h in range(HEADS):
                    turned_probs(m, m.start[stage] + h, h)
                    if h + 3 < HEADS:
                        row_max(m, n0 + h + 3)

            def divide(m, n0, branch, dst):
                link(m, nc.vector.reciprocal(rinv[:, n0:n0 + HEADS], rowsum[:, n0:n0 + HEADS]))
                dve.wait_ge(s_o, m.at("br", branch + 1))
                for i in range(NTOK):
                    ins = nc.vector.tensor_tensor(heads(dst(i), HEADS), heads(psum[:, SETS["C"][i]], HEADS),
                                                  each(rinv[:, n0:n0 + HEADS, i], HV), ALU.mult)
                ins.then_inc(s_y, 1)

            def table(i, at, w):
                return rope[:, i, at:at + w]

            dve.wait_ge(s_in, 32)
            dve.wait_ge(s_const, 2)
            g1 = lambda n: gains[:, G1[n][0]:G1[n][1]]

            def prep_latents(m):
                for i in range(NTOK):
                    for n, o, w in (("cq", OC_Q, C_QRANK), ("ckv", OC_KV, C_KVRANK)):
                        v = mix[:, i, o:o + w]
                        k = 0 if n == "cq" else 1
                        ins = nc.vector.tensor_tensor_reduce(
                            out=scr[:, 0:w], in0=v, in1=v, scale=1.0 / w, scalar=EPS, op0=ALU.mult, op1=ALU.add,
                            accum_out=slot(m)[:, k:k + 1])
                        if k == 0:
                            link(m, ins)
                    r = power(m, ins)
                    for n, o, w, k in (("cq", OC_Q, C_QRANK, 0), ("ckv", OC_KV, C_KVRANK, 1)):
                        v = mix[:, i, o:o + w]
                        ins = nc.vector.scalar_tensor_tensor(out=v, in0=v, scalar=r[:, k:k + 1], in1=g1(n),
                                                             op0=ALU.mult, op1=ALU.mult)
                ins.then_inc(s_prep, 1)

            def prep_a(m, i):
                qk = mix[:, i, 0:OA_V]
                n = A_HEADS + A_KV
                link(m, nc.vector.tensor_tensor(ropeU, qk, qk, ALU.mult))
                ms = slot(m)[:, 0:n]
                link(m, nc.vector.tensor_reduce(ms, heads(ropeU, n), AX.X, ALU.add))
                r = power(m, nc.vector.tensor_scalar(ms, ms, 1.0 / A_DIM, EPS, ALU.mult, ALU.add))
                link(m, nc.vector.tensor_tensor(heads(qk, n), heads(qk, n), each(r[:, 0:n], A_DIM), ALU.mult))
                q, k = qk[:, 0:OA_K], qk[:, OA_K:]
                nc.vector.tensor_tensor(heads(q, A_HEADS), heads(q, A_HEADS), over(g1("aq"), A_HEADS), ALU.mult)
                link(m, nc.vector.tensor_tensor(heads(k, A_KV), heads(k, A_KV), over(g1("ak"), A_KV), ALU.mult))
                u, v = rotate(m, heads(qk, n), None, table(i, 0, 64), table(i, 64, 64), 2, ropeU, ropeV)
                order = lambda t: t[:, 0:A_HEADS].rearrange("p (g c) d -> p g c d", g=A_KV)
                nc.vector.tensor_tensor(q.rearrange("p (c g d) -> p g c d", c=4, g=A_KV), order(u), order(v), ALU.add)
                ins = nc.vector.tensor_tensor(heads(k, A_KV), u[:, A_HEADS:], v[:, A_HEADS:], ALU.add)
                if i == NTOK - 1:
                    ins.then_inc(s_prep, 1)
                else:
                    link(m, ins)

            def prep_b(m, i):
                v = heads(mix[:, i, OB_Q:OB_V], 4 * B_HEADS)[:, :, 0:B_ROT]
                u, w = rotate(m, v, None, table(i, 128, 8), table(i, 136, 8), 1, scr[:, 0:256], scr[:, 256:512])
                ins = nc.vector.tensor_tensor(v, u, w, ALU.add)
                if i == NTOK - 1:
                    ins.then_inc(s_prep, 1)
                else:
                    link(m, ins)

            def prep_c(m):
                for i in range(NTOK):
                    cos, sin = table(i, 144, 32), table(i, 176, 32)
                    q = heads(q_c[:, i], C_HEADS)[:, :, C_NOPE:]
                    u, v = rotate(m, q, None, cos, sin, 1, scr[:, 0:256], scr[:, 256:512])
                    link(m, nc.vector.tensor_tensor(q, u, v, ALU.add))
                    k = heads(mix[:, i, OC_KR:MIX_W], 1)
                    u, v = rotate(m, k, None, cos, sin, 1, scr[:, 0:256], scr[:, 256:512])
                    link(m, nc.vector.tensor_tensor(k, u, v, ALU.add))
                    ins = nc.vector.tensor_copy(heads(k_c[:, i], C_HEADS)[:, :, C_NOPE:],
                                                over(mix[:, i, OC_KR:MIX_W], C_HEADS))
                ins.then_inc(s_prep, 1)

            def lambdas(m):
                l = g1("lam")
                for k in range(2):
                    ins = nc.vector.tensor_tensor_reduce(
                        out=scr[:, 0:B_QK], in0=l[:, 2 * k * B_QK:(2 * k + 1) * B_QK],
                        in1=l[:, (2 * k + 1) * B_QK:(2 * k + 2) * B_QK], scale=1.0, scalar=0.0,
                        op0=ALU.mult, op1=ALU.add, accum_out=lam[:, k:k + 1])
                    if k == 0:
                        link(m, ins)
                ins.then_inc(s_lam, 1)
                dve.wait_ge(s_lame, m.turn + 1)
                link(m, nc.vector.scalar_tensor_tensor(
                    out=lam[:, 4:5], in0=lam[:, 2:3], scalar=lam[:, 3:4], in1=g1("linit")[:, 0:1],
                    op0=ALU.subtract, op1=ALU.add))

            def combine(m, h):
                n = 8 + 2 * h
                p0, p1 = n % 4, (n + 1) % 4
                dve.wait_ge(s_pr, m.at("sb", n + 2))
                link(m, nc.vector.reciprocal(rinv[:, n:n + 2], rowsum[:, n:n + 2]))
                link(m, nc.vector.tensor_scalar(rinv[:, n + 1], rinv[:, n + 1], lam[:, 4:5], None, ALU.mult))
                for i in range(NTOK):
                    ins = nc.vector.tensor_scalar(probs[:, p1, i], probs[:, p1, i], rinv[:, n + 1, i:i + 1], None,
                                                  ALU.mult)
                link(m, ins)
                for i in range(NTOK):
                    ins = nc.vector.scalar_tensor_tensor(
                        out=probs[:, p0, i], in0=probs[:, p0, i], scalar=rinv[:, n, i:i + 1], in1=probs[:, p1, i],
                        op0=ALU.mult, op1=ALU.subtract)
                ins.then_inc(s_pw, 1)

            def finish_b(m):
                dve.wait_ge(s_o, m.at("br", 2))
                for i in range(NTOK):
                    y = mix[:, i, OB_Q:OB_Q + YW]
                    link(m, nc.vector.tensor_copy(y, psum[:, SETS["C"][i]]))
                    link(m, nc.vector.tensor_tensor(scr[:], y, y, ALU.mult))
                    ms = slot(m)[:, 0:B_HEADS]
                    link(m, nc.vector.tensor_reduce(ms, heads(scr[:], B_HEADS), AX.X, ALU.add))
                    r = power(m, nc.vector.tensor_scalar(ms, ms, 1.0 / HV, EPS, ALU.mult, ALU.add))
                    link(m, nc.vector.tensor_tensor(heads(y, B_HEADS), heads(y, B_HEADS), each(r[:, 0:B_HEADS], HV),
                                                    ALU.mult))
                    ins = nc.vector.scalar_tensor_tensor(
                        out=heads(y, B_HEADS), in0=heads(y, B_HEADS), scalar=g1("linit")[:, 1:2],
                        in1=over(g1("sub"), B_HEADS), op0=ALU.mult, op1=ALU.mult)
                    if i == 0:
                        link(m, ins)
                ins.then_inc(s_y, 1)

            chain["rise"] = STEP_LAYER1
            with dve.Fori(0, DEPTH) as r:
                m = span1(r)
                chain["n"] = powers[0] = split_turns[0] = 0
                low(m, 0)
                dve.wait_ge(s_gain, 16 * (r + 1))
                norm(m, G1["ln1"][0], xn)
                quarter_low(m, "ln1")
                lambdas(m)
                for g in range(12):
                    ahead(m, 2 * g)
                    ahead(m, 2 * g + 1)
                    if g == 6:
                        dve.wait_ge(s_free["A"], m.at("fA", 6))
                        dve.wait_ge(s_free["B"], m.at("fB", 6))
                        prep_latents(m)
                    elif g == 7:
                        prep_a(m, 0)
                    elif g == 8:
                        prep_a(m, 1)
                    elif g == 9:
                        prep_b(m, 0)
                        prep_b(m, 1)
                for i in range(NTOK):
                    c = slice(i * P, (i + 1) * P)
                    turned_low(m, m.start["cc"] + 2 * i, slice(0, 3), c, 3, P)
                    turned_low(m, m.start["cc"] + 2 * i + 1, slice(3, 5), c, 2, P)
                for j in range(T_UQ, T_BR):
                    ahead(m, j)
                dve.wait_ge(s_free["B"], m.at("fB", 16))
                prep_c(m)
                softmax_heads(m, 0, "pa")
                divide(m, 0, 0, lambda i: mix[:, i, 0:YW])
                for h in range(2):
                    row_max(m, 8 + 2 * h)
                    row_max(m, 9 + 2 * h)
                for h in range(B_HEADS):
                    combine(m, h)
                    if h + 2 < B_HEADS:
                        row_max(m, 12 + 2 * h)
                        row_max(m, 13 + 2 * h)
                finish_b(m)
                softmax_heads(m, 24, "pc")
                divide(m, 24, 2, lambda i: mix[:, i, OB_K:OB_K + YW])
                for n in range(NBR):
                    for i in range(NTOK):
                        turned_low(m, m.start["y"] + 2 * n + i, slice(4 * n, 4 * n + 4),
                                   slice(i * P, (i + 1) * P), 4, P)
                for n in range(NBR):
                    for h in range(2):
                        key, use = "AB"[h], 8 + n
                        ahead(m, T_BR + 2 * n + h)
                        dve.wait_ge(s_used, m.at("used", T_BR + 2 * n + h + 1))
                        for i in range(NTOK):
                            mg = merged[:, i, h * W:(h + 1) * W]
                            gt = gts[:, i, n * D + h * W:n * D + (h + 1) * W]
                            dst = mg if n == 0 else heads(scr[:], 1)[:, 0]
                            nc.vector.tensor_tensor(dst, psum[:, SETS[key][i]], gt, ALU.mult)\
                              .then_inc(s_free[key], 1)
                            if n:
                                dve.wait_ge(s_free[key], m.at("f" + key, NTOK * use + i + 1))
                                ins = nc.vector.tensor_tensor(mg, mg, scr[:], ALU.add)
                                if n < NBR - 1 or i == 0 or h == 0:
                                    link(m, ins)
                                else:
                                    ins.then_inc(s_mrg, 1)
                        if n == 0:
                            dve.wait_ge(s_free[key], m.at("f" + key, NTOK * (use + 1)))
                quarter_low(m, "mrg")
                for h in range(2):
                    ahead(m, T_OUT + 2 * h)
                    ahead(m, T_OUT + 2 * h + 1)
                    accumulate(m, "AB"[h], 11, h, T_OUT + 2 * h + 1)
                norm(m, G1["ln2"][0], xn)
                quarter_low(m, "ln2")
                ffn(m, FF1_STEPS, T_FF, D_FF, 12)
                accumulate(m, "B", 12, 0, len(tiles1) - 2)
                accumulate(m, "C", 0, 1, len(tiles1) - 1)
                assert chain["n"] == STEP_LAYER1, chain
            chain.update(base=DEPTH * STEP_LAYER1, n=0, rise=0)
            powers[0] = split_turns[0] = 0
            dve.wait_ge(s_gain2, 32)
            norm(spanf, 2 * D, x_sb)
            dve.wait_ge(s_xn, spanf.at("xn", NTOK))

            def mixer2(m, gains_in, ffn_gain_in):
                powers[0] = split_turns[0] = 0
                low(m, 0)
                dve.wait_ge(s_gain2, gains_in)
                norm(m, G2["mix"][0], xn)
                quarter_low(m, "mix")
                for g in range(4):
                    ahead(m, 2 * g)
                    ahead(m, 2 * g + 1)
                for n in range(2):
                    turned_low(m, m.start["dt"] + n, slice(8 + 2 * n, 10 + 2 * n), slice(0, S), 2, S)
                ahead(m, T_POOL)
                def masked_max(n):
                    dve.wait_ge(s_sc, m.at("sb", n + 1))
                    link(m, nc.vector.tensor_tensor(probs[:, n % 4], psum[:, n % 4].rearrange(
                        "p (i k) -> p i k", i=NTOK), mask, ALU.add))
                    nc.vector.tensor_reduce(negmax[:, n], probs[:, n % 4], AX.X, ALU.max, negate=True)\
                      .then_inc(s_nm, 1)

                def counted(n):
                    dve.wait_ge(s_pr, m.at("sb", n + 1))
                    for i in range(NTOK):
                        ins = nc.vector.tensor_tensor_reduce(
                            out=probs[:, n % 4, i], in0=probs[:, n % 4, i], in1=count[:, i], scale=1.0, scalar=0.0,
                            op0=ALU.mult, op1=ALU.add, accum_out=rowsum[:, n, i:i + 1])
                    ins.then_inc(s_pw, 1)

                dve.wait_ge(s_big, 16)
                for n in range(3):
                    masked_max(n)
                counted(0)
                for n in range(HEADS):
                    if n + 1 < HEADS:
                        counted(n + 1)
                    turned_probs(m, m.start["p2"] + n, n)
                    if n + 3 < HEADS:
                        masked_max(n + 3)
                divide(m, 0, 0, lambda i: o_2[:, i])
                dve.wait_ge(s_y, YS + 1 if m is span2 else YS + 2)
                for i in range(NTOK):
                    rms(m, z_2[:, i], gains[:, G2["pool"][0]:G2["pool"][1]], z_2[:, i], scr[:], W)
                    ins = rms(m, o_2[:, i], gains[:, G2["attn"][0]:G2["attn"][1]], o_2[:, i], scr[:], W)
                ins.then_inc(s_mrg, 1)
                quarter_low(m, "y2")
                for h in range(2):
                    ahead(m, T_OUT2 + 2 * h)
                    ahead(m, T_OUT2 + 2 * h + 1)
                    accumulate(m, "BA"[h], 2 + h, h, T_OUT2 + 2 * h + 1)
                dve.wait_ge(s_gain2, ffn_gain_in)
                norm(m, G2["ffn"][0], xn)
                quarter_low(m, "ffn")

            YS = DEPTH * NBR
            mixer2(span2, 32, 48)
            ffn(span2, FF2_STEPS, T_FF2, D_FF2, 4)
            accumulate(span2, "B", 3, 0, len(tiles2) - 2)
            accumulate(span2, "C", 0, 1, len(tiles2) - 1)
            mixer2(span3, 64, 64)

            m = span3
            b = m.bank(m.start["rt"])
            dve.wait_ge(s_tp, m.at("tp", m.start["rt"] + 1))
            logits = route[:, 0:16].rearrange("p (i e) -> p i e", i=NTOK)
            ins = nc.vector.tensor_copy(logits, psum[:, TB[b], 0:16].rearrange("p (i e) -> p i e", i=NTOK))
            ins.then_inc(s_tf[b], 1)
            dve.wait_ge(s_tf[b], m.turned(m.start["rt"]))
            best, place = (route[:, 32 + 16 * k:48 + 16 * k].rearrange("p (i e) -> p i e", i=NTOK) for k in range(2))
            for i in range(NTOK):
                link(m, nc.vector.max(best[:, i], logits[:, i]))
                link(m, nc.vector.max_index(route_i[:], best[:, i], logits[:, i]))
                link(m, nc.vector.tensor_copy(place[:, i], route_i[:]))
                ins = nc.vector.tensor_tensor(route[:, 16 + i:17 + i], best[:, i, 1:2], best[:, i, 0:1], ALU.subtract)
                if i == 0:
                    link(m, ins)
            ins.then_inc(s_rt, 1)
            dve.wait_ge(s_rte, 1)
            e_, w1, w2, tmp = (route[:, k:k + w] for k, w in ((24, 2), (64, 2), (66, 2), (72, 16)))
            link(m, nc.vector.tensor_scalar(w1, e_, 1.0, None, ALU.add))
            link(m, nc.vector.reciprocal(w1, w1))
            link(m, nc.vector.tensor_tensor(w2, e_, w1, ALU.mult))
            for i in range(NTOK):
                nc.vector.tensor_scalar(tmp[:, 0:8], iota, place[:, i, 0:1], w1[:, i:i + 1], ALU.is_equal, ALU.mult)
                link(m, nc.vector.tensor_scalar(tmp[:, 8:16], iota, place[:, i, 1:2], w2[:, i:i + 1],
                                                ALU.is_equal, ALU.mult))
                link(m, nc.vector.tensor_tensor(gate_e[:, :, i], tmp[:, 0:8], tmp[:, 8:16], ALU.add))

            def weighted(m, e):
                link(m, nc.vector.tensor_copy(gate_c[:], e))
                dve.wait_ge(s_used, m.at("used", 0))
                for half, key in enumerate("BC"):
                    for i in range(NTOK):
                        xs = x_sb[:, i, half * W:(half + 1) * W]
                        nc.vector.scalar_tensor_tensor(out=xs, in0=psum[:, SETS[key][i]], scalar=gate_c[:, i:i + 1],
                                                       in1=xs, op0=ALU.mult, op1=ALU.add).then_inc(s_free[key], 1)

            split_turns[0] = 0
            low(spane(0), 0)
            ffn(spane(0), FFE_STEPS, 0, D_FFE, 0)
            chain.update(base=chain["base"] + chain["n"] - STEP_EXPERT, rise=STEP_EXPERT)
            with dve.Fori(1, NEXP) as e:
                m = spane(e)
                chain["n"] = split_turns[0] = 0
                low(m, 0)
                weighted(m, gate_e[:, bass.ds(e - 1, 1), :].rearrange("p a i -> p (a i)"))
                ffn(m, FFE_STEPS, 0, D_FFE, 0)
                assert chain["n"] == STEP_EXPERT, chain
            chain.update(base=chain["base"] + NEXP * STEP_EXPERT, n=0, rise=0)
            m = spang
            powers[0] = 0
            weighted(m, gate_e[:, NEXP - 1])
            dve.wait_ge(s_free["C"], m.at("fC", 0))
            dve.wait_ge(s_gain2, 80)
            norm(m, 0, xn)

        @block.tensor
        def _(pe):
            for key in "ABC":
                pe.sem_inc(s_free[key], NTOK)
            for b in range(2):
                pe.sem_inc(s_tf[b], 1)
            pe.wait_ge(s_in, 32)

            def turn(m, k, blocks):
                b = m.bank(k)
                pe.wait_ge(s_tf[b], m.empty(k))
                for n, src in enumerate(blocks):
                    c = src.shape[-1]
                    ins = nc.tensor.transpose(psum[0:c, TB[b], n * P:(n + 1) * P], src, ident)
                ins.then_inc(s_tp, 1)

            def turned(m, k0, n):
                for k in range(max(k0, k0 + n - 2), k0 + n):
                    pe.wait_ge(s_tf[m.bank(k)], m.turned(k))

            def parts(v, n, w=P):
                return [v[:, k * w:(k + 1) * w] for k in range(n)]

            def free(m, key, use):
                pe.wait_ge(s_free[key], m.at("f" + key, NTOK * use))

            def group(m, j, ntiles, key, use, chunk=0, per=4):
                free(m, key, use)
                for k in range(ntiles):
                    product(m, j + k, key, chunk + per * k, k == 0, k == ntiles - 1)

            def product(m, j, key, chunk, first, last):
                t, (_, n, w) = m.tile(j) % SPLIT, m.tiles[j]
                pe.wait_ge(s_lo, m.at("lo", j + 1))
                for i in range(NTOK):
                    o = psum[:, SETS[key][i], 0:w]
                    for c in range(n):
                        hh, hl = (hT[:, k, chunk + c, i * P:(i + 1) * P] for k in range(2))
                        wh, wl = (t_[:, t, c * w:(c + 1) * w] for t_ in (whi, wlo))
                        nc.tensor.matmul(o, hh, wh, start=first and c == 0, stop=False)
                        nc.tensor.matmul(o, hh, wl, start=False, stop=False)
                        ins = nc.tensor.matmul(o, hl, wh, start=False, stop=last and c == n - 1)
                ins.then_inc(s_used, 1)

            def norm_turns(m, stage):
                for i in range(NTOK):
                    pe.wait_ge(s_xn, m.at("xn", {"ln1": 0, "mix": 0}.get(stage, NTOK) + i + 1))
                    for c in range(2):
                        turn(m, m.start[stage] + 2 * i + c, parts(xn[:, i, c * W:(c + 1) * W], 4))
                turned(m, m.start[stage], 4)

            def scores(m, n, q, k):
                if n >= 4:
                    pe.wait_ge(s_pr, m.at("sb", n - 3))
                for i in range(NTOK):
                    ins = nc.tensor.matmul(psum[:, n % 4, i * S:(i + 1) * S], q[:, i * P:(i + 1) * P], k,
                                           start=True, stop=True)
                ins.then_inc(s_sc, 1)

            def probs_turn(m, k, n):
                turn(m, k, [probs[:, n % 4, i, kb * P:(kb + 1) * P] for kb in range(2) for i in range(NTOK)])

            def values(m, k, h, v, done):
                pe.wait_ge(s_tf[m.bank(k)], m.turned(k))
                for i in range(NTOK):
                    for kb in range(2):
                        ins = nc.tensor.matmul(psum[:, SETS["C"][i], h * HV:(h + 1) * HV],
                                               probsT[:, h % 2, kb, i * P:(i + 1) * P], v(kb),
                                               start=kb == 0, stop=kb == 1)
                if done:
                    ins.then_inc(s_o, 1)

            def attend(m, n0, stage, q, k, v, per, ready):
                lead = 3 if per == 1 else 2
                for h in range(lead):
                    for b in range(per):
                        scores(m, n0 + per * h + b, q(h, b), k(h, b))
                for h in range(HEADS):
                    pe.wait_ge(*ready(h))
                    probs_turn(m, m.start[stage] + h, n0 + per * h)
                    if h + lead < HEADS:
                        for b in range(per):
                            scores(m, n0 + per * (h + lead) + b, q(h + lead, b), k(h + lead, b))
                    if h:
                        values(m, m.start[stage] + h - 1, h - 1, v(h - 1), False)
                values(m, m.start[stage] + HEADS - 1, HEADS - 1, v(HEADS - 1), True)

            def ffn(m, steps, j, hidden, a0, b0, c0):
                use, turns = a0, m.start["ff"]
                last = -(-hidden // W) - 1
                for kind, g, k in steps:
                    w = min(W, hidden - g * W)
                    if kind in ("gate", "up"):
                        if k == 0:
                            free(m, "A", use)
                        product(m, j, "A", 4 * k, k == 0, k == 1)
                        j += 1
                    elif kind in ("act_gate", "act_up"):
                        use += 1
                    elif kind == "turn":
                        pe.wait_ge(s_free["A"], m.at("fA", NTOK * use))
                        for i in range(NTOK):
                            turn(m, turns, parts(ff_a[:, i], w // P))
                            turns += 1
                    elif kind == "down":
                        key = "BC"[k]
                        if g == 0:
                            free(m, key, (b0, c0)[k])
                        if k == 0:
                            turned(m, turns - 2, 2)
                        product(m, j, key, 8 + 4 * (g % 2), g == 0, g == last)
                        j += 1

            with pe.Fori(0, DEPTH) as r:
                m = span1(r)
                norm_turns(m, "ln1")
                for g in range(12):
                    group(m, 2 * g, 2, "AB"[g % 2], g // 2)
                pe.wait_ge(s_prep, m.at("prep", 1))
                for i in range(NTOK):
                    turn(m, m.start["cc"] + 2 * i, parts(mix[:, i, OC_Q:], 3))
                    turn(m, m.start["cc"] + 2 * i + 1, parts(mix[:, i, OC_KV:], 2))
                turned(m, m.start["cc"], 4)
                for g in range(2):
                    group(m, T_UQ + g, 1, "AB"[g], 6)
                for g in range(2):
                    group(m, T_UKV + 2 * g, 2, "AB"[g], 7, chunk=3, per=1)
                pe.wait_ge(s_prep, m.at("prep", 2))
                for i in range(NTOK):
                    turn(m, m.start["qa"] + i, parts(mix[:, i, 0:], 4))
                for i in range(NTOK):
                    turn(m, m.start["ka"] + i, parts(mix[:, i, OA_K:], 1))
                pe.wait_ge(s_prep, m.at("prep", 3))
                for i in range(NTOK):
                    turn(m, m.start["qb"] + i, parts(mix[:, i, OB_Q:], 4))
                for i in range(NTOK):
                    turn(m, m.start["kb"] + i, parts(mix[:, i, OB_K:], 4))
                for key, use in (("A", 8), ("B", 8), ("C", 0)):
                    free(m, key, use)
                turned(m, m.start["qa"], 8)
                hp = lambda h: slice(64 * (h // 4), 64 * (h // 4) + 64)
                attend(m, 0, "pa", lambda h, b: qT_a[hp(h), h % 4], lambda h, b: kT_a[hp(h), 0],
                       lambda h: lambda kb: mix[:, kb, OA_V + HV * (h // 4):OA_V + HV * (h // 4) + HV],
                       1, lambda h: (s_pr, m.at("sb", h + 1)))
                pe.wait_ge(s_y, m.at("br", 1))
                cp = lambda h, b: slice(32 * ((2 * h + b) % 4), 32 * ((2 * h + b) % 4) + 32)
                attend(m, 8, "pb", lambda h, b: qT_b[cp(h, b), h // 2], lambda h, b: kT_b[cp(h, b), h // 2],
                       lambda h: lambda kb: mix[:, kb, OB_V + HV * h:OB_V + HV * (h + 1)],
                       2, lambda h: (s_pw, m.turn * B_HEADS + (h + 1)))
                pe.wait_ge(s_prep, m.at("prep", 4))
                for stage, v in (("qc", q_c), ("kc", k_c)):
                    for n in range(4):
                        i, c = n // 2, n % 2
                        turn(m, m.start[stage] + n, parts(v[:, i, 4 * c * C_DIM:], 4, C_DIM))
                turned(m, m.start["kc"], 4)
                pe.wait_ge(s_y, m.at("br", 2))
                attend(m, 24, "pc", lambda h, b: qT_c[0:C_DIM, h], lambda h, b: kT_c[0:C_DIM, h],
                       lambda h: lambda kb: v_c[:, kb, HV * h:HV * (h + 1)],
                       1, lambda h: (s_pr, m.at("sb", 24 + h + 1)))
                pe.wait_ge(s_y, m.at("br", 3))
                for n, o in enumerate((0, OB_Q, OB_K)):
                    for i in range(NTOK):
                        turn(m, m.start["y"] + 2 * n + i, parts(mix[:, i, o:], 4))
                turned(m, m.start["y"], 6)
                for n in range(NBR):
                    for h in range(2):
                        group(m, T_BR + 2 * n + h, 1, "AB"[h], 8 + n, chunk=4 * n)
                pe.wait_ge(s_mrg, m.turn + 1)
                for i in range(NTOK):
                    for c in range(2):
                        turn(m, m.start["mrg"] + 2 * i + c, parts(merged[:, i, c * W:], 4))
                turned(m, m.start["mrg"], 4)
                for h in range(2):
                    group(m, T_OUT + 2 * h, 2, "AB"[h], 11)
                norm_turns(m, "ln2")
                ffn(m, FF1_STEPS, T_FF, D_FF, 12, 12, 0)

            def mixer2(m, n):
                norm_turns(m, "mix")
                for g in range(4):
                    group(m, 2 * g, 2, "AB"[g % 2], g // 2)
                free(m, "A", 2)
                free(m, "B", 2)
                pe.wait_ge(s_big, 16)
                for t in range(2):
                    b = m.bank(m.start["dt"] + t)
                    pe.wait_ge(s_tf[b], m.empty(m.start["dt"] + t))
                    for g in range(2):
                        for i in range(NTOK):
                            c = (2 * t + g) * P
                            ins = nc.tensor.matmul(psum[:, TB[b], g * S:(g + 1) * S], mix2[:, i, c:c + P],
                                                   poolT[:, i, 2 * t + g], start=i == 0, stop=i == 1)
                    ins.then_inc(s_tp, 1)
                turned(m, m.start["dt"], 2)
                pe.wait_ge(s_lo, m.at("lo", T_POOL + 1))
                w_buf = m.tile(T_POOL) % SPLIT
                for i in range(NTOK):
                    for g in range(4):
                        o = psum[:, SETS["A"][i], g * P:(g + 1) * P]
                        hh, hl = (hT[:, k, 8 + g, i * P:(i + 1) * P] for k in range(2))
                        wh, wl = (t_[:, w_buf, g * P:(g + 1) * P] for t_ in (whi, wlo))
                        nc.tensor.matmul(o, hh, wh, start=True, stop=False)
                        nc.tensor.matmul(o, hh, wl, start=False, stop=False)
                        ins = nc.tensor.matmul(o, hl, wh, start=False, stop=True)
                ins.then_inc(s_used, 1)
                for stage, o in (("q2", W), ("k2", 2 * W)):
                    for i in range(NTOK):
                        turn(m, m.start[stage] + i, parts(mix2[:, i, o:], 4))
                turned(m, m.start["q2"], 4)
                for key, use in (("A", 3), ("B", 2), ("C", 0)):
                    free(m, key, use)
                hp = lambda h: slice(64 * (h % 2), 64 * (h % 2) + 64)
                attend(m, 0, "p2", lambda h, b: qT_2[hp(h), h // 2], lambda h, b: kT_2[hp(h), h // 2],
                       lambda h: lambda kb: mix2[:, kb, 3 * W + HV * h:3 * W + HV * (h + 1)],
                       1, lambda h: (s_pw, DEPTH * B_HEADS + n * HEADS + h + 1))
                pe.wait_ge(s_mrg, DEPTH + n + 1)
                for i in range(NTOK):
                    turn(m, m.start["y2"] + 2 * i, parts(z_2[:, i], 4))
                    turn(m, m.start["y2"] + 2 * i + 1, parts(o_2[:, i], 4))
                turned(m, m.start["y2"], 4)
                for h in range(2):
                    group(m, T_OUT2 + 2 * h, 2, "BA"[h], 2 + h)
                norm_turns(m, "ffn")

            mixer2(span2, 0)
            ffn(span2, FF2_STEPS, T_FF2, D_FF2, 4, 3, 0)
            mixer2(span3, 1)
            m = span3
            b = m.bank(m.start["rt"])
            pe.wait_ge(s_wr, 16)
            pe.wait_ge(s_tf[b], m.empty(m.start["rt"]))
            for i in range(NTOK):
                for c in range(KD):
                    for k in range(2):
                        ins = nc.tensor.matmul(psum[:, TB[b], i * NEXP:(i + 1) * NEXP],
                                               hT[:, k, c, i * P:(i + 1) * P].bitcast(F32), w_route[:, c],
                                               start=c == 0 and k == 0, stop=c == KD - 1 and k == 1)
            ins.then_inc(s_tp, 1)
            with pe.Fori(0, NEXP) as e:
                ffn(spane(e), FFE_STEPS, 0, D_FFE, 0, 0, 0)


DIRECT = ["x", "w_in", "c_w_uq", "c_w_ukv", "w_branch", "w_out", "w_ff1", "w_ff2", "final_g", "w_in_2", "w_pool_2",
          "w_out_2", "ffn_wg_2", "ffn_wu_2", "ffn_wd_2", "w_router_2", "moe_wg_2", "moe_wu_2", "moe_wd_2",
          "final_norm_2"]


def kernel(**inputs):
    import concourse.bacc as bacc
    from concourse.bass_utils import run_bass_kernel_spmd

    nc = bacc.Bacc("TRN2", target_bir_lowering=False, num_devices=1)
    arrays = {n: np.ascontiguousarray(inputs[n]) for n in DIRECT}
    init = [0.8 - 0.6 * math.exp(-0.3 * l) for l in range(DEPTH)]
    rows = [inputs[n].reshape(DEPTH, -1) for n in ("ln1_g", "ln2_g", "a_q_norm", "a_k_norm", "b_subln", "c_q_norm",
                                                   "c_kv_norm", "b_lambda")]
    rows.append(np.array([[v, 1.0 - v] for v in init], np.float32))
    arrays["gains1"] = np.ascontiguousarray(np.concatenate(rows, 1))
    arrays["gains2"] = np.ascontiguousarray(np.concatenate(
        [inputs[n] for n in ("norm_mix_2", "pool_scale_2", "attn_gain_2", "norm_ffn_2")], 1))
    arrays["tables"], arrays["big"] = make_tables()
    args = {n: nc.dram_tensor(f"in_{n}", v.shape, mybir.dt.from_np(v.dtype), kind="ExternalInput").ap()
            for n, v in arrays.items()}
    out = nc.dram_tensor("out_0", (1, S, D), F32, kind="ExternalOutput").ap()
    build(nc, args, out)
    r = run_bass_kernel_spmd(nc, [{f"in_{n}": v for n, v in arrays.items()}], core_ids=[0])
    return r.results[0]["out_0"]
```

```python
import math
from contextlib import ExitStack

import concourse.bass as bass
import numpy as np
from concourse import mybir

F32 = mybir.dt.float32
F32R = mybir.dt.float32r
U32 = mybir.dt.uint32
ALU = mybir.AluOpType
ACT = mybir.ActivationFunctionType
AX = mybir.AxisListType

D, S, DEPTH, GRID_W, EPS = 1024, 256, 2, 64, 1e-6
P = 128
NTOK = S // P
KD = D // P
A_HEADS, A_KV, A_DIM = 8, 2, 64
B_HEADS, B_QK, B_ROT = 8, 32, 8
C_HEADS, C_QRANK, C_KVRANK, C_NOPE, C_ROPE, C_V = 8, 384, 256, 64, 32, 64
C_DIM = C_NOPE + C_ROPE
HV = 64
HEADS = 8
YW = HEADS * HV
NBR = 3
D_FF, D_FF2, D_FFE, NEXP = 4096, 2816, 3584, 8
POOL_WINDOWS = (2, 4, 8, 16)
PATTERNS = ((128, 1), (512, 4), (2048, 16))
W = 512

OA_Q, OA_K, OA_V = 0, 512, 640
OB_Q, OB_K, OB_V = 768, 1280, 1792
OC_Q, OC_KV, OC_KR = 2304, 2688, 2944
MIX_W = 2976
GATE_W = NBR * D

G1 = {}
_at = 0
for _n, _w in (("ln1", D), ("ln2", D), ("aq", A_DIM), ("ak", A_DIM), ("sub", HV), ("cq", C_QRANK),
               ("ckv", C_KVRANK), ("lam", 4 * B_QK), ("linit", 2)):
    G1[_n] = (_at, _at + _w)
    _at += _w
G1_W = _at
G2 = {"mix": (0, D), "pool": (D, D + 512), "attn": (D + 512, 2 * D), "ffn": (2 * D, 3 * D)}
G2_W = 3 * D

ROPE_W = 2 * (64 + B_ROT + C_ROPE)
TAB_W = P + NTOK * ROPE_W + P
BIG_W = 2 * NTOK * S + NTOK * len(POOL_WINDOWS) * S + 2 * P


def rope_rows(pos, dim, theta):
    inv = np.float32(theta) ** (-np.arange(0, dim, 2, dtype=np.float32) / np.float32(dim))
    ang = pos.astype(np.float32)[:, None] * inv[None, :].astype(np.float32)
    c, s = np.cos(ang), np.sin(ang)
    return np.concatenate([c, c], 1), np.concatenate([-s, s], 1)


def make_tables():
    t = np.arange(S)
    row, col = rope_rows(t // GRID_W, 32, 10000.0), rope_rows(t % GRID_W, 32, 10000.0)
    b, c = rope_rows(t, B_ROT, 500000.0), rope_rows(t, C_ROPE, 10000.0)
    rope = np.concatenate([row[0], col[0], row[1], col[1], b[0], b[1], c[0], c[1]], 1)
    rope = rope.reshape(NTOK, P, ROPE_W).transpose(1, 0, 2).reshape(P, -1)
    iota = np.tile(np.arange(P), (P, 1))
    small = np.concatenate([np.eye(P), rope, iota], 1).astype(np.float32)
    d = t[:, None] - t[None, :]
    count = sum(((d >= 0) & (d % dil == 0) & (d <= win)).astype(np.float32) for win, dil in PATTERNS)
    mask = np.where(count > 0, 0.0, -1e30)
    pool = []
    for w in POOL_WINDOWS:
        n = np.minimum(t + 1, w).astype(np.float32)
        pool.append((((d >= 0) & (d < w)) / n[:, None] - np.eye(S)).T)
    pool = np.stack(pool, 1)
    tiles = lambda a: a.reshape(NTOK, P, -1).transpose(1, 0, 2).reshape(P, -1)
    earlier = np.triu(np.ones((P, P)), 1)
    big = np.concatenate([tiles(count), tiles(mask), tiles(pool), earlier, np.ones((P, P))], 1).astype(np.float32)
    return small, big


def columns(w, rows, c0, width, k0=0, per=4):
    for k in range(0, rows, per * P):
        n = min(per * P, rows - k) // P
        yield (lambda r, k=k, n=n: w(r, k0 + k, n * P, c0, width).rearrange("(c p) n -> p c n", p=P), n, width)


def at_layer(w, rows):
    flat = w.rearrange("l r n -> (l r) n")

    def get(layer, k, n, c0, width):
        if isinstance(layer, int):
            return flat[layer * rows + k:layer * rows + k + n, c0:c0 + width]
        return flat[bass.ds(layer * rows + k, n), c0:c0 + width]
    return get


def ffn_steps(groups, gated):
    up = ("gate", "up") if gated else ("up",)
    for g in range(groups + 1):
        for n, kind in enumerate(up):
            if g < groups:
                yield kind, g, 0
                if n == 0 and g:
                    yield "turn", g - 1, 0
                yield kind, g, 1
                yield "act_" + kind, g, 0
            elif n == 0:
                yield "turn", g - 1, 0
            if g:
                if gated:
                    yield "down", g - 1, n
                else:
                    yield "down", g - 1, 0
                    yield "down", g - 1, 1


FF1_STEPS = list(ffn_steps(D_FF // W, False))
FF2_STEPS = list(ffn_steps(-(-D_FF2 // W), True))
FFE_STEPS = list(ffn_steps(D_FFE // W, True))
TILE_STEPS = ("gate", "up", "down")


def ffn_tiles(steps, gate, up, down, hidden):
    for kind, g, k in steps:
        w = min(W, hidden - g * W)
        if kind in ("gate", "up"):
            yield from columns(gate if kind == "gate" else up, D // 2, g * W, w, k0=k * D // 2)
        elif kind == "down":
            yield from columns(down, w, k * W, W, k0=g * W)


def halves(n):
    if n == 1:
        return [(0, 0, 1, 2)]
    return [(0, 0, -(-n // 2), 1), (1, -(-n // 2), n, 1)]


RAW, RAW_E, SPLIT = 3, 6, 2
HALVED = ("lo", "hi", "used")
CREDIT = {"lo": RAW, "used": SPLIT, "fA": NTOK, "fB": NTOK, "fC": NTOK, "xn": 1, "fG": 1}

TURNS1 = [("ln1", 4), ("cc", 4), ("qa", 2), ("ka", 2), ("qb", 2), ("kb", 2), ("pa", 8), ("pb", 8),
          ("qc", 4), ("kc", 4), ("pc", 8), ("y", 6), ("mrg", 4), ("ln2", 4), ("ff", 16)]
TURNS2 = [("mix", 4), ("dt", 2), ("q2", 2), ("k2", 2), ("p2", 8), ("y2", 4), ("ffn", 4), ("ff", 12)]
TURNS3 = TURNS2[:-1] + [("rt", 1), ("place", 1)]
TURNSE = [("take", 2), ("give", 1), ("ff", 7)]


def starts(turns):
    out, at = {}, 0
    for name, n in turns:
        out[name] = at
        at += n
    return out, at


STEP_LAYER1 = 68
STEP_EXPERT = 3
PLAIN = ("qa", "ka", "qb", "kb", "pa", "pb", "qc", "kc", "pc", "q2", "k2", "p2", "rt", "place",
         "give")

def rises(tiles, turns, a, b, c, norms, powers, banks, branches, preps=0, relu=0):
    return dict(fG=0, lo=tiles, used=tiles, hi=tiles, tp=starts(turns)[1],
                th=sum(n for name, n in turns if name not in PLAIN), fA=NTOK * a, fB=NTOK * b, fC=NTOK * c, xn=NTOK * norms, pw=powers, sb=banks, br=branches, prep=preps, relu=relu)


R1 = rises(72, TURNS1, 20, 13, 1, 2, 10, 32, 3, 4, 16)
RF = rises(0, [], 0, 0, 0, 1, 2, 0, 0)
R2 = rises(49, TURNS2, 16, 4, 1, 2, 8, 8, 1)
R3 = rises(13, TURNS3, 4, 3, 0, 2, 8, 8, 1)
RE = rises(42, TURNSE, 0, 0, 1, 0, 0, 0, 0)
RE.update(fA=7, fB=7, fG=4)


class Span:

    def __init__(self, turns, rise, base, turn=0, tiles=(), ring=RAW, first=0):
        self.start, self.turn, self.rise, self.base = starts(turns)[0], turn, rise, base
        self.tiles, self.ring, self.first = tiles, ring, first

    def value(self, fixed, rise):
        return self.turn * rise + fixed if rise else fixed

    def at(self, name, k, part=0):
        n = 2 if name in HALVED else 1
        return self.value(n * (self.base[name] + CREDIT.get(name, 0) + k) + part, n * self.rise[name])

    def bank(self, k):
        return (self.base["tp"] + k) % 2

    def empty(self, k):
        return self.value((self.base["tp"] + k) // 2 + 1, self.rise["tp"] // 2)

    def turned(self, k):
        return self.value((self.base["tp"] + k) // 2 + 2, self.rise["tp"] // 2)

    def landed(self, j):
        return self.value(16 * ((self.tile(j) - self.first) // self.ring + 1), 16 * (self.rise["lo"] // self.ring))

    def buffer(self, j):
        return (self.tile(j) - self.first) % self.ring

    def tile(self, j):
        return self.base["lo"] + j


def after(base, rise, rounds=1):
    return {k: base[k] + rise[k] * rounds for k in rise}


BASE1 = {k: 0 for k in R1}
BASEF = after(BASE1, R1, DEPTH)
BASE2 = after(BASEF, RF)
BASE3 = after(BASE2, R2)
BASEE = after(BASE3, R3)


def build(nc, a, out):
    ctx = ExitStack()
    with ctx:
        def sb(name, shape, dt=F32):
            return ctx.enter_context(nc.sbuf_tensor(name, shape, dt))

        def sem(name):
            return ctx.enter_context(nc.semaphore(name))

        x_sb = sb("x_res", [P, NTOK, D])
        hT = sb("hT", [P, 2, 16, S], F32R)
        work = sb("work", [P, 20288])
        raw = sb("raw", [P, RAW, 4 * W])
        whi = sb("w_high", [P, SPLIT, 2, 2 * W], F32R)
        wlo = sb("w_low", [P, SPLIT, 2, 2 * W], F32R)
        gains = sb("gains", [P, G2_W])
        tab = sb("tables", [P, TAB_W])
        probs = sb("probs", [P, 4, NTOK, S])
        probsT = sb("probsT", [P, 2, NTOK, S])
        scr = sb("scratch", [P, W])
        negmax = sb("negmax", [P, 32, NTOK])
        rowsum = sb("rowsum", [P, 32, NTOK])
        rinv = sb("rinv", [P, 32, NTOK])
        meansq = sb("meansq", [P, 2, 16])
        rstd = sb("rstd", [P, 2, 16])
        neghalf = sb("neghalf", [P, 16])
        lam = sb("lam", [P, 8])
        route = sb("route", [P, 96])
        route_i = sb("route_i", [P, 8], U32)
        gate_e = sb("gate_e", [P, NEXP, NTOK])
        gate_c = sb("gate_c", [P, NTOK])
        member = sb("member", [P, NTOK, NEXP])
        place_e = sb("place_e", [P, NEXP, NTOK])
        place_c = sb("place_c", [P, NTOK])
        rounds_i = sb("rounds_i", [P, 2, NEXP], mybir.dt.int32)
        w_route = sb("w_route", [P, KD, NEXP])
        psum = ctx.enter_context(nc.psum_tensor("acc", [P, 8, W], F32))
        SETS = {"A": (0, 1), "B": (2, 3), "C": (4, 5)}
        TB = (6, 7)

        def region(at, *shape):
            n = int(np.prod(shape))
            v = work[:, at:at + n]
            return v if len(shape) == 1 else v.rearrange("p (a b) -> p a b", a=shape[0])

        mix = region(0, NTOK, MIX_W)
        gts = region(5952, NTOK, GATE_W)
        qT_a, kT_a = region(12096, 4, S), region(13120, 1, S)
        qT_b, kT_b = region(13376, 4, S), region(14400, 4, S)
        qT_c, kT_c = region(12096, HEADS, S), region(14144, HEADS, S)
        q_c = region(16192, NTOK, C_HEADS * C_DIM)
        v_c = region(17728, NTOK, YW)
        k_c = region(18752, NTOK, C_HEADS * C_DIM)
        ropeU, ropeV = region(16192, 640), region(16832, 640)
        merged = region(0, NTOK, D)
        xn = region(12096, NTOK, D)
        ff_s, ff_a = region(14144, NTOK, W), region(15168, NTOK, W)
        mix2 = region(0, NTOK, 4 * W)
        qT_2, kT_2 = region(4096, 4, S), region(5120, 4, S)
        big = region(6144, BIG_W)
        count = big[:, 0:NTOK * S].rearrange("p (a b) -> p a b", a=NTOK)
        mask = big[:, NTOK * S:2 * NTOK * S].rearrange("p (a b) -> p a b", a=NTOK)
        earlier, ones = big[:, BIG_W - 2 * P:BIG_W - P], big[:, BIG_W - P:]
        poolT = big[:, 2 * NTOK * S:BIG_W - 2 * P].rearrange("p (a g t) -> p a g t", a=NTOK, g=4)
        z_2, o_2 = region(9472, NTOK, W), region(10496, NTOK, W)
        y_e = region(16192, D)
        sel = region(17216, NTOK, P)
        sel_w = region(17472, NTOK, P)
        give = region(17728, NTOK, P)

        ident = tab[:, 0:P]
        rope = tab[:, P:P + NTOK * ROPE_W].rearrange("p (a b) -> p a b", a=NTOK)
        iota = tab[:, P + NTOK * ROPE_W:TAB_W]

        s_raw = [sem(f"raw_landed{i}") for i in range(RAW)]
        s_rawe = [sem(f"expert_raw_landed{i}") for i in range(RAW_E)]
        s_in, s_gain, s_gain2, s_big, s_wr, s_out = (sem(n) for n in (
            "inputs_landed", "gains_landed", "gains2_landed", "big_landed", "router_landed", "out_landed"))
        s_hi, s_lo, s_used = sem("w_high_ready"), sem("w_low_ready"), sem("w_tile_used")
        s_free = {k: sem(f"acc{k}_emptied") for k in "ABC"}
        s_tp = sem("turned")
        s_tf = [sem("turn_bank0_emptied"), sem("turn_bank1_emptied")]
        s_thi = sem("turned_high_ready")
        s_xn = sem("normed_ready")
        s_pow_in, s_pow = sem("meansq_ready"), sem("rstd_ready")
        s_step = sem("vector_step")
        s_prep = sem("qk_prepared")
        s_sc, s_nm, s_pr = sem("scores_ready"), sem("negmax_ready"), sem("probs_ready")
        s_pw = sem("probs_weighted")
        s_o, s_y = sem("heads_done"), sem("branch_ready")
        s_mrg = sem("merged_ready")
        s_lam, s_lame = sem("lambda_sums"), sem("lambda_exp")
        s_relu = sem("relu_ready")
        s_rt, s_rte = sem("route_diff"), sem("route_exp")
        s_member, s_rounds = sem("members_ready"), sem("rounds_ready")
        s_sel, s_back, s_given = sem("selection_ready"), sem("given_back"), sem("given_back_emptied")
        s_const = sem("constants_set")

        w_in = at_layer(a["w_in"], D)
        uq, ukv = at_layer(a["c_w_uq"], C_QRANK), at_layer(a["c_w_ukv"], C_KVRANK)
        w_br = at_layer(a["w_branch"].rearrange("l n r c -> l (n r) c"), NBR * YW)
        w_o, ff1, ff2 = at_layer(a["w_out"], D), at_layer(a["w_ff1"], D), at_layer(a["w_ff2"], D_FF)
        WIN_W = [W] * 5 + [MIX_W - 5 * W] + [W] * 6
        WIN_0 = [sum(WIN_W[:g]) for g in range(12)]
        tiles1 = []
        for g in range(12):
            tiles1 += columns(w_in, D, WIN_0[g], WIN_W[g])
        T_UQ = len(tiles1)
        UQ_W = (W, 256)
        for g in range(2):
            tiles1 += columns(uq, C_QRANK, g * W, UQ_W[g])
        T_UKV = len(tiles1)
        for g in range(2):
            tiles1 += columns(ukv, C_KVRANK, g * W, W, per=1)
        T_BR = len(tiles1)
        for n in range(NBR):
            for h in range(2):
                tiles1 += columns(w_br, YW, h * W, W, k0=n * YW)
        T_OUT = len(tiles1)
        for h in range(2):
            tiles1 += columns(w_o, D, h * W, W)
        T_FF = len(tiles1)
        tiles1 += ffn_tiles(FF1_STEPS, None, ff1, ff2, D_FF)
        assert len(tiles1) == R1["lo"]

        w_in2, w_o2 = at_layer(a["w_in_2"], D), at_layer(a["w_out_2"], D)
        w_pl = at_layer(a["w_pool_2"].rearrange("l g r c -> l (g r) c"), W)
        wg2, wu2, wd2 = at_layer(a["ffn_wg_2"], D), at_layer(a["ffn_wu_2"], D), at_layer(a["ffn_wd_2"], D_FF2)
        mixer2 = []
        for g in range(4):
            mixer2 += columns(w_in2, D, g * W, W)
        T_POOL = len(mixer2)
        mixer2 += columns(w_pl, W, 0, P)
        T_OUT2 = len(mixer2)
        for h in range(2):
            mixer2 += columns(w_o2, D, h * W, W)
        T_FF2 = len(mixer2)
        fix = lambda ts, r: [(lambda _, f=f: f(r), n, w) for f, n, w in ts]
        tiles2 = fix(mixer2, 0) + list(ffn_tiles(FF2_STEPS, wg2, wu2, wd2, D_FF2))
        tiles3 = fix(mixer2, 1)
        assert len(tiles2) == R2["lo"] and len(tiles3) == R3["lo"], (len(tiles2), len(tiles3))
        wge, wue, wde = (at_layer(a[n].rearrange("m e r c -> (m e) r c"), r) for n, r in (
            ("moe_wg_2", D), ("moe_wu_2", D), ("moe_wd_2", D_FFE)))
        tilese = list(ffn_tiles(FFE_STEPS, wge, wue, wde, D_FFE))
        assert len(tilese) == RE["lo"]

        span1 = lambda r: Span(TURNS1, R1, BASE1, r, tiles1)
        spanf = Span([], RF, BASEF)
        span2 = Span(TURNS2, R2, BASE2, 0, tiles2)
        span3 = Span(TURNS3, R3, BASE3, 0, tiles3)
        spane = lambda r: Span(TURNSE, RE, BASEE, r, tilese, RAW_E, BASEE["lo"])
        spang = Span([], RF, BASEE)

        raws = [raw[:, b] for b in range(RAW)]
        raws_e = raws + [region(4 * W * b, 4 * W) for b in range(RAW_E - RAW)]

        def raw_of(m, j):
            b = m.buffer(j)
            return (raws_e[b], s_rawe[b]) if m.ring == RAW_E else (raws[b], s_raw[b])

        def rounds(eng, body):
            eng.wait_ge(s_rounds, 1)
            with eng.Fori(0, NEXP) as e:
                n = eng.value_load(rounds_i[0:1, 0, bass.ds(e, 1)], min_val=1, max_val=2)
                before = eng.value_load(rounds_i[0:1, 1, bass.ds(e, 1)], min_val=0, max_val=2 * NEXP)
                with eng.Fori(0, n) as b:
                    body(spane(before + b), e)

        block = ctx.enter_context(nc.Block())

        @block.sync
        def _(sp):
            sp.sem_inc(s_lo, 2 * RAW)
            sp.sem_inc(s_xn, 1)
            sp.dma_start(x_sb[:], a["x"][0].rearrange("(i p) d -> p i d", p=P)).then_inc(s_in, 16)
            sp.dma_start(tab[:], a["tables"]).then_inc(s_in, 16)
            sp.dma_start(w_route[:], a["w_router_2"][0].rearrange("(c p) e -> p c e", p=P)).then_inc(s_wr, 16)

            def load(m, r, j0, j1):
                for j in range(j0, j1):
                    src, n, w = m.tiles[j]
                    buf, landed = raw_of(m, j)
                    sp.wait_ge(s_lo, m.at("lo", j + 1 - m.ring))
                    sp.dma_start(buf[:, 0:n * w].rearrange("p (c n) -> p c n", c=n), src(r)).then_inc(landed, 16)

            def gain(cols, src, done):
                sp.dma_start(gains[:, cols[0]:cols[1]], src.partition_broadcast(P)).then_inc(done, 16)

            with sp.Fori(0, DEPTH) as r:
                m = span1(r)
                sp.wait_ge(s_xn, m.at("xn", 0))
                gain((0, G1_W), a["gains1"][bass.ds(r, 1), :].rearrange("a n -> (a n)"), s_gain)
                load(m, r, 0, len(tiles1))
            sp.wait_ge(s_xn, spanf.at("xn", 0))
            gain((2 * D, 3 * D), a["final_g"], s_gain2)
            gain((0, 2 * D), a["gains2"][0, 0:2 * D], s_gain2)
            sp.dma_start(big, a["big"]).then_inc(s_big, 16)
            load(span2, 0, 0, RAW)
            sp.wait_ge(s_xn, span2.at("xn", 0))
            gain((2 * D, 3 * D), a["gains2"][0, 2 * D:3 * D], s_gain2)
            load(span2, 0, RAW, T_FF2 + RAW)
            sp.wait_ge(s_xn, span3.at("xn", 0))
            gain((0, 3 * D), a["gains2"][1, :], s_gain2)
            load(span2, 0, T_FF2 + RAW, len(tiles2))
            load(span3, 0, 0, len(tiles3))
            sp.wait_ge(s_xn, spang.at("xn", 0))
            gain((0, D), a["final_norm_2"], s_gain2)
            rounds(sp, lambda m, e: load(m, e, 0, len(tilese)))
            sp.wait_ge(s_xn, spang.at("xn", NTOK))
            sp.dma_start(out[0].rearrange("(i p) d -> p i d", p=P), xn).then_inc(s_out, 16)
            sp.wait_ge(s_out, 16)

        @block.gpsimd
        def _(pool):
            nc.gpsimd.memset(neghalf[:], -0.5).then_inc(s_const, 1)
            nc.gpsimd.memset(meansq[:], 1.0).then_inc(s_const, 1)
            pool.wait_ge(s_const, 2)
            with pool.Fori(0, (BASEE["pw"] + RF["pw"]) // 2) as r:
                for b in range(2):
                    pool.wait_ge(s_pow_in, 2 * r + (b + 1))
                    nc.gpsimd.tensor_tensor(rstd[:, b], meansq[:, b], neghalf[:], ALU.pow).then_inc(s_pow, 1)

        @block.scalar
        def _(act):
            def high(m, j):
                t = m.tile(j)
                n, w = m.tiles[j][1:]
                buf, landed = raw_of(m, j)
                act.wait_ge(landed, m.landed(j))
                for half, c0, c1, count in halves(n):
                    act.wait_ge(s_used, m.at("used", j - SPLIT, half + count))
                    nc.scalar.activation(whi[:, t % SPLIT, half, 0:(c1 - c0) * w], buf[:, c0 * w:c1 * w], ACT.Copy)\
                      .then_inc(s_hi, count)

            def ahead(m, j):
                if j + 1 < len(m.tiles):
                    high(m, j + 1)

            def turned_high(m, k, view, blocks, cols):
                b = m.bank(k)
                act.wait_ge(s_tp, m.at("tp", k + 1))
                src = psum[:, TB[b], 0:blocks * cols].rearrange("p (c t) -> p c t", c=blocks)
                nc.scalar.activation(view, src, ACT.Copy).then_inc(s_thi, 1)

            def normed_high(m, stage):
                for n in range(4):
                    i, c = n // 2, n % 2
                    turned_high(m, m.start[stage] + n, hT[:, 0, 4 * c:4 * c + 4, i * P:(i + 1) * P], 4, P)

            def plain_turn(m, k, dst, parts, blocks, cols, scale):
                b = m.bank(k)
                act.wait_ge(s_tp, m.at("tp", k + 1))
                src = psum[0:parts, TB[b], 0:blocks * cols].rearrange("p (c t) -> p c t", c=blocks)
                nc.scalar.activation(dst, src, ACT.Copy, scale=scale).then_inc(s_tf[b], 1)

            def softmax_exp(m, n):
                act.wait_ge(s_nm, m.at("sb", n + 1))
                for i in range(NTOK):
                    ins = nc.scalar.activation(probs[:, n % 4, i], psum[:, n % 4, i * S:(i + 1) * S], ACT.Exp,
                                               bias=negmax[:, n, i:i + 1], accum_out=rowsum[:, n, i:i + 1])
                ins.then_inc(s_pr, 1)

            def evac(m, key, j, dst, w, func=ACT.Copy):
                act.wait_ge(s_used, m.at("used", j + 1))
                for i in range(NTOK):
                    ins = nc.scalar.activation(dst(i), psum[:, SETS[key][i], 0:w], func)
                    ins.then_inc(s_free[key], 1)

            def ffn(m, steps, j, hidden, a0):
                use, turn, gated = a0, m.start["ff"], steps is not FF1_STEPS
                for kind, g, k in steps:
                    w = min(W, hidden - g * W)
                    if kind in TILE_STEPS:
                        ahead(m, j)
                        j += 1
                    elif kind in ("act_up", "act_gate"):
                        if kind == "act_gate":
                            evac(m, "A", j - 1, lambda i: ff_s[:, i, 0:w], w, ACT.Silu)
                        elif not gated:
                            act.wait_ge(s_used, m.at("used", j))
                            for i in range(NTOK):
                                nc.scalar.activation(ff_s[:, i, 0:w], psum[:, SETS["A"][i], 0:w], ACT.Relu)\
                                  .then_inc(s_relu, 1)
                        use += 1
                    elif kind == "turn":
                        c = 8 + 4 * (g % 2)
                        for i in range(NTOK):
                            turned_high(m, turn, hT[:, 0, c:c + w // P, i * P:(i + 1) * P], w // P, P)
                            turn += 1

            act.sem_inc(s_used, 2 * SPLIT)

            with act.Fori(0, DEPTH) as r:
                m = span1(r)
                high(m, 0)
                normed_high(m, "ln1")
                act.wait_ge(s_lam, r + 1)
                nc.scalar.activation(lam[:, 2:4], lam[:, 0:2], ACT.Exp).then_inc(s_lame, 1)
                for g in range(12):
                    ahead(m, 2 * g)
                    ahead(m, 2 * g + 1)
                    key, w = "AB"[g % 2], WIN_W[g]
                    if g < 6:
                        evac(m, key, 2 * g + 1, lambda i: mix[:, i, WIN_0[g]:WIN_0[g] + w], w)
                    else:
                        evac(m, key, 2 * g + 1, lambda i: gts[:, i, (g - 6) * W:(g - 5) * W], w, ACT.Sigmoid)
                for i in range(NTOK):
                    turned_high(m, m.start["cc"] + 2 * i, hT[:, 0, 0:3, i * P:(i + 1) * P], 3, P)
                    turned_high(m, m.start["cc"] + 2 * i + 1, hT[:, 0, 3:5, i * P:(i + 1) * P], 2, P)
                for g in range(2):
                    ahead(m, T_UQ + g)
                    evac(m, "AB"[g], T_UQ + g, lambda i: q_c[:, i, g * W:g * W + UQ_W[g]], UQ_W[g])
                for g in range(2):
                    ahead(m, T_UKV + 2 * g)
                    ahead(m, T_UKV + 2 * g + 1)
                    key = "AB"[g]
                    act.wait_ge(s_used, m.at("used", T_UKV + 2 * g + 2))
                    for i in range(NTOK):
                        src = psum[:, SETS[key][i], :].rearrange("p (h e) -> p h e", h=4)
                        kd = k_c[:, i].rearrange("p (h e) -> p h e", h=8)[:, 4 * g:4 * g + 4, 0:C_NOPE]
                        vd = v_c[:, i].rearrange("p (h e) -> p h e", h=8)[:, 4 * g:4 * g + 4, :]
                        nc.scalar.activation(kd, src[:, :, 0:C_NOPE], ACT.Copy)
                        nc.scalar.activation(vd, src[:, :, C_NOPE:], ACT.Copy).then_inc(s_free[key], 1)
                for i in range(NTOK):
                    plain_turn(m, m.start["qa"] + i, qT_a[:, :, i * P:(i + 1) * P], P, 4, P, A_DIM ** -0.5)
                for i in range(NTOK):
                    plain_turn(m, m.start["ka"] + i, kT_a[:, :, i * P:(i + 1) * P], P, 1, P, 1.0)
                for i in range(NTOK):
                    plain_turn(m, m.start["qb"] + i, qT_b[:, :, i * P:(i + 1) * P], P, 4, P, B_QK ** -0.5)
                for i in range(NTOK):
                    plain_turn(m, m.start["kb"] + i, kT_b[:, :, i * P:(i + 1) * P], P, 4, P, 1.0)
                for n in range(8):
                    softmax_exp(m, n)
                for h in range(B_HEADS + 1):
                    if h < B_HEADS:
                        softmax_exp(m, 8 + 2 * h)
                        softmax_exp(m, 9 + 2 * h)
                    if h:
                        b = m.bank(m.start["pb"] + h - 1)
                        act.wait_ge(s_tp, m.at("tp", m.start["pb"] + h))
                        nc.scalar.activation(probsT[:, (h - 1) % 2], psum[:, TB[b]].rearrange(
                            "p (c t) -> p c t", c=2), ACT.Copy).then_inc(s_tf[b], 1)
                for stage, dst, scale in (("qc", qT_c, C_DIM ** -0.5), ("kc", kT_c, 1.0)):
                    for n in range(4):
                        i, c = n // 2, n % 2
                        plain_turn(m, m.start[stage] + n, dst[0:C_DIM, 4 * c:4 * c + 4, i * P:(i + 1) * P],
                                   C_DIM, 4, P, scale)
                for n in range(24, 32):
                    softmax_exp(m, n)
                for n in range(NBR):
                    for i in range(NTOK):
                        turned_high(m, m.start["y"] + 2 * n + i, hT[:, 0, 4 * n:4 * n + 4, i * P:(i + 1) * P], 4, P)
                for j in range(T_BR, T_OUT):
                    ahead(m, j)
                normed_high(m, "mrg")
                for j in range(T_OUT, T_FF):
                    ahead(m, j)
                normed_high(m, "ln2")
                ffn(m, FF1_STEPS, T_FF, D_FF, 12)

            def mixer2_act(m):
                high(m, 0)
                normed_high(m, "mix")
                for g in range(4):
                    ahead(m, 2 * g)
                    ahead(m, 2 * g + 1)
                    evac(m, "AB"[g % 2], 2 * g + 1, lambda i: mix2[:, i, g * W:(g + 1) * W], W)
                for n in range(2):
                    turned_high(m, m.start["dt"] + n, hT[:, 0, 8 + 2 * n:10 + 2 * n, :], 2, S)
                ahead(m, T_POOL)
                evac(m, "A", T_POOL, lambda i: z_2[:, i], W)
                for stage, dst, scale in (("q2", qT_2, HV ** -0.5), ("k2", kT_2, 1.0)):
                    for i in range(NTOK):
                        plain_turn(m, m.start[stage] + i, dst[:, :, i * P:(i + 1) * P], P, 4, P, scale)
                for n in range(8):
                    act.wait_ge(s_nm, m.at("sb", n + 1))
                    for i in range(NTOK):
                        ins = nc.scalar.activation(probs[:, n % 4, i], probs[:, n % 4, i], ACT.Exp,
                                                   bias=negmax[:, n, i:i + 1])
                    ins.then_inc(s_pr, 1)
                for n in range(4):
                    i, c = n // 2, n % 2
                    turned_high(m, m.start["y2"] + n, hT[:, 0, 4 * c:4 * c + 4, i * P:(i + 1) * P], 4, P)
                for j in range(T_OUT2, T_FF2):
                    ahead(m, j)
                normed_high(m, "ffn")

            mixer2_act(span2)
            ffn(span2, FF2_STEPS, T_FF2, D_FF2, 4)
            mixer2_act(span3)
            act.wait_ge(s_rt, 1)
            nc.scalar.activation(route[:, 24:26], route[:, 16:18], ACT.Exp).then_inc(s_rte, 1)

            def expert(m, e):
                high(m, 0)
                for n in range(2):
                    turned_high(m, m.start["take"] + n, hT[:, 0, 4 * n:4 * n + 4, 0:P], 4, P)
                plain_turn(m, m.start["give"], give, P, 2, P, 1.0)
                j, turn = 0, m.start["ff"]
                for kind, g, k in FFE_STEPS:
                    if kind in TILE_STEPS:
                        ahead(m, j)
                        j += 1
                        if kind == "down" and g == D_FFE // W - 1:
                            act.wait_ge(s_used, m.at("used", j))
                            nc.scalar.activation(y_e[:, k * W:(k + 1) * W], psum[:, 2 + k], ACT.Copy)\
                              .then_inc(s_free["C"], 1)
                    elif kind == "act_gate":
                        act.wait_ge(s_used, m.at("used", j))
                        nc.scalar.activation(ff_s[:, 0], psum[:, 0], ACT.Silu).then_inc(s_free["A"], 1)
                    elif kind == "turn":
                        c = 8 + 4 * (g % 2)
                        turned_high(m, turn, hT[:, 0, c:c + 4, 0:P], 4, P)
                        turn += 1

            rounds(act, expert)

        @block.vector
        def _(dve):
            chain = {"base": 0, "n": 0, "rise": 0}
            powers = [0]

            def link(m, ins):
                chain["n"] += 1
                ins.then_inc(s_step, 1)
                fixed = chain["base"] + chain["n"]
                dve.wait_ge(s_step, m.turn * chain["rise"] + fixed if chain["rise"] else fixed)

            def low(m, j):
                t = m.tile(j)
                n, w = m.tiles[j][1:]
                for half, c0, c1, count in halves(n):
                    dve.wait_ge(s_hi, m.at("hi", j, half + count))
                    hi, lo = (t_[:, t % SPLIT, half, 0:(c1 - c0) * w] for t_ in (whi, wlo))
                    nc.vector.tensor_tensor(lo, raw_of(m, j)[0][:, c0 * w:c1 * w], hi.bitcast(F32), ALU.subtract)\
                      .then_inc(s_lo, count)

            def ahead(m, j):
                if j + 1 < len(m.tiles):
                    low(m, j + 1)

            split_turns = [0]

            def turned_low(m, k, chunks, cols, blocks, width):
                b = m.bank(k)
                split_turns[0] += 1
                dve.wait_ge(s_thi, m.at("th", split_turns[0]))
                src = psum[:, TB[b], 0:blocks * width].rearrange("p (c t) -> p c t", c=blocks)
                nc.vector.tensor_tensor(hT[:, 1, chunks, cols], src, hT[:, 0, chunks, cols].bitcast(F32),
                                        ALU.subtract).then_inc(s_tf[b], 1)

            def quarter_low(m, stage):
                for n in range(4):
                    i, c = n // 2, n % 2
                    turned_low(m, m.start[stage] + n, slice(4 * c, 4 * c + 4), slice(i * P, (i + 1) * P), 4, P)

            def slot(m):
                return meansq[:, (m.base["pw"] + powers[0]) % 2]

            def power(m, ins):
                r = rstd[:, (m.base["pw"] + powers[0]) % 2]
                powers[0] += 1
                ins.then_inc(s_pow_in, 1)
                dve.wait_ge(s_pow, m.at("pw", powers[0]))
                return r

            def rms(m, src, gain, dst, junk, n, part=None):
                r = power(m, nc.vector.tensor_tensor_reduce(out=junk, in0=src, in1=src, scale=1.0 / n, scalar=EPS,
                                                            op0=ALU.mult, op1=ALU.add, accum_out=slot(m)[:, 0:1]))
                return nc.vector.scalar_tensor_tensor(out=dst, in0=src, scalar=r[:, 0:1], in1=gain,
                                                      op0=ALU.mult, op1=ALU.mult)

            def norm(m, g0, dst):
                for i in range(NTOK):
                    rms(m, x_sb[:, i], gains[:, g0:g0 + D], dst[:, i], xn[:, i], D).then_inc(s_xn, 1)

            def over(v, h):
                return v.unsqueeze(1).broadcast_to([P, h, v.shape[-1]])

            def each(v, n):
                return v.unsqueeze(2).broadcast_to([P, v.shape[-1], n])

            def heads(v, h):
                return v.rearrange("p (h e) -> p h e", h=h)

            def rotate(m, src, dst, cos, sin, axes, u, v):
                h, w = src.shape[1], src.shape[2]
                half = w // axes // 2
                u, v = (heads(t[:, 0:h * w], h) for t in (u, v))
                nc.vector.tensor_tensor(u, src, over(cos, h), ALU.mult)
                ax = lambda t: t.rearrange("p h (a d) -> p h a d", a=axes)
                sb_ = over(sin, h)
                for o in (0, half):
                    s0 = half - o
                    if axes == 1:
                        ins = nc.vector.tensor_tensor(v[:, :, o:o + half], src[:, :, s0:s0 + half],
                                                      sb_[:, :, o:o + half], ALU.mult)
                    else:
                        ins = nc.vector.tensor_tensor(ax(v)[:, :, :, o:o + half], ax(src)[:, :, :, s0:s0 + half],
                                                      ax(sb_)[:, :, :, o:o + half], ALU.mult)
                link(m, ins)
                return u, v

            def accumulate(m, key, use, half, j):
                dve.wait_ge(s_used, m.at("used", j + 1))
                for i in range(NTOK):
                    xs = x_sb[:, i, half * W:(half + 1) * W]
                    nc.vector.tensor_tensor(xs, psum[:, SETS[key][i]], xs, ALU.add).then_inc(s_free[key], 1)
                dve.wait_ge(s_free[key], m.at("f" + key, NTOK * (use + 1)))

            def ffn(m, steps, j, hidden, a0):
                use, turn, gated = a0, m.start["ff"], steps is not FF1_STEPS
                relu = 0
                for kind, g, k in steps:
                    w = min(W, hidden - g * W)
                    if kind in TILE_STEPS:
                        ahead(m, j)
                        j += 1
                    elif kind == "act_gate":
                        use += 1
                    elif kind == "act_up":
                        dve.wait_ge(s_used, m.at("used", j))
                        for i in range(NTOK):
                            ps = psum[:, SETS["A"][i], 0:w]
                            if gated:
                                ins = nc.vector.tensor_tensor(ff_a[:, i, 0:w], ps, ff_s[:, i, 0:w], ALU.mult)
                            else:
                                relu += 1
                                dve.wait_ge(s_relu, m.at("relu", relu))
                                ins = nc.vector.scalar_tensor_tensor(out=ff_a[:, i, 0:w], in0=ps, scalar=0.0,
                                                                     in1=ff_s[:, i, 0:w], op0=ALU.max, op1=ALU.mult)
                            ins.then_inc(s_free["A"], 1)
                        use += 1
                    elif kind == "turn":
                        c = 8 + 4 * (g % 2)
                        for i in range(NTOK):
                            turned_low(m, turn, slice(c, c + w // P), slice(i * P, (i + 1) * P), w // P, P)
                            turn += 1

            def row_max(m, n):
                dve.wait_ge(s_sc, m.at("sb", n + 1))
                nc.vector.tensor_reduce(negmax[:, n], psum[:, n % 4].rearrange("p (i k) -> p i k", i=NTOK),
                                        AX.X, ALU.max, negate=True).then_inc(s_nm, 1)

            def turned_probs(m, k, h):
                b = m.bank(k)
                dve.wait_ge(s_tp, m.at("tp", k + 1))
                nc.vector.tensor_copy(probsT[:, h % 2], psum[:, TB[b]].rearrange("p (c t) -> p c t", c=2))\
                  .then_inc(s_tf[b], 1)

            def softmax_heads(m, n0, stage):
                for h in range(3):
                    row_max(m, n0 + h)
                for h in range(HEADS):
                    turned_probs(m, m.start[stage] + h, h)
                    if h + 3 < HEADS:
                        row_max(m, n0 + h + 3)

            def divide(m, n0, branch, dst):
                link(m, nc.vector.reciprocal(rinv[:, n0:n0 + HEADS], rowsum[:, n0:n0 + HEADS]))
                dve.wait_ge(s_o, m.at("br", branch + 1))
                for i in range(NTOK):
                    ins = nc.vector.tensor_tensor(heads(dst(i), HEADS), heads(psum[:, SETS["C"][i]], HEADS),
                                                  each(rinv[:, n0:n0 + HEADS, i], HV), ALU.mult)
                ins.then_inc(s_y, 1)

            def table(i, at, w):
                return rope[:, i, at:at + w]

            dve.wait_ge(s_in, 32)
            dve.wait_ge(s_const, 2)
            g1 = lambda n: gains[:, G1[n][0]:G1[n][1]]

            def prep_latents(m):
                for i in range(NTOK):
                    for n, o, w in (("cq", OC_Q, C_QRANK), ("ckv", OC_KV, C_KVRANK)):
                        v = mix[:, i, o:o + w]
                        k = 0 if n == "cq" else 1
                        ins = nc.vector.tensor_tensor_reduce(
                            out=scr[:, 0:w], in0=v, in1=v, scale=1.0 / w, scalar=EPS, op0=ALU.mult, op1=ALU.add,
                            accum_out=slot(m)[:, k:k + 1])
                        if k == 0:
                            link(m, ins)
                    r = power(m, ins)
                    for n, o, w, k in (("cq", OC_Q, C_QRANK, 0), ("ckv", OC_KV, C_KVRANK, 1)):
                        v = mix[:, i, o:o + w]
                        ins = nc.vector.scalar_tensor_tensor(out=v, in0=v, scalar=r[:, k:k + 1], in1=g1(n),
                                                             op0=ALU.mult, op1=ALU.mult)
                ins.then_inc(s_prep, 1)

            def prep_a(m, i):
                qk = mix[:, i, 0:OA_V]
                n = A_HEADS + A_KV
                link(m, nc.vector.tensor_tensor(ropeU, qk, qk, ALU.mult))
                ms = slot(m)[:, 0:n]
                link(m, nc.vector.tensor_reduce(ms, heads(ropeU, n), AX.X, ALU.add))
                r = power(m, nc.vector.tensor_scalar(ms, ms, 1.0 / A_DIM, EPS, ALU.mult, ALU.add))
                link(m, nc.vector.tensor_tensor(heads(qk, n), heads(qk, n), each(r[:, 0:n], A_DIM), ALU.mult))
                q, k = qk[:, 0:OA_K], qk[:, OA_K:]
                nc.vector.tensor_tensor(heads(q, A_HEADS), heads(q, A_HEADS), over(g1("aq"), A_HEADS), ALU.mult)
                link(m, nc.vector.tensor_tensor(heads(k, A_KV), heads(k, A_KV), over(g1("ak"), A_KV), ALU.mult))
                u, v = rotate(m, heads(qk, n), None, table(i, 0, 64), table(i, 64, 64), 2, ropeU, ropeV)
                order = lambda t: t[:, 0:A_HEADS].rearrange("p (g c) d -> p g c d", g=A_KV)
                nc.vector.tensor_tensor(q.rearrange("p (c g d) -> p g c d", c=4, g=A_KV), order(u), order(v), ALU.add)
                ins = nc.vector.tensor_tensor(heads(k, A_KV), u[:, A_HEADS:], v[:, A_HEADS:], ALU.add)
                if i == NTOK - 1:
                    ins.then_inc(s_prep, 1)
                else:
                    link(m, ins)

            def prep_b(m, i):
                v = heads(mix[:, i, OB_Q:OB_V], 4 * B_HEADS)[:, :, 0:B_ROT]
                u, w = rotate(m, v, None, table(i, 128, 8), table(i, 136, 8), 1, scr[:, 0:256], scr[:, 256:512])
                ins = nc.vector.tensor_tensor(v, u, w, ALU.add)
                if i == NTOK - 1:
                    ins.then_inc(s_prep, 1)
                else:
                    link(m, ins)

            def prep_c(m):
                for i in range(NTOK):
                    cos, sin = table(i, 144, 32), table(i, 176, 32)
                    q = heads(q_c[:, i], C_HEADS)[:, :, C_NOPE:]
                    u, v = rotate(m, q, None, cos, sin, 1, scr[:, 0:256], scr[:, 256:512])
                    link(m, nc.vector.tensor_tensor(q, u, v, ALU.add))
                    k = heads(mix[:, i, OC_KR:MIX_W], 1)
                    u, v = rotate(m, k, None, cos, sin, 1, scr[:, 0:256], scr[:, 256:512])
                    link(m, nc.vector.tensor_tensor(k, u, v, ALU.add))
                    ins = nc.vector.tensor_copy(heads(k_c[:, i], C_HEADS)[:, :, C_NOPE:],
                                                over(mix[:, i, OC_KR:MIX_W], C_HEADS))
                ins.then_inc(s_prep, 1)

            def lambdas(m):
                l = g1("lam")
                for k in range(2):
                    ins = nc.vector.tensor_tensor_reduce(
                        out=scr[:, 0:B_QK], in0=l[:, 2 * k * B_QK:(2 * k + 1) * B_QK],
                        in1=l[:, (2 * k + 1) * B_QK:(2 * k + 2) * B_QK], scale=1.0, scalar=0.0,
                        op0=ALU.mult, op1=ALU.add, accum_out=lam[:, k:k + 1])
                    if k == 0:
                        link(m, ins)
                ins.then_inc(s_lam, 1)
                dve.wait_ge(s_lame, m.turn + 1)
                link(m, nc.vector.scalar_tensor_tensor(
                    out=lam[:, 4:5], in0=lam[:, 2:3], scalar=lam[:, 3:4], in1=g1("linit")[:, 0:1],
                    op0=ALU.subtract, op1=ALU.add))

            def combine(m, h):
                n = 8 + 2 * h
                p0, p1 = n % 4, (n + 1) % 4
                dve.wait_ge(s_pr, m.at("sb", n + 2))
                link(m, nc.vector.reciprocal(rinv[:, n:n + 2], rowsum[:, n:n + 2]))
                link(m, nc.vector.tensor_scalar(rinv[:, n + 1], rinv[:, n + 1], lam[:, 4:5], None, ALU.mult))
                for i in range(NTOK):
                    ins = nc.vector.tensor_scalar(probs[:, p1, i], probs[:, p1, i], rinv[:, n + 1, i:i + 1], None,
                                                  ALU.mult)
                link(m, ins)
                for i in range(NTOK):
                    ins = nc.vector.scalar_tensor_tensor(
                        out=probs[:, p0, i], in0=probs[:, p0, i], scalar=rinv[:, n, i:i + 1], in1=probs[:, p1, i],
                        op0=ALU.mult, op1=ALU.subtract)
                ins.then_inc(s_pw, 1)

            def finish_b(m):
                dve.wait_ge(s_o, m.at("br", 2))
                for i in range(NTOK):
                    y = mix[:, i, OB_Q:OB_Q + YW]
                    link(m, nc.vector.tensor_copy(y, psum[:, SETS["C"][i]]))
                    link(m, nc.vector.tensor_tensor(scr[:], y, y, ALU.mult))
                    ms = slot(m)[:, 0:B_HEADS]
                    link(m, nc.vector.tensor_reduce(ms, heads(scr[:], B_HEADS), AX.X, ALU.add))
                    r = power(m, nc.vector.tensor_scalar(ms, ms, 1.0 / HV, EPS, ALU.mult, ALU.add))
                    link(m, nc.vector.tensor_tensor(heads(y, B_HEADS), heads(y, B_HEADS), each(r[:, 0:B_HEADS], HV),
                                                    ALU.mult))
                    ins = nc.vector.scalar_tensor_tensor(
                        out=heads(y, B_HEADS), in0=heads(y, B_HEADS), scalar=g1("linit")[:, 1:2],
                        in1=over(g1("sub"), B_HEADS), op0=ALU.mult, op1=ALU.mult)
                    if i == 0:
                        link(m, ins)
                ins.then_inc(s_y, 1)

            chain["rise"] = STEP_LAYER1
            with dve.Fori(0, DEPTH) as r:
                m = span1(r)
                chain["n"] = powers[0] = split_turns[0] = 0
                low(m, 0)
                dve.wait_ge(s_gain, 16 * (r + 1))
                norm(m, G1["ln1"][0], xn)
                quarter_low(m, "ln1")
                lambdas(m)
                for g in range(12):
                    ahead(m, 2 * g)
                    ahead(m, 2 * g + 1)
                    if g == 6:
                        dve.wait_ge(s_free["A"], m.at("fA", 6))
                        dve.wait_ge(s_free["B"], m.at("fB", 6))
                        prep_latents(m)
                    elif g == 7:
                        prep_a(m, 0)
                    elif g == 8:
                        prep_a(m, 1)
                    elif g == 9:
                        prep_b(m, 0)
                        prep_b(m, 1)
                for i in range(NTOK):
                    c = slice(i * P, (i + 1) * P)
                    turned_low(m, m.start["cc"] + 2 * i, slice(0, 3), c, 3, P)
                    turned_low(m, m.start["cc"] + 2 * i + 1, slice(3, 5), c, 2, P)
                for j in range(T_UQ, T_BR):
                    ahead(m, j)
                dve.wait_ge(s_free["B"], m.at("fB", 16))
                prep_c(m)
                softmax_heads(m, 0, "pa")
                divide(m, 0, 0, lambda i: mix[:, i, 0:YW])
                for h in range(2):
                    row_max(m, 8 + 2 * h)
                    row_max(m, 9 + 2 * h)
                for h in range(B_HEADS):
                    combine(m, h)
                    if h + 2 < B_HEADS:
                        row_max(m, 12 + 2 * h)
                        row_max(m, 13 + 2 * h)
                finish_b(m)
                softmax_heads(m, 24, "pc")
                divide(m, 24, 2, lambda i: mix[:, i, OB_K:OB_K + YW])
                for n in range(NBR):
                    for i in range(NTOK):
                        turned_low(m, m.start["y"] + 2 * n + i, slice(4 * n, 4 * n + 4),
                                   slice(i * P, (i + 1) * P), 4, P)
                for n in range(NBR):
                    for h in range(2):
                        key, use = "AB"[h], 8 + n
                        ahead(m, T_BR + 2 * n + h)
                        dve.wait_ge(s_used, m.at("used", T_BR + 2 * n + h + 1))
                        for i in range(NTOK):
                            mg = merged[:, i, h * W:(h + 1) * W]
                            gt = gts[:, i, n * D + h * W:n * D + (h + 1) * W]
                            dst = mg if n == 0 else heads(scr[:], 1)[:, 0]
                            nc.vector.tensor_tensor(dst, psum[:, SETS[key][i]], gt, ALU.mult)\
                              .then_inc(s_free[key], 1)
                            if n:
                                dve.wait_ge(s_free[key], m.at("f" + key, NTOK * use + i + 1))
                                ins = nc.vector.tensor_tensor(mg, mg, scr[:], ALU.add)
                                if n < NBR - 1 or i == 0 or h == 0:
                                    link(m, ins)
                                else:
                                    ins.then_inc(s_mrg, 1)
                        if n == 0:
                            dve.wait_ge(s_free[key], m.at("f" + key, NTOK * (use + 1)))
                quarter_low(m, "mrg")
                for h in range(2):
                    ahead(m, T_OUT + 2 * h)
                    ahead(m, T_OUT + 2 * h + 1)
                    accumulate(m, "AB"[h], 11, h, T_OUT + 2 * h + 1)
                norm(m, G1["ln2"][0], xn)
                quarter_low(m, "ln2")
                ffn(m, FF1_STEPS, T_FF, D_FF, 12)
                accumulate(m, "B", 12, 0, len(tiles1) - 2)
                accumulate(m, "C", 0, 1, len(tiles1) - 1)
                assert chain["n"] == STEP_LAYER1, chain
            chain.update(base=DEPTH * STEP_LAYER1, n=0, rise=0)
            powers[0] = split_turns[0] = 0
            dve.wait_ge(s_gain2, 32)
            norm(spanf, 2 * D, x_sb)
            dve.wait_ge(s_xn, spanf.at("xn", NTOK))

            def mixer2(m, gains_in, ffn_gain_in):
                powers[0] = split_turns[0] = 0
                low(m, 0)
                dve.wait_ge(s_gain2, gains_in)
                norm(m, G2["mix"][0], xn)
                quarter_low(m, "mix")
                for g in range(4):
                    ahead(m, 2 * g)
                    ahead(m, 2 * g + 1)
                for n in range(2):
                    turned_low(m, m.start["dt"] + n, slice(8 + 2 * n, 10 + 2 * n), slice(0, S), 2, S)
                ahead(m, T_POOL)
                def masked_max(n):
                    dve.wait_ge(s_sc, m.at("sb", n + 1))
                    link(m, nc.vector.tensor_tensor(probs[:, n % 4], psum[:, n % 4].rearrange(
                        "p (i k) -> p i k", i=NTOK), mask, ALU.add))
                    nc.vector.tensor_reduce(negmax[:, n], probs[:, n % 4], AX.X, ALU.max, negate=True)\
                      .then_inc(s_nm, 1)

                def counted(n):
                    dve.wait_ge(s_pr, m.at("sb", n + 1))
                    for i in range(NTOK):
                        ins = nc.vector.tensor_tensor_reduce(
                            out=probs[:, n % 4, i], in0=probs[:, n % 4, i], in1=count[:, i], scale=1.0, scalar=0.0,
                            op0=ALU.mult, op1=ALU.add, accum_out=rowsum[:, n, i:i + 1])
                    ins.then_inc(s_pw, 1)

                dve.wait_ge(s_big, 16)
                for n in range(3):
                    masked_max(n)
                counted(0)
                for n in range(HEADS):
                    if n + 1 < HEADS:
                        counted(n + 1)
                    turned_probs(m, m.start["p2"] + n, n)
                    if n + 3 < HEADS:
                        masked_max(n + 3)
                divide(m, 0, 0, lambda i: o_2[:, i])
                dve.wait_ge(s_y, YS + 1 if m is span2 else YS + 2)
                for i in range(NTOK):
                    rms(m, z_2[:, i], gains[:, G2["pool"][0]:G2["pool"][1]], z_2[:, i], scr[:], W)
                    ins = rms(m, o_2[:, i], gains[:, G2["attn"][0]:G2["attn"][1]], o_2[:, i], scr[:], W)
                ins.then_inc(s_mrg, 1)
                quarter_low(m, "y2")
                for h in range(2):
                    ahead(m, T_OUT2 + 2 * h)
                    ahead(m, T_OUT2 + 2 * h + 1)
                    accumulate(m, "BA"[h], 2 + h, h, T_OUT2 + 2 * h + 1)
                dve.wait_ge(s_gain2, ffn_gain_in)
                norm(m, G2["ffn"][0], xn)
                quarter_low(m, "ffn")

            YS = DEPTH * NBR
            mixer2(span2, 32, 48)
            ffn(span2, FF2_STEPS, T_FF2, D_FF2, 4)
            accumulate(span2, "B", 3, 0, len(tiles2) - 2)
            accumulate(span2, "C", 0, 1, len(tiles2) - 1)
            mixer2(span3, 64, 64)

            m = span3
            b = m.bank(m.start["rt"])
            dve.wait_ge(s_tp, m.at("tp", m.start["rt"] + 1))
            logits = route[:, 0:16].rearrange("p (i e) -> p i e", i=NTOK)
            ins = nc.vector.tensor_copy(logits, psum[:, TB[b], 0:16].rearrange("p (i e) -> p i e", i=NTOK))
            ins.then_inc(s_tf[b], 1)
            dve.wait_ge(s_tf[b], m.turned(m.start["rt"]))
            best, place = (route[:, 32 + 16 * k:48 + 16 * k].rearrange("p (i e) -> p i e", i=NTOK) for k in range(2))
            for i in range(NTOK):
                link(m, nc.vector.max(best[:, i], logits[:, i]))
                link(m, nc.vector.max_index(route_i[:], best[:, i], logits[:, i]))
                link(m, nc.vector.tensor_copy(place[:, i], route_i[:]))
                ins = nc.vector.tensor_tensor(route[:, 16 + i:17 + i], best[:, i, 1:2], best[:, i, 0:1], ALU.subtract)
                if i == 0:
                    link(m, ins)
            ins.then_inc(s_rt, 1)
            dve.wait_ge(s_rte, 1)
            e_, w1, w2, tmp = (route[:, k:k + w] for k, w in ((24, 2), (64, 2), (66, 2), (72, 16)))
            link(m, nc.vector.tensor_scalar(w1, e_, 1.0, None, ALU.add))
            link(m, nc.vector.reciprocal(w1, w1))
            link(m, nc.vector.tensor_tensor(w2, e_, w1, ALU.mult))
            names = iota[:, 0:NEXP]
            for i in range(NTOK):
                nc.vector.tensor_scalar(tmp[:, 0:8], names, place[:, i, 0:1], w1[:, i:i + 1], ALU.is_equal, ALU.mult)
                link(m, nc.vector.tensor_scalar(tmp[:, 8:16], names, place[:, i, 1:2], w2[:, i:i + 1],
                                                ALU.is_equal, ALU.mult))
                link(m, nc.vector.tensor_tensor(gate_e[:, :, i], tmp[:, 0:8], tmp[:, 8:16], ALU.add))
                nc.vector.tensor_scalar(tmp[:, 0:8], names, place[:, i, 0:1], None, ALU.is_equal)
                link(m, nc.vector.tensor_scalar(tmp[:, 8:16], names, place[:, i, 1:2], None, ALU.is_equal))
                ins = nc.vector.tensor_tensor(member[:, i], tmp[:, 0:8], tmp[:, 8:16], ALU.add)
                if i == 0:
                    link(m, ins)
            ins.then_inc(s_member, 1)
            b = m.bank(m.start["place"])
            dve.wait_ge(s_tp, m.at("tp", m.start["place"] + 1))
            before = route[:, 0:24]
            nc.vector.tensor_copy(before, psum[:, TB[b], 0:24]).then_inc(s_tf[b], 1)
            dve.wait_ge(s_tf[b], m.turned(m.start["place"]))
            own, prior = route[:, 24:32], route[:, 80:88]
            nc.vector.tensor_scalar(own, before[:, 16:24], float(P), 1.0, ALU.is_gt, ALU.add)
            link(m, nc.vector.memset(prior, 0.0))
            for n in range(1, NEXP):
                link(m, nc.vector.tensor_tensor(prior[:, n:n + 1], prior[:, n - 1:n], own[:, n - 1:n], ALU.add))
            nc.vector.tensor_copy(rounds_i[:, 0], own)
            nc.vector.tensor_copy(rounds_i[:, 1], prior).then_inc(s_rounds, 1)
            for i in range(NTOK):
                link(m, nc.vector.scalar_tensor_tensor(out=tmp[:, 0:8], in0=before[:, 8 * i:8 * i + 8], scalar=1.0,
                                                       in1=member[:, i], op0=ALU.add, op1=ALU.mult))
                link(m, nc.vector.tensor_scalar(place_e[:, :, i], tmp[:, 0:8], P - 1.0, None, ALU.add))

            def expert(m, e):
                chain["n"] = split_turns[0] = 0
                column = lambda v: v[:, bass.ds(e, 1), :].rearrange("p a i -> p (a i)")
                nc.vector.tensor_copy(gate_c[:], column(gate_e))
                link(m, nc.vector.tensor_copy(place_c[:], column(place_e)))
                link(m, nc.vector.tensor_scalar(place_c[:], place_c[:], -float(P), None, ALU.add))
                for i in range(NTOK):
                    ins = nc.vector.tensor_scalar(sel[:, i], iota, place_c[:, i:i + 1], None, ALU.is_equal)
                ins.then_inc(s_sel, 1)
                for i in range(NTOK):
                    ins = nc.vector.tensor_scalar(sel_w[:, i], iota, place_c[:, i:i + 1], gate_c[:, i:i + 1],
                                                  ALU.is_equal, ALU.mult)
                ins.then_inc(s_sel, 1)
                link(m, nc.vector.tensor_copy(column(place_e), place_c[:]))
                low(m, 0)
                for n in range(2):
                    turned_low(m, m.start["take"] + n, slice(4 * n, 4 * n + 4), slice(0, P), 4, P)
                j, turn = 0, m.start["ff"]
                for kind, g, k in FFE_STEPS:
                    if kind in TILE_STEPS:
                        ahead(m, j)
                        j += 1
                    elif kind == "act_up":
                        dve.wait_ge(s_used, m.at("used", j))
                        nc.vector.tensor_tensor(ff_a[:, 0], psum[:, 1], ff_s[:, 0], ALU.mult)\
                          .then_inc(s_free["B"], 1)
                    elif kind == "turn":
                        c = 8 + 4 * (g % 2)
                        turned_low(m, turn, slice(c, c + 4), slice(0, P), 4, P)
                        turn += 1
                for half in range(2):
                    dve.wait_ge(s_back, m.turn * 2 + (half + 1))
                    for i in range(NTOK):
                        xs = x_sb[:, i, half * W:(half + 1) * W]
                        nc.vector.tensor_tensor(xs, psum[:, SETS["C"][i]], xs, ALU.add).then_inc(s_given, 1)
                dve.wait_ge(s_given, m.at("fG", 4))
                assert chain["n"] == STEP_EXPERT, chain

            chain.update(base=chain["base"] + chain["n"], rise=STEP_EXPERT)
            rounds(dve, expert)
            powers[0] = 0
            dve.wait_ge(s_gain2, 80)
            norm(spang, 0, xn)

        @block.tensor
        def _(pe):
            for key in "ABC":
                pe.sem_inc(s_free[key], NTOK)
            for b in range(2):
                pe.sem_inc(s_tf[b], 1)
            pe.sem_inc(s_given, 1)
            pe.wait_ge(s_in, 32)

            def turn(m, k, blocks):
                b = m.bank(k)
                pe.wait_ge(s_tf[b], m.empty(k))
                for n, src in enumerate(blocks):
                    c = src.shape[-1]
                    ins = nc.tensor.transpose(psum[0:c, TB[b], n * P:(n + 1) * P], src, ident)
                ins.then_inc(s_tp, 1)

            def turned(m, k0, n):
                for k in range(max(k0, k0 + n - 2), k0 + n):
                    pe.wait_ge(s_tf[m.bank(k)], m.turned(k))

            def parts(v, n, w=P):
                return [v[:, k * w:(k + 1) * w] for k in range(n)]

            def free(m, key, use):
                pe.wait_ge(s_free[key], m.at("f" + key, NTOK * use))

            def group(m, j, ntiles, key, use, chunk=0, per=4):
                free(m, key, use)
                for k in range(ntiles):
                    product(m, j + k, key, chunk + per * k, k == 0, k == ntiles - 1)

            def product(m, j, key, chunk, first, last):
                t, (_, n, w) = m.tile(j) % SPLIT, m.tiles[j]
                for half, c0, c1, count in halves(n):
                    pe.wait_ge(s_lo, m.at("lo", j, half + count))
                    for i in range(NTOK):
                        o = psum[:, SETS[key][i], 0:w]
                        for c in range(c0, c1):
                            hh, hl = (hT[:, k, chunk + c, i * P:(i + 1) * P] for k in range(2))
                            wh, wl = (t_[:, t, half, (c - c0) * w:(c - c0 + 1) * w] for t_ in (whi, wlo))
                            nc.tensor.matmul(o, hh, wh, start=first and c == 0, stop=False)
                            nc.tensor.matmul(o, hh, wl, start=False, stop=False)
                            ins = nc.tensor.matmul(o, hl, wh, start=False, stop=last and c == n - 1)
                    ins.then_inc(s_used, count)

            def norm_turns(m, stage):
                for i in range(NTOK):
                    pe.wait_ge(s_xn, m.at("xn", {"ln1": 0, "mix": 0}.get(stage, NTOK) + i + 1))
                    for c in range(2):
                        turn(m, m.start[stage] + 2 * i + c, parts(xn[:, i, c * W:(c + 1) * W], 4))
                turned(m, m.start[stage], 4)

            def scores(m, n, q, k):
                if n >= 4:
                    pe.wait_ge(s_pr, m.at("sb", n - 3))
                for i in range(NTOK):
                    ins = nc.tensor.matmul(psum[:, n % 4, i * S:(i + 1) * S], q[:, i * P:(i + 1) * P], k,
                                           start=True, stop=True)
                ins.then_inc(s_sc, 1)

            def probs_turn(m, k, n):
                turn(m, k, [probs[:, n % 4, i, kb * P:(kb + 1) * P] for kb in range(2) for i in range(NTOK)])

            def values(m, k, h, v, done):
                pe.wait_ge(s_tf[m.bank(k)], m.turned(k))
                for i in range(NTOK):
                    for kb in range(2):
                        ins = nc.tensor.matmul(psum[:, SETS["C"][i], h * HV:(h + 1) * HV],
                                               probsT[:, h % 2, kb, i * P:(i + 1) * P], v(kb),
                                               start=kb == 0, stop=kb == 1)
                if done:
                    ins.then_inc(s_o, 1)

            def attend(m, n0, stage, q, k, v, per, ready):
                lead = 3 if per == 1 else 2
                for h in range(lead):
                    for b in range(per):
                        scores(m, n0 + per * h + b, q(h, b), k(h, b))
                for h in range(HEADS):
                    pe.wait_ge(*ready(h))
                    probs_turn(m, m.start[stage] + h, n0 + per * h)
                    if h + lead < HEADS:
                        for b in range(per):
                            scores(m, n0 + per * (h + lead) + b, q(h + lead, b), k(h + lead, b))
                    if h:
                        values(m, m.start[stage] + h - 1, h - 1, v(h - 1), False)
                values(m, m.start[stage] + HEADS - 1, HEADS - 1, v(HEADS - 1), True)

            def ffn(m, steps, j, hidden, a0, b0, c0):
                use, turns = a0, m.start["ff"]
                last = -(-hidden // W) - 1
                for kind, g, k in steps:
                    w = min(W, hidden - g * W)
                    if kind in ("gate", "up"):
                        if k == 0:
                            free(m, "A", use)
                        product(m, j, "A", 4 * k, k == 0, k == 1)
                        j += 1
                    elif kind in ("act_gate", "act_up"):
                        use += 1
                    elif kind == "turn":
                        pe.wait_ge(s_free["A"], m.at("fA", NTOK * use))
                        for i in range(NTOK):
                            turn(m, turns, parts(ff_a[:, i], w // P))
                            turns += 1
                    elif kind == "down":
                        key = "BC"[k]
                        if g == 0:
                            free(m, key, (b0, c0)[k])
                        if k == 0:
                            turned(m, turns - 2, 2)
                        product(m, j, key, 8 + 4 * (g % 2), g == 0, g == last)
                        j += 1

            with pe.Fori(0, DEPTH) as r:
                m = span1(r)
                norm_turns(m, "ln1")
                for g in range(12):
                    group(m, 2 * g, 2, "AB"[g % 2], g // 2)
                pe.wait_ge(s_prep, m.at("prep", 1))
                for i in range(NTOK):
                    turn(m, m.start["cc"] + 2 * i, parts(mix[:, i, OC_Q:], 3))
                    turn(m, m.start["cc"] + 2 * i + 1, parts(mix[:, i, OC_KV:], 2))
                turned(m, m.start["cc"], 4)
                for g in range(2):
                    group(m, T_UQ + g, 1, "AB"[g], 6)
                for g in range(2):
                    group(m, T_UKV + 2 * g, 2, "AB"[g], 7, chunk=3, per=1)
                pe.wait_ge(s_prep, m.at("prep", 2))
                for i in range(NTOK):
                    turn(m, m.start["qa"] + i, parts(mix[:, i, 0:], 4))
                for i in range(NTOK):
                    turn(m, m.start["ka"] + i, parts(mix[:, i, OA_K:], 1))
                pe.wait_ge(s_prep, m.at("prep", 3))
                for i in range(NTOK):
                    turn(m, m.start["qb"] + i, parts(mix[:, i, OB_Q:], 4))
                for i in range(NTOK):
                    turn(m, m.start["kb"] + i, parts(mix[:, i, OB_K:], 4))
                for key, use in (("A", 8), ("B", 8), ("C", 0)):
                    free(m, key, use)
                turned(m, m.start["qa"], 8)
                hp = lambda h: slice(64 * (h // 4), 64 * (h // 4) + 64)
                attend(m, 0, "pa", lambda h, b: qT_a[hp(h), h % 4], lambda h, b: kT_a[hp(h), 0],
                       lambda h: lambda kb: mix[:, kb, OA_V + HV * (h // 4):OA_V + HV * (h // 4) + HV],
                       1, lambda h: (s_pr, m.at("sb", h + 1)))
                pe.wait_ge(s_y, m.at("br", 1))
                cp = lambda h, b: slice(32 * ((2 * h + b) % 4), 32 * ((2 * h + b) % 4) + 32)
                attend(m, 8, "pb", lambda h, b: qT_b[cp(h, b), h // 2], lambda h, b: kT_b[cp(h, b), h // 2],
                       lambda h: lambda kb: mix[:, kb, OB_V + HV * h:OB_V + HV * (h + 1)],
                       2, lambda h: (s_pw, m.turn * B_HEADS + (h + 1)))
                pe.wait_ge(s_prep, m.at("prep", 4))
                for stage, v in (("qc", q_c), ("kc", k_c)):
                    for n in range(4):
                        i, c = n // 2, n % 2
                        turn(m, m.start[stage] + n, parts(v[:, i, 4 * c * C_DIM:], 4, C_DIM))
                turned(m, m.start["kc"], 4)
                pe.wait_ge(s_y, m.at("br", 2))
                attend(m, 24, "pc", lambda h, b: qT_c[0:C_DIM, h], lambda h, b: kT_c[0:C_DIM, h],
                       lambda h: lambda kb: v_c[:, kb, HV * h:HV * (h + 1)],
                       1, lambda h: (s_pr, m.at("sb", 24 + h + 1)))
                pe.wait_ge(s_y, m.at("br", 3))
                for n, o in enumerate((0, OB_Q, OB_K)):
                    for i in range(NTOK):
                        turn(m, m.start["y"] + 2 * n + i, parts(mix[:, i, o:], 4))
                turned(m, m.start["y"], 6)
                for n in range(NBR):
                    for h in range(2):
                        group(m, T_BR + 2 * n + h, 1, "AB"[h], 8 + n, chunk=4 * n)
                pe.wait_ge(s_mrg, m.turn + 1)
                for i in range(NTOK):
                    for c in range(2):
                        turn(m, m.start["mrg"] + 2 * i + c, parts(merged[:, i, c * W:], 4))
                turned(m, m.start["mrg"], 4)
                for h in range(2):
                    group(m, T_OUT + 2 * h, 2, "AB"[h], 11)
                norm_turns(m, "ln2")
                ffn(m, FF1_STEPS, T_FF, D_FF, 12, 12, 0)

            def mixer2(m, n):
                norm_turns(m, "mix")
                for g in range(4):
                    group(m, 2 * g, 2, "AB"[g % 2], g // 2)
                free(m, "A", 2)
                free(m, "B", 2)
                pe.wait_ge(s_big, 16)
                for t in range(2):
                    b = m.bank(m.start["dt"] + t)
                    pe.wait_ge(s_tf[b], m.empty(m.start["dt"] + t))
                    for g in range(2):
                        for i in range(NTOK):
                            c = (2 * t + g) * P
                            ins = nc.tensor.matmul(psum[:, TB[b], g * S:(g + 1) * S], mix2[:, i, c:c + P],
                                                   poolT[:, i, 2 * t + g], start=i == 0, stop=i == 1)
                    ins.then_inc(s_tp, 1)
                turned(m, m.start["dt"], 2)
                pe.wait_ge(s_lo, m.at("lo", T_POOL + 1))
                w_buf = m.tile(T_POOL) % SPLIT
                for i in range(NTOK):
                    for g in range(4):
                        o = psum[:, SETS["A"][i], g * P:(g + 1) * P]
                        hh, hl = (hT[:, k, 8 + g, i * P:(i + 1) * P] for k in range(2))
                        wh, wl = (t_[:, w_buf, g // 2, g % 2 * P:(g % 2 + 1) * P] for t_ in (whi, wlo))
                        nc.tensor.matmul(o, hh, wh, start=True, stop=False)
                        nc.tensor.matmul(o, hh, wl, start=False, stop=False)
                        ins = nc.tensor.matmul(o, hl, wh, start=False, stop=True)
                ins.then_inc(s_used, 2)
                for stage, o in (("q2", W), ("k2", 2 * W)):
                    for i in range(NTOK):
                        turn(m, m.start[stage] + i, parts(mix2[:, i, o:], 4))
                turned(m, m.start["q2"], 4)
                for key, use in (("A", 3), ("B", 2), ("C", 0)):
                    free(m, key, use)
                hp = lambda h: slice(64 * (h % 2), 64 * (h % 2) + 64)
                attend(m, 0, "p2", lambda h, b: qT_2[hp(h), h // 2], lambda h, b: kT_2[hp(h), h // 2],
                       lambda h: lambda kb: mix2[:, kb, 3 * W + HV * h:3 * W + HV * (h + 1)],
                       1, lambda h: (s_pw, DEPTH * B_HEADS + n * HEADS + h + 1))
                pe.wait_ge(s_mrg, DEPTH + n + 1)
                for i in range(NTOK):
                    turn(m, m.start["y2"] + 2 * i, parts(z_2[:, i], 4))
                    turn(m, m.start["y2"] + 2 * i + 1, parts(o_2[:, i], 4))
                turned(m, m.start["y2"], 4)
                for h in range(2):
                    group(m, T_OUT2 + 2 * h, 2, "BA"[h], 2 + h)
                norm_turns(m, "ffn")

            mixer2(span2, 0)
            ffn(span2, FF2_STEPS, T_FF2, D_FF2, 4, 3, 0)
            mixer2(span3, 1)
            m = span3
            b = m.bank(m.start["rt"])
            pe.wait_ge(s_wr, 16)
            pe.wait_ge(s_tf[b], m.empty(m.start["rt"]))
            for i in range(NTOK):
                for c in range(KD):
                    for k in range(2):
                        ins = nc.tensor.matmul(psum[:, TB[b], i * NEXP:(i + 1) * NEXP],
                                               hT[:, k, c, i * P:(i + 1) * P].bitcast(F32), w_route[:, c],
                                               start=c == 0 and k == 0, stop=c == KD - 1 and k == 1)
            ins.then_inc(s_tp, 1)
            b = m.bank(m.start["place"])
            pe.wait_ge(s_member, 1)
            pe.wait_ge(s_tf[b], m.empty(m.start["place"]))
            for n, terms in enumerate((((earlier, 0),), ((ones, 0), (earlier, 1)), ((ones, 0), (ones, 1)))):
                for k, (before, i) in enumerate(terms):
                    ins = nc.tensor.matmul(psum[:, TB[b], n * NEXP:(n + 1) * NEXP], before, member[:, i],
                                           start=k == 0, stop=k == len(terms) - 1)
            ins.then_inc(s_tp, 1)

            def slots(m, j, bank, chunk, first, last):
                t, (_, n, w) = m.tile(j) % SPLIT, m.tiles[j]
                for half, c0, c1, count in halves(n):
                    pe.wait_ge(s_lo, m.at("lo", j, half + count))
                    for c in range(c0, c1):
                        hh, hl = (hT[:, k, chunk + c, 0:P] for k in range(2))
                        wh, wl = (t_[:, t, half, (c - c0) * w:(c - c0 + 1) * w] for t_ in (whi, wlo))
                        nc.tensor.matmul(psum[:, bank], hh, wh, start=first and c == 0, stop=False)
                        nc.tensor.matmul(psum[:, bank], hh, wl, start=False, stop=False)
                        ins = nc.tensor.matmul(psum[:, bank], hl, wh, start=False, stop=last and c == n - 1)
                    ins.then_inc(s_used, count)

            def expert(m, e):
                pe.wait_ge(s_sel, m.turn * 2 + 1)
                for n in range(2):
                    b = m.bank(m.start["take"] + n)
                    pe.wait_ge(s_tf[b], m.empty(m.start["take"] + n))
                    for c in range(4):
                        f = (4 * n + c) * P
                        for i in range(NTOK):
                            ins = nc.tensor.matmul(psum[:, TB[b], c * P:(c + 1) * P], xn[:, i, f:f + P], sel[:, i],
                                                   start=i == 0, stop=i == NTOK - 1)
                    ins.then_inc(s_tp, 1)
                pe.wait_ge(s_sel, m.turn * 2 + 2)
                turn(m, m.start["give"], [sel_w[:, i] for i in range(NTOK)])
                turned(m, m.start["take"], 2)
                j, turns, last = 0, m.start["ff"], D_FFE // W - 1
                for kind, g, k in FFE_STEPS:
                    if kind in ("gate", "up"):
                        if k == 0:
                            key = "AB"[kind == "up"]
                            pe.wait_ge(s_free[key], m.at("f" + key, g))
                        slots(m, j, int(kind == "up"), 4 * k, k == 0, k == 1)
                        j += 1
                    elif kind == "turn":
                        pe.wait_ge(s_free["B"], m.at("fB", g + 1))
                        turn(m, turns, parts(ff_a[:, 0], 4))
                        turns += 1
                    elif kind == "down":
                        if g == 0 and k == 0:
                            pe.wait_ge(s_free["C"], m.at("fC", 0))
                        if k == 0:
                            pe.wait_ge(s_tf[m.bank(turns - 1)], m.turned(turns - 1))
                        slots(m, j, 2 + k, 8 + 4 * (g % 2), g == 0, g == last)
                        j += 1
                pe.wait_ge(s_tf[m.bank(m.start["give"])], m.turned(m.start["give"]))
                for half in range(2):
                    pe.wait_ge(s_free["C"], m.at("fC", half + 1))
                    pe.wait_ge(s_given, m.at("fG", 2 * half))
                    for i in range(NTOK):
                        ins = nc.tensor.matmul(psum[:, SETS["C"][i]], give[:, i], y_e[:, half * W:(half + 1) * W],
                                               start=True, stop=True)
                    ins.then_inc(s_back, 1)

            rounds(pe, expert)


DIRECT = ["x", "w_in", "c_w_uq", "c_w_ukv", "w_branch", "w_out", "w_ff1", "w_ff2", "final_g", "w_in_2", "w_pool_2",
          "w_out_2", "ffn_wg_2", "ffn_wu_2", "ffn_wd_2", "w_router_2", "moe_wg_2", "moe_wu_2", "moe_wd_2",
          "final_norm_2"]


def kernel(**inputs):
    import concourse.bacc as bacc
    from concourse.bass_utils import run_bass_kernel_spmd

    nc = bacc.Bacc("TRN2", target_bir_lowering=False, num_devices=1)
    arrays = {n: np.ascontiguousarray(inputs[n]) for n in DIRECT}
    init = [0.8 - 0.6 * math.exp(-0.3 * l) for l in range(DEPTH)]
    rows = [inputs[n].reshape(DEPTH, -1) for n in ("ln1_g", "ln2_g", "a_q_norm", "a_k_norm", "b_subln", "c_q_norm",
                                                   "c_kv_norm", "b_lambda")]
    rows.append(np.array([[v, 1.0 - v] for v in init], np.float32))
    arrays["gains1"] = np.ascontiguousarray(np.concatenate(rows, 1))
    arrays["gains2"] = np.ascontiguousarray(np.concatenate(
        [inputs[n] for n in ("norm_mix_2", "pool_scale_2", "attn_gain_2", "norm_ffn_2")], 1))
    arrays["tables"], arrays["big"] = make_tables()
    args = {n: nc.dram_tensor(f"in_{n}", v.shape, mybir.dt.from_np(v.dtype), kind="ExternalInput").ap()
            for n, v in arrays.items()}
    out = nc.dram_tensor("out_0", (1, S, D), F32, kind="ExternalOutput").ap()
    build(nc, args, out)
    r = run_bass_kernel_spmd(nc, [{f"in_{n}": v for n, v in arrays.items()}], core_ids=[0])
    return r.results[0]["out_0"]
```

```python
import math
from contextlib import ExitStack

import concourse.bass as bass
import numpy as np
from concourse import mybir

F32 = mybir.dt.float32
F32R = mybir.dt.float32r
U32 = mybir.dt.uint32
ALU = mybir.AluOpType
ACT = mybir.ActivationFunctionType
AX = mybir.AxisListType

D, S, DEPTH, GRID_W, EPS = 1024, 256, 2, 64, 1e-6
P = 128
NTOK = S // P
KD = D // P
A_HEADS, A_KV, A_DIM = 8, 2, 64
B_HEADS, B_QK, B_ROT = 8, 32, 8
C_HEADS, C_QRANK, C_KVRANK, C_NOPE, C_ROPE, C_V = 8, 384, 256, 64, 32, 64
C_DIM = C_NOPE + C_ROPE
HV = 64
HEADS = 8
YW = HEADS * HV
NBR = 3
D_FF, D_FF2, D_FFE, NEXP = 4096, 2816, 3584, 8
POOL_WINDOWS = (2, 4, 8, 16)
PATTERNS = ((128, 1), (512, 4), (2048, 16))
W = 512

OA_Q, OA_K, OA_V = 0, 512, 640
OB_Q, OB_K, OB_V = 768, 1280, 1792
OC_Q, OC_KV, OC_KR = 2304, 2688, 2944
MIX_W = 2976
GATE_W = NBR * D

G1 = {}
_at = 0
for _n, _w in (("ln1", D), ("ln2", D), ("aq", A_DIM), ("ak", A_DIM), ("sub", HV), ("cq", C_QRANK),
               ("ckv", C_KVRANK), ("lam", 4 * B_QK), ("linit", 2)):
    G1[_n] = (_at, _at + _w)
    _at += _w
G1_W = _at
G2 = {"mix": (0, D), "pool": (D, D + 512), "attn": (D + 512, 2 * D), "ffn": (2 * D, 3 * D)}
G2_W = 3 * D

ROPE_W = 2 * (64 + B_ROT + C_ROPE)
TAB_W = P + NTOK * ROPE_W + P
BIG_W = 2 * NTOK * S + NTOK * len(POOL_WINDOWS) * S + 2 * P


def rope_rows(pos, dim, theta):
    inv = np.float32(theta) ** (-np.arange(0, dim, 2, dtype=np.float32) / np.float32(dim))
    ang = pos.astype(np.float32)[:, None] * inv[None, :].astype(np.float32)
    c, s = np.cos(ang), np.sin(ang)
    return np.concatenate([c, c], 1), np.concatenate([-s, s], 1)


def make_tables():
    t = np.arange(S)
    row, col = rope_rows(t // GRID_W, 32, 10000.0), rope_rows(t % GRID_W, 32, 10000.0)
    b, c = rope_rows(t, B_ROT, 500000.0), rope_rows(t, C_ROPE, 10000.0)
    rope = np.concatenate([row[0], col[0], row[1], col[1], b[0], b[1], c[0], c[1]], 1)
    rope = rope.reshape(NTOK, P, ROPE_W).transpose(1, 0, 2).reshape(P, -1)
    iota = np.tile(np.arange(P), (P, 1))
    small = np.concatenate([np.eye(P), rope, iota], 1).astype(np.float32)
    d = t[:, None] - t[None, :]
    count = sum(((d >= 0) & (d % dil == 0) & (d <= win)).astype(np.float32) for win, dil in PATTERNS)
    mask = np.where(count > 0, 0.0, -1e30)
    pool = []
    for w in POOL_WINDOWS:
        n = np.minimum(t + 1, w).astype(np.float32)
        pool.append((((d >= 0) & (d < w)) / n[:, None] - np.eye(S)).T)
    pool = np.stack(pool, 1)
    tiles = lambda a: a.reshape(NTOK, P, -1).transpose(1, 0, 2).reshape(P, -1)
    earlier = np.triu(np.ones((P, P)), 1)
    big = np.concatenate([tiles(count), tiles(mask), tiles(pool), earlier, np.ones((P, P))], 1).astype(np.float32)
    return small, big


def columns(w, rows, c0, width, k0=0, per=4):
    for k in range(0, rows, per * P):
        n = min(per * P, rows - k) // P
        yield (lambda r, k=k, n=n: w(r, k0 + k, n * P, c0, width).rearrange("(c p) n -> p c n", p=P), n, width)


def at_layer(w, rows):
    flat = w.rearrange("l r n -> (l r) n")

    def get(layer, k, n, c0, width):
        if isinstance(layer, int):
            return flat[layer * rows + k:layer * rows + k + n, c0:c0 + width]
        return flat[bass.ds(layer * rows + k, n), c0:c0 + width]
    return get


def ffn_steps(groups, gated):
    up = ("gate", "up") if gated else ("up",)
    for g in range(groups + 1):
        for n, kind in enumerate(up):
            if g < groups:
                yield kind, g, 0
                if n == 0 and g:
                    yield "turn", g - 1, 0
                yield kind, g, 1
                yield "act_" + kind, g, 0
            elif n == 0:
                yield "turn", g - 1, 0
            if g:
                if gated:
                    yield "down", g - 1, n
                else:
                    yield "down", g - 1, 0
                    yield "down", g - 1, 1


FF1_STEPS = list(ffn_steps(D_FF // W, False))
FF2_STEPS = list(ffn_steps(-(-D_FF2 // W), True))
FFE_STEPS = list(ffn_steps(D_FFE // W, True))
TILE_STEPS = ("gate", "up", "down")


def ffn_tiles(steps, gate, up, down, hidden):
    for kind, g, k in steps:
        w = min(W, hidden - g * W)
        if kind in ("gate", "up"):
            yield from columns(gate if kind == "gate" else up, D // 2, g * W, w, k0=k * D // 2)
        elif kind == "down":
            yield from columns(down, w, k * W, W, k0=g * W)


def halves(n):
    if n == 1:
        return [(0, 0, 1, 2)]
    return [(0, 0, -(-n // 2), 1), (1, -(-n // 2), n, 1)]


RAW, RAW_E, SPLIT = 3, 6, 2
HALVED = ("lo", "hi", "used")
CREDIT = {"lo": RAW, "used": SPLIT, "fA": NTOK, "fB": NTOK, "fC": NTOK, "xn": 1, "fG": 1}

TURNS1 = [("ln1", 4), ("cc", 4), ("qa", 2), ("ka", 2), ("qb", 2), ("kb", 2), ("pa", 8), ("pb", 8),
          ("qc", 4), ("kc", 4), ("pc", 8), ("y", 6), ("mrg", 4), ("ln2", 4), ("ff", 16)]
TURNS2 = [("mix", 4), ("dt", 2), ("q2", 2), ("k2", 2), ("p2", 8), ("y2", 4), ("ffn", 4), ("ff", 12)]
TURNS3 = TURNS2[:-1] + [("rt", 1), ("place", 1)]
TURNSE = [("take", 2), ("give", 1), ("ff", 7)]


def starts(turns):
    out, at = {}, 0
    for name, n in turns:
        out[name] = at
        at += n
    return out, at


STEP_LAYER1 = 66
STEP_EXPERT = 3
PLAIN = ("qa", "ka", "qb", "kb", "pa", "pb", "qc", "kc", "pc", "q2", "k2", "p2", "rt", "place",
         "give")

def rises(tiles, turns, a, b, c, normed, powers, banks, branches, preps=0, relu=0, scales=0):
    return dict(fG=0, lo=tiles, used=tiles, hi=tiles, tp=starts(turns)[1],
                th=sum(n for name, n in turns if name not in PLAIN), fA=NTOK * a, fB=NTOK * b, fC=NTOK * c,
                xn=normed, pw=powers, rs=scales, sb=banks, br=branches, prep=preps, relu=relu)


R1 = rises(72, TURNS1, 20, 13, 1, 8, 6, 32, 3, 4, 16, 2)
RF = rises(0, [], 0, 0, 0, 0, 1, 0, 0)
R2 = rises(49, TURNS2, 16, 4, 1, 8, 4, 8, 1, scales=2)
R3 = rises(13, TURNS3, 4, 3, 0, 6, 4, 8, 1, scales=1)
RE = rises(42, TURNSE, 0, 0, 1, 0, 0, 0, 0)
RE.update(fA=7, fB=7, fG=4)


class Span:

    def __init__(self, turns, rise, base, turn=0, tiles=(), ring=RAW, first=0):
        self.start, self.turn, self.rise, self.base = starts(turns)[0], turn, rise, base
        self.tiles, self.ring, self.first = tiles, ring, first

    def value(self, fixed, rise):
        return self.turn * rise + fixed if rise else fixed

    def at(self, name, k, part=0):
        n = 2 if name in HALVED else 1
        return self.value(n * (self.base[name] + CREDIT.get(name, 0) + k) + part, n * self.rise[name])

    def bank(self, k):
        return (self.base["tp"] + k) % 2

    def empty(self, k):
        return self.value((self.base["tp"] + k) // 2 + 1, self.rise["tp"] // 2)

    def turned(self, k):
        return self.value((self.base["tp"] + k) // 2 + 2, self.rise["tp"] // 2)

    def landed(self, j):
        return self.value(16 * ((self.tile(j) - self.first) // self.ring + 1), 16 * (self.rise["lo"] // self.ring))

    def buffer(self, j):
        return (self.tile(j) - self.first) % self.ring

    def tile(self, j):
        return self.base["lo"] + j


def after(base, rise, rounds=1):
    return {k: base[k] + rise[k] * rounds for k in rise}


BASE1 = {k: 0 for k in R1}
BASEF = after(BASE1, R1, DEPTH)
BASE2 = after(BASEF, RF)
BASE3 = after(BASE2, R2)
BASEE = after(BASE3, R3)


def build(nc, a, out):
    ctx = ExitStack()
    with ctx:
        def sb(name, shape, dt=F32):
            return ctx.enter_context(nc.sbuf_tensor(name, shape, dt))

        def sem(name):
            return ctx.enter_context(nc.semaphore(name))

        x_sb = sb("x_res", [P, NTOK, D])
        hT = sb("hT", [P, 2, 16, S], F32R)
        work = sb("work", [P, 20288])
        raw = sb("raw", [P, RAW, 4 * W])
        whi = sb("w_high", [P, SPLIT, 2, 2 * W], F32R)
        wlo = sb("w_low", [P, SPLIT, 2, 2 * W], F32R)
        gains = sb("gains", [P, G2_W])
        tab = sb("tables", [P, TAB_W])
        probs = sb("probs", [P, 4, NTOK, S])
        probsT = sb("probsT", [P, 2, NTOK, S])
        scr = sb("scratch", [P, W])
        negmax = sb("negmax", [P, 32, NTOK])
        rowsum = sb("rowsum", [P, 32, NTOK])
        rinv = sb("rinv", [P, 32, NTOK])
        meansq = sb("meansq", [P, 2, 16])
        rstd = sb("rstd", [P, 2, 16])
        neghalf = sb("neghalf", [P, 16])
        row_scale = sb("row_scale", [P, 2, NTOK])
        lam = sb("lam", [P, 8])
        route = sb("route", [P, 96])
        route_i = sb("route_i", [P, 8], U32)
        gate_e = sb("gate_e", [P, NEXP, NTOK])
        gate_c = sb("gate_c", [P, NTOK])
        member = sb("member", [P, NTOK, NEXP])
        place_e = sb("place_e", [P, NEXP, NTOK])
        place_c = sb("place_c", [P, NTOK])
        rounds_i = sb("rounds_i", [P, 2, NEXP + 1], mybir.dt.int32)
        w_route = sb("w_route", [P, KD, NEXP])
        psum = ctx.enter_context(nc.psum_tensor("acc", [P, 8, W], F32))
        SETS = {"A": (0, 1), "B": (2, 3), "C": (4, 5)}
        TB = (6, 7)

        def region(at, *shape):
            n = int(np.prod(shape))
            v = work[:, at:at + n]
            return v if len(shape) == 1 else v.rearrange("p (a b) -> p a b", a=shape[0])

        mix = region(0, NTOK, MIX_W)
        gts = region(5952, NTOK, GATE_W)
        qT_a, kT_a = region(12096, 4, S), region(13120, 1, S)
        qT_b, kT_b = region(13376, 4, S), region(14400, 4, S)
        qT_c, kT_c = region(12096, HEADS, S), region(14144, HEADS, S)
        q_c = region(16192, NTOK, C_HEADS * C_DIM)
        v_c = region(17728, NTOK, YW)
        k_c = region(18752, NTOK, C_HEADS * C_DIM)
        ropeU, ropeV = region(16192, 640), region(16832, 640)
        merged = region(0, NTOK, D)
        xn = region(12096, NTOK, D)
        ff_s, ff_a = region(14144, NTOK, W), region(15168, NTOK, W)
        junk = region(14144, NTOK, D)
        mix2 = region(0, NTOK, 4 * W)
        qT_2, kT_2 = region(4096, 4, S), region(5120, 4, S)
        big = region(6144, BIG_W)
        count = big[:, 0:NTOK * S].rearrange("p (a b) -> p a b", a=NTOK)
        mask = big[:, NTOK * S:2 * NTOK * S].rearrange("p (a b) -> p a b", a=NTOK)
        earlier, ones = big[:, BIG_W - 2 * P:BIG_W - P], big[:, BIG_W - P:]
        poolT = big[:, 2 * NTOK * S:BIG_W - 2 * P].rearrange("p (a g t) -> p a g t", a=NTOK, g=4)
        z_2, o_2 = region(9472, NTOK, W), region(10496, NTOK, W)
        y_e = region(16192, D)
        sel = region(17216, NTOK, P)
        sel_w = region(17472, NTOK, P)
        give = region(17728, NTOK, P)

        ident = tab[:, 0:P]
        rope = tab[:, P:P + NTOK * ROPE_W].rearrange("p (a b) -> p a b", a=NTOK)
        iota = tab[:, P + NTOK * ROPE_W:TAB_W]

        s_raw = [sem(f"raw_landed{i}") for i in range(RAW)]
        s_rawe = [sem(f"expert_raw_landed{i}") for i in range(RAW_E)]
        s_in, s_gain, s_gain_rest, s_gain2, s_big, s_wr, s_out = (sem(n) for n in (
            "inputs_landed", "gains_landed", "other_gains_landed", "gains2_landed", "big_landed", "router_landed",
            "out_landed"))
        s_hi, s_lo, s_used = sem("w_high_ready"), sem("w_low_ready"), sem("w_tile_used")
        s_free = {k: sem(f"acc{k}_emptied") for k in "ABC"}
        s_tp = sem("turned")
        s_tf = [sem("turn_bank0_emptied"), sem("turn_bank1_emptied")]
        s_thi = sem("turned_high_ready")
        s_xn = sem("normed_ready")
        s_pow_in, s_pow = sem("meansq_ready"), sem("rstd_ready")
        s_rs = sem("row_scale_ready")
        s_step = sem("vector_step")
        s_prep = sem("qk_prepared")
        s_sc, s_nm, s_pr = sem("scores_ready"), sem("negmax_ready"), sem("probs_ready")
        s_pw = sem("probs_weighted")
        s_o, s_y = sem("heads_done"), sem("branch_ready")
        s_mrg = sem("merged_ready")
        s_lam, s_lame = sem("lambda_sums"), sem("lambda_exp")
        s_relu = sem("relu_ready")
        s_rt, s_rte = sem("route_diff"), sem("route_exp")
        s_member, s_rounds = sem("members_ready"), sem("rounds_ready")
        s_sel, s_back, s_given = sem("selection_ready"), sem("given_back"), sem("given_back_emptied")
        s_const = sem("constants_set")

        w_in = at_layer(a["w_in"], D)
        uq, ukv = at_layer(a["c_w_uq"], C_QRANK), at_layer(a["c_w_ukv"], C_KVRANK)
        w_br = at_layer(a["w_branch"].rearrange("l n r c -> l (n r) c"), NBR * YW)
        w_o, ff1, ff2 = at_layer(a["w_out"], D), at_layer(a["w_ff1"], D), at_layer(a["w_ff2"], D_FF)
        WIN_W = [W] * 5 + [MIX_W - 5 * W] + [W] * 6
        WIN_0 = [sum(WIN_W[:g]) for g in range(12)]
        tiles1 = []
        for g in range(12):
            tiles1 += columns(w_in, D, WIN_0[g], WIN_W[g])
        T_UQ = len(tiles1)
        UQ_W = (W, 256)
        for g in range(2):
            tiles1 += columns(uq, C_QRANK, g * W, UQ_W[g])
        T_UKV = len(tiles1)
        for g in range(2):
            tiles1 += columns(ukv, C_KVRANK, g * W, W, per=1)
        T_BR = len(tiles1)
        for n in range(NBR):
            for h in range(2):
                tiles1 += columns(w_br, YW, h * W, W, k0=n * YW)
        T_OUT = len(tiles1)
        for h in range(2):
            tiles1 += columns(w_o, D, h * W, W)
        T_FF = len(tiles1)
        tiles1 += ffn_tiles(FF1_STEPS, None, ff1, ff2, D_FF)
        assert len(tiles1) == R1["lo"]

        w_in2, w_o2 = at_layer(a["w_in_2"], D), at_layer(a["w_out_2"], D)
        w_pl = at_layer(a["w_pool_2"].rearrange("l g r c -> l (g r) c"), W)
        wg2, wu2, wd2 = at_layer(a["ffn_wg_2"], D), at_layer(a["ffn_wu_2"], D), at_layer(a["ffn_wd_2"], D_FF2)
        mixer2 = []
        for g in range(4):
            mixer2 += columns(w_in2, D, g * W, W)
        T_POOL = len(mixer2)
        mixer2 += columns(w_pl, W, 0, P)
        T_OUT2 = len(mixer2)
        for h in range(2):
            mixer2 += columns(w_o2, D, h * W, W)
        T_FF2 = len(mixer2)
        fix = lambda ts, r: [(lambda _, f=f: f(r), n, w) for f, n, w in ts]
        tiles2 = fix(mixer2, 0) + list(ffn_tiles(FF2_STEPS, wg2, wu2, wd2, D_FF2))
        tiles3 = fix(mixer2, 1)
        assert len(tiles2) == R2["lo"] and len(tiles3) == R3["lo"], (len(tiles2), len(tiles3))
        wge, wue, wde = (at_layer(a[n].rearrange("m e r c -> (m e) r c"), r) for n, r in (
            ("moe_wg_2", D), ("moe_wu_2", D), ("moe_wd_2", D_FFE)))
        tilese = list(ffn_tiles(FFE_STEPS, wge, wue, wde, D_FFE))
        assert len(tilese) == RE["lo"]

        span1 = lambda r: Span(TURNS1, R1, BASE1, r, tiles1)
        spanf = Span([], RF, BASEF)
        span2 = Span(TURNS2, R2, BASE2, 0, tiles2)
        span3 = Span(TURNS3, R3, BASE3, 0, tiles3)
        spane = lambda r: Span(TURNSE, RE, BASEE, r, tilese, RAW_E, BASEE["lo"])
        spang = Span([], RF, BASEE)

        raws = [raw[:, b] for b in range(RAW)]
        raws_e = raws + [region(4 * W * b, 4 * W) for b in range(RAW_E - RAW)]

        def raw_of(m, j):
            b = m.buffer(j)
            return (raws_e[b], s_rawe[b]) if m.ring == RAW_E else (raws[b], s_raw[b])

        def rounds(eng, body, finish=None):
            eng.wait_ge(s_rounds, 1)
            with eng.Fori(0, NEXP) as e:
                n = eng.value_load(rounds_i[0:1, 0, bass.ds(e, 1)], min_val=1, max_val=2)
                before = eng.value_load(rounds_i[0:1, 1, bass.ds(e, 1)], min_val=0, max_val=2 * NEXP)
                with eng.Fori(0, n) as b:
                    body(spane(before + b), e)
            if finish:
                total = eng.value_load(rounds_i[0:1, 1, NEXP:NEXP + 1], min_val=NEXP, max_val=2 * NEXP)
                finish(spane(total))

        block = ctx.enter_context(nc.Block())

        @block.sync
        def _(sp):
            sp.sem_inc(s_lo, 2 * RAW)
            sp.sem_inc(s_xn, 1)
            sp.dma_start(x_sb[:], a["x"][0].rearrange("(i p) d -> p i d", p=P)).then_inc(s_in, 16)
            sp.dma_start(tab[:], a["tables"]).then_inc(s_in, 16)

            def load(m, r, j0, j1):
                for j in range(j0, j1):
                    src, n, w = m.tiles[j]
                    buf, landed = raw_of(m, j)
                    sp.wait_ge(s_lo, m.at("lo", j + 1 - m.ring))
                    sp.dma_start(buf[:, 0:n * w].rearrange("p (c n) -> p c n", c=n), src(r)).then_inc(landed, 16)

            def gain(cols, src, done):
                sp.dma_start(gains[:, cols[0]:cols[1]], src.partition_broadcast(P)).then_inc(done, 16)

            with sp.Fori(0, DEPTH) as r:
                m = span1(r)
                sp.wait_ge(s_xn, m.at("xn", 0))
                row = a["gains1"][bass.ds(r, 1), :].rearrange("a n -> (a n)")
                gain((0, D), row[0:D], s_gain)
                load(m, r, 0, RAW)
                gain((D, G1_W), row[D:G1_W], s_gain_rest)
                load(m, r, RAW, len(tiles1))
            sp.wait_ge(s_xn, spanf.at("xn", 0))
            gain((2 * D, 3 * D), a["final_g"], s_gain2)
            gain((0, 2 * D), a["gains2"][0, 0:2 * D], s_gain2)
            sp.dma_start(w_route[:], a["w_router_2"][0].rearrange("(c p) e -> p c e", p=P)).then_inc(s_wr, 16)
            sp.dma_start(big, a["big"]).then_inc(s_big, 16)
            load(span2, 0, 0, RAW)
            sp.wait_ge(s_xn, span2.at("xn", 1))
            gain((2 * D, 3 * D), a["gains2"][0, 2 * D:3 * D], s_gain2)
            load(span2, 0, RAW, T_FF2 + RAW)
            sp.wait_ge(s_xn, span3.at("xn", 0))
            gain((0, 3 * D), a["gains2"][1, :], s_gain2)
            load(span2, 0, T_FF2 + RAW, len(tiles2))
            load(span3, 0, 0, len(tiles3))
            sp.wait_ge(s_xn, spang.at("xn", 0))
            gain((0, D), a["final_norm_2"], s_gain2)
            rounds(sp, lambda m, e: load(m, e, 0, len(tilese)))
            sp.wait_ge(s_xn, spang.at("xn", NTOK))
            sp.dma_start(out[0].rearrange("(i p) d -> p i d", p=P), xn).then_inc(s_out, 16)
            sp.wait_ge(s_out, 16)

        @block.gpsimd
        def _(pool):
            nc.gpsimd.memset(neghalf[:], -0.5).then_inc(s_const, 1)
            nc.gpsimd.memset(meansq[:], 1.0).then_inc(s_const, 1)
            pool.wait_ge(s_const, 2)
            with pool.Fori(0, (BASEE["pw"] + RF["pw"]) // 2) as r:
                for b in range(2):
                    pool.wait_ge(s_pow_in, 2 * r + (b + 1))
                    nc.gpsimd.tensor_tensor(rstd[:, b], meansq[:, b], neghalf[:], ALU.pow).then_inc(s_pow, 1)

        @block.scalar
        def _(act):
            def high(m, j):
                t = m.tile(j)
                n, w = m.tiles[j][1:]
                buf, landed = raw_of(m, j)
                act.wait_ge(landed, m.landed(j))
                for half, c0, c1, count in halves(n):
                    act.wait_ge(s_used, m.at("used", j - SPLIT, half + count))
                    nc.scalar.activation(whi[:, t % SPLIT, half, 0:(c1 - c0) * w], buf[:, c0 * w:c1 * w], ACT.Copy)\
                      .then_inc(s_hi, count)

            def ahead(m, j):
                if j + 1 < len(m.tiles):
                    high(m, j + 1)

            def turned_high(m, k, view, blocks, cols):
                b = m.bank(k)
                act.wait_ge(s_tp, m.at("tp", k + 1))
                src = psum[:, TB[b], 0:blocks * cols].rearrange("p (c t) -> p c t", c=blocks)
                nc.scalar.activation(view, src, ACT.Copy).then_inc(s_thi, 1)

            def halves_high(m, stage, j):
                for c in range(2):
                    for i in range(NTOK):
                        turned_high(m, m.start[stage] + 2 * c + i, hT[:, 0, 4 * c:4 * c + 4, i * P:(i + 1) * P], 4, P)
                    if c == 0:
                        high(m, j + 1)

            def normed_high(m, stage):
                for n in range(4):
                    i, c = n // 2, n % 2
                    turned_high(m, m.start[stage] + n, hT[:, 0, 4 * c:4 * c + 4, i * P:(i + 1) * P], 4, P)

            def plain_turn(m, k, dst, parts, blocks, cols, scale):
                b = m.bank(k)
                act.wait_ge(s_tp, m.at("tp", k + 1))
                src = psum[0:parts, TB[b], 0:blocks * cols].rearrange("p (c t) -> p c t", c=blocks)
                nc.scalar.activation(dst, src, ACT.Copy, scale=scale).then_inc(s_tf[b], 1)

            def softmax_exp(m, n):
                act.wait_ge(s_nm, m.at("sb", n + 1))
                for i in range(NTOK):
                    ins = nc.scalar.activation(probs[:, n % 4, i], psum[:, n % 4, i * S:(i + 1) * S], ACT.Exp,
                                               bias=negmax[:, n, i:i + 1], accum_out=rowsum[:, n, i:i + 1])
                ins.then_inc(s_pr, 1)

            def evac(m, key, j, dst, w, func=ACT.Copy, norm=None):
                act.wait_ge(s_used, m.at("used", j + 1))
                for i in range(NTOK):
                    scale = 1.0 if norm is None else row_scale[:, norm, i:i + 1]
                    ins = nc.scalar.activation(dst(i), psum[:, SETS[key][i], 0:w], func, scale=scale)
                    ins.then_inc(s_free[key], 1)

            def ffn(m, steps, j, hidden, a0):
                use, turn, gated = a0, m.start["ff"], hidden != D_FF
                act.wait_ge(s_rs, m.at("rs", 2))
                for kind, g, k in steps[1:]:
                    w = min(W, hidden - g * W)
                    if kind in TILE_STEPS:
                        ahead(m, j)
                        j += 1
                    elif kind in ("act_up", "act_gate"):
                        if kind == "act_gate":
                            evac(m, "A", j - 1, lambda i: ff_s[:, i, 0:w], w, ACT.Silu, 1)
                        elif not gated:
                            act.wait_ge(s_used, m.at("used", j))
                            for i in range(NTOK):
                                nc.scalar.activation(ff_s[:, i, 0:w], psum[:, SETS["A"][i], 0:w], ACT.Relu,
                                                     scale=row_scale[:, 1, i:i + 1]).then_inc(s_relu, 1)
                        use += 1
                    elif kind == "turn":
                        c = 8 + 4 * (g % 2)
                        for i in range(NTOK):
                            turned_high(m, turn, hT[:, 0, c:c + w // P, i * P:(i + 1) * P], w // P, P)
                            turn += 1

            act.sem_inc(s_used, 2 * SPLIT)

            with act.Fori(0, DEPTH) as r:
                m = span1(r)
                high(m, 0)
                halves_high(m, "ln1", 0)
                act.wait_ge(s_lam, r + 1)
                nc.scalar.activation(lam[:, 2:4], lam[:, 0:2], ACT.Exp).then_inc(s_lame, 1)
                act.wait_ge(s_rs, m.at("rs", 1))
                for g in range(12):
                    if g:
                        ahead(m, 2 * g)
                    ahead(m, 2 * g + 1)
                    key, w = "AB"[g % 2], WIN_W[g]
                    if g < 6:
                        evac(m, key, 2 * g + 1, lambda i: mix[:, i, WIN_0[g]:WIN_0[g] + w], w, norm=0)
                    else:
                        evac(m, key, 2 * g + 1, lambda i: gts[:, i, (g - 6) * W:(g - 5) * W], w, ACT.Sigmoid, 0)
                for i in range(NTOK):
                    turned_high(m, m.start["cc"] + 2 * i, hT[:, 0, 0:3, i * P:(i + 1) * P], 3, P)
                    turned_high(m, m.start["cc"] + 2 * i + 1, hT[:, 0, 3:5, i * P:(i + 1) * P], 2, P)
                for g in range(2):
                    ahead(m, T_UQ + g)
                    evac(m, "AB"[g], T_UQ + g, lambda i: q_c[:, i, g * W:g * W + UQ_W[g]], UQ_W[g])
                for g in range(2):
                    ahead(m, T_UKV + 2 * g)
                    ahead(m, T_UKV + 2 * g + 1)
                    key = "AB"[g]
                    act.wait_ge(s_used, m.at("used", T_UKV + 2 * g + 2))
                    for i in range(NTOK):
                        src = psum[:, SETS[key][i], :].rearrange("p (h e) -> p h e", h=4)
                        kd = k_c[:, i].rearrange("p (h e) -> p h e", h=8)[:, 4 * g:4 * g + 4, 0:C_NOPE]
                        vd = v_c[:, i].rearrange("p (h e) -> p h e", h=8)[:, 4 * g:4 * g + 4, :]
                        nc.scalar.activation(kd, src[:, :, 0:C_NOPE], ACT.Copy)
                        nc.scalar.activation(vd, src[:, :, C_NOPE:], ACT.Copy).then_inc(s_free[key], 1)
                for i in range(NTOK):
                    plain_turn(m, m.start["qa"] + i, qT_a[:, :, i * P:(i + 1) * P], P, 4, P, A_DIM ** -0.5)
                for i in range(NTOK):
                    plain_turn(m, m.start["ka"] + i, kT_a[:, :, i * P:(i + 1) * P], P, 1, P, 1.0)
                for i in range(NTOK):
                    plain_turn(m, m.start["qb"] + i, qT_b[:, :, i * P:(i + 1) * P], P, 4, P, B_QK ** -0.5)
                for i in range(NTOK):
                    plain_turn(m, m.start["kb"] + i, kT_b[:, :, i * P:(i + 1) * P], P, 4, P, 1.0)
                for n in range(8):
                    softmax_exp(m, n)
                for h in range(B_HEADS + 1):
                    if h < B_HEADS:
                        softmax_exp(m, 8 + 2 * h)
                        softmax_exp(m, 9 + 2 * h)
                    if h:
                        b = m.bank(m.start["pb"] + h - 1)
                        act.wait_ge(s_tp, m.at("tp", m.start["pb"] + h))
                        nc.scalar.activation(probsT[:, (h - 1) % 2], psum[:, TB[b]].rearrange(
                            "p (c t) -> p c t", c=2), ACT.Copy).then_inc(s_tf[b], 1)
                for stage, dst, scale in (("qc", qT_c, C_DIM ** -0.5), ("kc", kT_c, 1.0)):
                    for n in range(4):
                        i, c = n // 2, n % 2
                        plain_turn(m, m.start[stage] + n, dst[0:C_DIM, 4 * c:4 * c + 4, i * P:(i + 1) * P],
                                   C_DIM, 4, P, scale)
                for n in range(24, 32):
                    softmax_exp(m, n)
                for n in range(NBR):
                    for i in range(NTOK):
                        turned_high(m, m.start["y"] + 2 * n + i, hT[:, 0, 4 * n:4 * n + 4, i * P:(i + 1) * P], 4, P)
                for j in range(T_BR, T_OUT):
                    ahead(m, j)
                halves_high(m, "mrg", T_OUT)
                for j in range(T_OUT + 1, T_FF):
                    ahead(m, j)
                halves_high(m, "ln2", T_FF)
                ffn(m, FF1_STEPS, T_FF + 1, D_FF, 12)

            def mixer2_act(m):
                high(m, 0)
                halves_high(m, "mix", 0)
                act.wait_ge(s_rs, m.at("rs", 1))
                for g in range(4):
                    if g:
                        ahead(m, 2 * g)
                    ahead(m, 2 * g + 1)
                    evac(m, "AB"[g % 2], 2 * g + 1, lambda i: mix2[:, i, g * W:(g + 1) * W], W, norm=0)
                for n in range(2):
                    turned_high(m, m.start["dt"] + n, hT[:, 0, 8 + 2 * n:10 + 2 * n, :], 2, S)
                ahead(m, T_POOL)
                evac(m, "A", T_POOL, lambda i: z_2[:, i], W)
                for stage, dst, scale in (("q2", qT_2, HV ** -0.5), ("k2", kT_2, 1.0)):
                    for i in range(NTOK):
                        plain_turn(m, m.start[stage] + i, dst[:, :, i * P:(i + 1) * P], P, 4, P, scale)
                for n in range(8):
                    act.wait_ge(s_nm, m.at("sb", n + 1))
                    for i in range(NTOK):
                        ins = nc.scalar.activation(probs[:, n % 4, i], probs[:, n % 4, i], ACT.Exp,
                                                   bias=negmax[:, n, i:i + 1])
                    ins.then_inc(s_pr, 1)
                halves_high(m, "y2", T_OUT2)
                for j in range(T_OUT2 + 1, T_FF2):
                    ahead(m, j)

            mixer2_act(span2)
            halves_high(span2, "ffn", T_FF2)
            ffn(span2, FF2_STEPS, T_FF2 + 1, D_FF2, 4)
            mixer2_act(span3)
            normed_high(span3, "ffn")
            act.wait_ge(s_rt, 1)
            nc.scalar.activation(route[:, 24:26], route[:, 16:18], ACT.Exp).then_inc(s_rte, 1)

            def finish(m, half):
                act.wait_ge(s_used, m.at("used", 0))
                nc.scalar.activation(y_e[:, half * W:(half + 1) * W], psum[:, 2 + half], ACT.Copy)\
                  .then_inc(s_free["C"], 1)

            def expert(m, e):
                high(m, 0)
                for n in range(2):
                    turned_high(m, m.start["take"] + n, hT[:, 0, 4 * n:4 * n + 4, 0:P], 4, P)
                j, turn = 0, m.start["ff"]
                for kind, g, k in FFE_STEPS:
                    if kind in TILE_STEPS:
                        if j < 2:
                            finish(m, j)
                        ahead(m, j)
                        if j == 1:
                            plain_turn(m, m.start["give"], give, P, 2, P, 1.0)
                        j += 1
                    elif kind == "act_gate":
                        act.wait_ge(s_used, m.at("used", j))
                        nc.scalar.activation(ff_s[:, 0], psum[:, 0], ACT.Silu).then_inc(s_free["A"], 1)
                    elif kind == "turn":
                        c = 8 + 4 * (g % 2)
                        turned_high(m, turn, hT[:, 0, c:c + 4, 0:P], 4, P)
                        turn += 1

            rounds(act, expert, lambda m: [finish(m, half) for half in range(2)])

        @block.vector
        def _(dve):
            chain = {"base": 0, "n": 0, "rise": 0}
            powers = [0]

            def link(m, ins):
                chain["n"] += 1
                ins.then_inc(s_step, 1)
                fixed = chain["base"] + chain["n"]
                dve.wait_ge(s_step, m.turn * chain["rise"] + fixed if chain["rise"] else fixed)

            def low(m, j):
                t = m.tile(j)
                n, w = m.tiles[j][1:]
                for half, c0, c1, count in halves(n):
                    dve.wait_ge(s_hi, m.at("hi", j, half + count))
                    hi, lo = (t_[:, t % SPLIT, half, 0:(c1 - c0) * w] for t_ in (whi, wlo))
                    nc.vector.tensor_tensor(lo, raw_of(m, j)[0][:, c0 * w:c1 * w], hi.bitcast(F32), ALU.subtract)\
                      .then_inc(s_lo, count)

            def ahead(m, j):
                if j + 1 < len(m.tiles):
                    low(m, j + 1)

            split_turns = [0]

            def turned_low(m, k, chunks, cols, blocks, width):
                b = m.bank(k)
                split_turns[0] += 1
                dve.wait_ge(s_thi, m.at("th", split_turns[0]))
                src = psum[:, TB[b], 0:blocks * width].rearrange("p (c t) -> p c t", c=blocks)
                nc.vector.tensor_tensor(hT[:, 1, chunks, cols], src, hT[:, 0, chunks, cols].bitcast(F32),
                                        ALU.subtract).then_inc(s_tf[b], 1)

            def quarter_low(m, stage):
                for n in range(4):
                    i, c = n // 2, n % 2
                    turned_low(m, m.start[stage] + n, slice(4 * c, 4 * c + 4), slice(i * P, (i + 1) * P), 4, P)

            def slot(m):
                return meansq[:, (m.base["pw"] + powers[0]) % 2]

            def send(m, ins):
                r = rstd[:, (m.base["pw"] + powers[0]) % 2]
                powers[0] += 1
                ins.then_inc(s_pow_in, 1)
                return r, powers[0]

            def mean_squares(m, rows, eps=EPS):
                for k, (src, squares) in enumerate(rows):
                    n = src.shape[-1]
                    ins = nc.vector.tensor_tensor_reduce(out=squares, in0=src, in1=src, scale=1.0 / n, scalar=eps,
                                                         op0=ALU.mult, op1=ALU.add, accum_out=slot(m)[:, k:k + 1])
                    if k < len(rows) - 1:
                        link(m, ins)
                return ins

            def gain_rows(m, rows, r, sent):
                dve.wait_ge(s_pow, m.at("pw", sent))
                for k, (src, gain, dst, _) in enumerate(rows):
                    yield nc.vector.scalar_tensor_tensor(out=dst, in0=src, scalar=r[:, k:k + 1], in1=gain,
                                                         op0=ALU.mult, op1=ALU.mult)

            def norm(m, rows):
                yield from gain_rows(m, rows, *send(m, mean_squares(m, [(src, squares) for src, _, _, squares in rows])))

            def norm_residual(m, g0):
                for ins in norm(m, [(x_sb[:, i], gains[:, g0:g0 + D], xn[:, i], xn[:, i]) for i in range(NTOK)]):
                    ins.then_inc(s_xn, 1)

            def gained(m, g0):
                for c in range(2):
                    cols = slice(c * W, (c + 1) * W)
                    for i in range(NTOK):
                        nc.vector.tensor_tensor(xn[:, i, cols], x_sb[:, i, cols], gains[:, g0 + c * W:g0 + (c + 1) * W],
                                                ALU.mult).then_inc(s_xn, 1)

            def half_low(m, stage, c):
                for i in range(NTOK):
                    turned_low(m, m.start[stage] + 2 * c + i, slice(4 * c, 4 * c + 4), slice(i * P, (i + 1) * P), 4, P)

            def scaled(m, stage, g0, j, squared=False):
                gained(m, g0)
                half_low(m, stage, 0)
                ins = mean_squares(m, [(x_sb[:, i], junk[:, i]) for i in range(NTOK)])
                r, n = send(m, ins)
                low(m, j + 1)
                half_low(m, stage, 1)
                dve.wait_ge(s_pow, m.at("pw", n))
                k = int(stage in ("ln2", "ffn"))
                if squared:
                    ins = nc.vector.tensor_tensor(row_scale[:, k], r[:, 0:NTOK], r[:, 0:NTOK], ALU.mult)
                else:
                    ins = nc.vector.tensor_copy(row_scale[:, k], r[:, 0:NTOK])
                ins.then_inc(s_rs, 1)
                dve.wait_ge(s_rs, m.at("rs", k + 1))

            def over(v, h):
                return v.unsqueeze(1).broadcast_to([P, h, v.shape[-1]])

            def each(v, n):
                return v.unsqueeze(2).broadcast_to([P, v.shape[-1], n])

            def heads(v, h):
                return v.rearrange("p (h e) -> p h e", h=h)

            def rotate(m, src, cos, sin, axes, u, v):
                h, w = src.shape[1], src.shape[2]
                half = w // axes // 2
                u, v = (heads(t[:, 0:h * w], h) for t in (u, v))
                nc.vector.tensor_tensor(u, src, over(cos, h), ALU.mult)
                ax = lambda t: t.rearrange("p h (a d) -> p h a d", a=axes)
                sb_ = over(sin, h)
                for o in (0, half):
                    s0 = half - o
                    if axes == 1:
                        ins = nc.vector.tensor_tensor(v[:, :, o:o + half], src[:, :, s0:s0 + half],
                                                      sb_[:, :, o:o + half], ALU.mult)
                    else:
                        ins = nc.vector.tensor_tensor(ax(v)[:, :, :, o:o + half], ax(src)[:, :, :, s0:s0 + half],
                                                      ax(sb_)[:, :, :, o:o + half], ALU.mult)
                link(m, ins)
                return u, v

            def accumulate(m, key, use, half, j):
                dve.wait_ge(s_used, m.at("used", j + 1))
                for i in range(NTOK):
                    xs = x_sb[:, i, half * W:(half + 1) * W]
                    nc.vector.tensor_tensor(xs, psum[:, SETS[key][i]], xs, ALU.add).then_inc(s_free[key], 1)
                dve.wait_ge(s_free[key], m.at("f" + key, NTOK * (use + 1)))

            def ffn(m, steps, j, hidden, a0):
                use, turn, gated = a0, m.start["ff"], hidden != D_FF
                relu = 0
                for kind, g, k in steps[1:]:
                    w = min(W, hidden - g * W)
                    if kind in TILE_STEPS:
                        ahead(m, j)
                        j += 1
                    elif kind == "act_gate":
                        use += 1
                    elif kind == "act_up":
                        dve.wait_ge(s_used, m.at("used", j))
                        for i in range(NTOK):
                            ps = psum[:, SETS["A"][i], 0:w]
                            if gated:
                                ins = nc.vector.scalar_tensor_tensor(
                                    out=ff_a[:, i, 0:w], in0=ps, scalar=row_scale[:, 1, i:i + 1],
                                    in1=ff_s[:, i, 0:w], op0=ALU.mult, op1=ALU.mult)
                            else:
                                relu += 1
                                dve.wait_ge(s_relu, m.at("relu", relu))
                                ins = nc.vector.scalar_tensor_tensor(out=ff_a[:, i, 0:w], in0=ps, scalar=0.0,
                                                                     in1=ff_s[:, i, 0:w], op0=ALU.max, op1=ALU.mult)
                            ins.then_inc(s_free["A"], 1)
                        use += 1
                    elif kind == "turn":
                        c = 8 + 4 * (g % 2)
                        for i in range(NTOK):
                            turned_low(m, turn, slice(c, c + w // P), slice(i * P, (i + 1) * P), w // P, P)
                            turn += 1

            def row_max(m, n):
                dve.wait_ge(s_sc, m.at("sb", n + 1))
                nc.vector.tensor_reduce(negmax[:, n], psum[:, n % 4].rearrange("p (i k) -> p i k", i=NTOK),
                                        AX.X, ALU.max, negate=True).then_inc(s_nm, 1)

            def turned_probs(m, k, h):
                b = m.bank(k)
                dve.wait_ge(s_tp, m.at("tp", k + 1))
                nc.vector.tensor_copy(probsT[:, h % 2], psum[:, TB[b]].rearrange("p (c t) -> p c t", c=2))\
                  .then_inc(s_tf[b], 1)

            def softmax_heads(m, n0, stage, between=iter(())):
                for h in range(3):
                    row_max(m, n0 + h)
                for h in range(HEADS):
                    turned_probs(m, m.start[stage] + h, h)
                    if h + 3 < HEADS:
                        row_max(m, n0 + h + 3)
                    if h % 2:
                        next(between, None)

            def divide(m, n0, branch, dst):
                link(m, nc.vector.reciprocal(rinv[:, n0:n0 + HEADS], rowsum[:, n0:n0 + HEADS]))
                dve.wait_ge(s_o, m.at("br", branch + 1))
                for i in range(NTOK):
                    ins = nc.vector.tensor_tensor(heads(dst(i), HEADS), heads(psum[:, SETS["C"][i]], HEADS),
                                                  each(rinv[:, n0:n0 + HEADS, i], HV), ALU.mult)
                ins.then_inc(s_y, 1)

            def table(i, at, w):
                return rope[:, i, at:at + w]

            dve.wait_ge(s_in, 32)
            dve.wait_ge(s_const, 2)
            g1 = lambda n: gains[:, G1[n][0]:G1[n][1]]

            def prep_latents(m):
                v = [(mix[:, i, o:o + w], n) for i in range(NTOK)
                     for n, o, w in (("cq", OC_Q, C_QRANK), ("ckv", OC_KV, C_KVRANK))]
                r, n = send(m, mean_squares(m, [(src, scr[:, 0:src.shape[-1]]) for src, _ in v]))
                yield
                dve.wait_ge(s_pow, m.at("pw", n))
                for k, (src, name) in enumerate(v):
                    ins = nc.vector.scalar_tensor_tensor(out=src, in0=src, scalar=r[:, k:k + 1], in1=g1(name),
                                                         op0=ALU.mult, op1=ALU.mult)
                ins.then_inc(s_prep, 1)
                yield

            def prep_a(m, i):
                qk = mix[:, i, 0:OA_V]
                n = A_HEADS + A_KV
                link(m, nc.vector.tensor_tensor(ropeU, qk, qk, ALU.mult))
                ms = slot(m)[:, 0:n]
                link(m, nc.vector.tensor_reduce(ms, heads(ropeU, n), AX.X, ALU.add))
                r, sent = send(m, nc.vector.tensor_scalar(ms, ms, 1.0 / A_DIM, EPS, ALU.mult, ALU.add))
                yield
                dve.wait_ge(s_pow, m.at("pw", sent))
                link(m, nc.vector.tensor_tensor(heads(qk, n), heads(qk, n), each(r[:, 0:n], A_DIM), ALU.mult))
                q, k = qk[:, 0:OA_K], qk[:, OA_K:]
                nc.vector.tensor_tensor(heads(q, A_HEADS), heads(q, A_HEADS), over(g1("aq"), A_HEADS), ALU.mult)
                link(m, nc.vector.tensor_tensor(heads(k, A_KV), heads(k, A_KV), over(g1("ak"), A_KV), ALU.mult))
                yield
                u, v = rotate(m, heads(qk, n), table(i, 0, 64), table(i, 64, 64), 2, ropeU, ropeV)
                yield
                order = lambda t: t[:, 0:A_HEADS].rearrange("p (g c) d -> p g c d", g=A_KV)
                nc.vector.tensor_tensor(q.rearrange("p (c g d) -> p g c d", c=4, g=A_KV), order(u), order(v), ALU.add)
                ins = nc.vector.tensor_tensor(heads(k, A_KV), u[:, A_HEADS:], v[:, A_HEADS:], ALU.add)
                if i == NTOK - 1:
                    ins.then_inc(s_prep, 1)
                else:
                    link(m, ins)
                yield

            def prep_b(m, i):
                v = heads(mix[:, i, OB_Q:OB_V], 4 * B_HEADS)[:, :, 0:B_ROT]
                u, w = rotate(m, v, table(i, 128, 8), table(i, 136, 8), 1, scr[:, 0:256], scr[:, 256:512])
                ins = nc.vector.tensor_tensor(v, u, w, ALU.add)
                if i == NTOK - 1:
                    ins.then_inc(s_prep, 1)
                else:
                    link(m, ins)
                yield

            def prep(m):
                yield from prep_latents(m)
                for i in range(NTOK):
                    yield from prep_a(m, i)
                for i in range(NTOK):
                    yield from prep_b(m, i)

            def prep_c(m):
                for i in range(NTOK):
                    cos, sin = table(i, 144, 32), table(i, 176, 32)
                    q = heads(q_c[:, i], C_HEADS)[:, :, C_NOPE:]
                    u, v = rotate(m, q, cos, sin, 1, scr[:, 0:256], scr[:, 256:512])
                    link(m, nc.vector.tensor_tensor(q, u, v, ALU.add))
                    k = heads(mix[:, i, OC_KR:MIX_W], 1)
                    u, v = rotate(m, k, cos, sin, 1, scr[:, 0:256], scr[:, 256:512])
                    link(m, nc.vector.tensor_tensor(k, u, v, ALU.add))
                    ins = nc.vector.tensor_copy(heads(k_c[:, i], C_HEADS)[:, :, C_NOPE:],
                                                over(mix[:, i, OC_KR:MIX_W], C_HEADS))
                ins.then_inc(s_prep, 1)

            def lambdas(m):
                l = g1("lam")
                for k in range(2):
                    ins = nc.vector.tensor_tensor_reduce(
                        out=scr[:, 0:B_QK], in0=l[:, 2 * k * B_QK:(2 * k + 1) * B_QK],
                        in1=l[:, (2 * k + 1) * B_QK:(2 * k + 2) * B_QK], scale=1.0, scalar=0.0,
                        op0=ALU.mult, op1=ALU.add, accum_out=lam[:, k:k + 1])
                    if k == 0:
                        link(m, ins)
                ins.then_inc(s_lam, 1)
                dve.wait_ge(s_lame, m.turn + 1)
                link(m, nc.vector.scalar_tensor_tensor(
                    out=lam[:, 4:5], in0=lam[:, 2:3], scalar=lam[:, 3:4], in1=g1("linit")[:, 0:1],
                    op0=ALU.subtract, op1=ALU.add))

            def combine(m, h):
                n = 8 + 2 * h
                p0, p1 = n % 4, (n + 1) % 4
                dve.wait_ge(s_pr, m.at("sb", n + 2))
                link(m, nc.vector.reciprocal(rinv[:, n:n + 2], rowsum[:, n:n + 2]))
                link(m, nc.vector.tensor_scalar(rinv[:, n + 1], rinv[:, n + 1], lam[:, 4:5], None, ALU.mult))
                for i in range(NTOK):
                    ins = nc.vector.tensor_scalar(probs[:, p1, i], probs[:, p1, i], rinv[:, n + 1, i:i + 1], None,
                                                  ALU.mult)
                link(m, ins)
                for i in range(NTOK):
                    ins = nc.vector.scalar_tensor_tensor(
                        out=probs[:, p0, i], in0=probs[:, p0, i], scalar=rinv[:, n, i:i + 1], in1=probs[:, p1, i],
                        op0=ALU.mult, op1=ALU.subtract)
                ins.then_inc(s_pw, 1)

            def copy_b(m):
                dve.wait_ge(s_o, m.at("br", 2))
                for i in range(NTOK):
                    ins = nc.vector.tensor_copy(mix[:, i, OB_Q:OB_Q + YW], psum[:, SETS["C"][i]])
                ins.then_inc(s_y, 1)

            def finish_b(m):
                y = [mix[:, i, OB_Q:OB_Q + YW] for i in range(NTOK)]
                ms = slot(m)
                dve.wait_ge(s_y, m.at("br", 2))
                for i in range(NTOK):
                    link(m, nc.vector.tensor_tensor(scr[:], y[i], y[i], ALU.mult))
                    link(m, nc.vector.tensor_reduce(ms[:, i * B_HEADS:(i + 1) * B_HEADS], heads(scr[:], B_HEADS),
                                                    AX.X, ALU.add))
                r, n = send(m, nc.vector.tensor_scalar(ms, ms, 1.0 / HV, EPS, ALU.mult, ALU.add))
                yield
                dve.wait_ge(s_pow, m.at("pw", n))
                for i in range(NTOK):
                    ins = nc.vector.tensor_tensor(heads(y[i], B_HEADS), heads(y[i], B_HEADS),
                                                  each(r[:, i * B_HEADS:(i + 1) * B_HEADS], HV), ALU.mult)
                link(m, ins)
                for i in range(NTOK):
                    nc.vector.scalar_tensor_tensor(
                        out=heads(y[i], B_HEADS), in0=heads(y[i], B_HEADS), scalar=g1("linit")[:, 1:2],
                        in1=over(g1("sub"), B_HEADS), op0=ALU.mult, op1=ALU.mult)
                yield

            chain["rise"] = STEP_LAYER1
            with dve.Fori(0, DEPTH) as r:
                m = span1(r)
                chain["n"] = powers[0] = split_turns[0] = 0
                low(m, 0)
                dve.wait_ge(s_gain, 16 * (r + 1))
                scaled(m, "ln1", G1["ln1"][0], 0)
                dve.wait_ge(s_gain_rest, 16 * (r + 1))
                lambdas(m)
                pieces = prep(m)
                for j in range(1, T_BR):
                    if j == 24:
                        for i in range(NTOK):
                            c = slice(i * P, (i + 1) * P)
                            turned_low(m, m.start["cc"] + 2 * i, slice(0, 3), c, 3, P)
                            turned_low(m, m.start["cc"] + 2 * i + 1, slice(3, 5), c, 2, P)
                    ahead(m, j)
                    if j == 12:
                        dve.wait_ge(s_free["A"], m.at("fA", 6))
                        dve.wait_ge(s_free["B"], m.at("fB", 6))
                    if j >= 12:
                        next(pieces, None)
                dve.wait_ge(s_free["B"], m.at("fB", 16))
                prep_c(m)
                softmax_heads(m, 0, "pa")
                divide(m, 0, 0, lambda i: mix[:, i, 0:YW])
                for h in range(2):
                    row_max(m, 8 + 2 * h)
                    row_max(m, 9 + 2 * h)
                for h in range(B_HEADS):
                    combine(m, h)
                    if h + 2 < B_HEADS:
                        row_max(m, 12 + 2 * h)
                        row_max(m, 13 + 2 * h)
                copy_b(m)
                softmax_heads(m, 24, "pc", finish_b(m))
                divide(m, 24, 2, lambda i: mix[:, i, OB_K:OB_K + YW])
                for n in range(NBR):
                    for i in range(NTOK):
                        turned_low(m, m.start["y"] + 2 * n + i, slice(4 * n, 4 * n + 4),
                                   slice(i * P, (i + 1) * P), 4, P)
                for n in range(NBR):
                    for h in range(2):
                        key, use = "AB"[h], 8 + n
                        ahead(m, T_BR + 2 * n + h)
                        dve.wait_ge(s_used, m.at("used", T_BR + 2 * n + h + 1))
                        for i in range(NTOK):
                            mg = merged[:, i, h * W:(h + 1) * W]
                            gt = gts[:, i, n * D + h * W:n * D + (h + 1) * W]
                            dst = mg if n == 0 else heads(scr[:], 1)[:, 0]
                            nc.vector.tensor_tensor(dst, psum[:, SETS[key][i]], gt, ALU.mult)\
                              .then_inc(s_free[key], 1)
                            if n:
                                dve.wait_ge(s_free[key], m.at("f" + key, NTOK * use + i + 1))
                                ins = nc.vector.tensor_tensor(mg, mg, scr[:], ALU.add)
                                if n < NBR - 1 or i < NTOK - 1:
                                    link(m, ins)
                                else:
                                    ins.then_inc(s_mrg, 1)
                                    dve.wait_ge(s_mrg, m.turn * 2 + (h + 1))
                        if n == 0:
                            dve.wait_ge(s_free[key], m.at("f" + key, NTOK * (use + 1)))
                half_low(m, "mrg", 0)
                low(m, T_OUT + 1)
                half_low(m, "mrg", 1)
                for h in range(2):
                    if h:
                        ahead(m, T_OUT + 2 * h)
                    ahead(m, T_OUT + 2 * h + 1)
                    accumulate(m, "AB"[h], 11, h, T_OUT + 2 * h + 1)
                scaled(m, "ln2", G1["ln2"][0], T_FF, squared=True)
                ffn(m, FF1_STEPS, T_FF + 1, D_FF, 12)
                accumulate(m, "B", 12, 0, len(tiles1) - 2)
                accumulate(m, "C", 0, 1, len(tiles1) - 1)
                assert chain["n"] == STEP_LAYER1, chain
            chain.update(base=DEPTH * STEP_LAYER1, n=0, rise=0)
            powers[0] = split_turns[0] = 0
            dve.wait_ge(s_gain2, 32)
            m = spanf
            mean_squares(m, [(x_sb[:, i], junk[:, i]) for i in range(NTOK)]).then_inc(s_pow_in, 1)
            powers[0] = 1
            dve.wait_ge(s_pow_in, m.at("pw", 1))
            r_final = rstd[:, m.base["pw"] % 2, 0:NTOK]
            for i in range(NTOK):
                ins = nc.vector.tensor_tensor(x_sb[:, i], x_sb[:, i], gains[:, 2 * D:3 * D], ALU.mult)
            link(m, ins)
            gained(span2, G2["mix"][0])
            powers[0] = split_turns[0] = 0
            m = span2
            low(m, 0)
            half_low(m, "mix", 0)
            link(m, mean_squares(m, [(x_sb[:, i], junk[:, i]) for i in range(NTOK)], eps=0.0))
            dve.wait_ge(s_pow, m.at("pw", 0))
            ms, r_mix = slot(m)[:, 0:NTOK], rstd[:, m.base["pw"] % 2, 0:NTOK]
            for _ in range(2):
                link(m, nc.vector.tensor_tensor(ms, ms, r_final, ALU.mult))
            nc.vector.tensor_scalar(ms, ms, EPS, None, ALU.add).then_inc(s_pow_in, 1)
            powers[0] = 1
            low(m, 1)
            half_low(m, "mix", 1)
            for i in range(NTOK):
                ins = nc.vector.tensor_scalar(x_sb[:, i], x_sb[:, i], r_final[:, i:i + 1], None, ALU.mult)
            link(m, ins)
            dve.wait_ge(s_pow, m.at("pw", 1))
            nc.vector.tensor_tensor(row_scale[:, 0], r_final, r_mix, ALU.mult).then_inc(s_rs, 1)

            def mixer2(m):
                for g in range(4):
                    if g:
                        ahead(m, 2 * g)
                    ahead(m, 2 * g + 1)
                for n in range(2):
                    turned_low(m, m.start["dt"] + n, slice(8 + 2 * n, 10 + 2 * n), slice(0, S), 2, S)
                ahead(m, T_POOL)
                def masked_max(n):
                    dve.wait_ge(s_sc, m.at("sb", n + 1))
                    link(m, nc.vector.tensor_tensor(probs[:, n % 4], psum[:, n % 4].rearrange(
                        "p (i k) -> p i k", i=NTOK), mask, ALU.add))
                    nc.vector.tensor_reduce(negmax[:, n], probs[:, n % 4], AX.X, ALU.max, negate=True)\
                      .then_inc(s_nm, 1)

                def counted(n):
                    dve.wait_ge(s_pr, m.at("sb", n + 1))
                    for i in range(NTOK):
                        ins = nc.vector.tensor_tensor_reduce(
                            out=probs[:, n % 4, i], in0=probs[:, n % 4, i], in1=count[:, i], scale=1.0, scalar=0.0,
                            op0=ALU.mult, op1=ALU.add, accum_out=rowsum[:, n, i:i + 1])
                    ins.then_inc(s_pw, 1)

                dve.wait_ge(s_big, 16)
                for n in range(3):
                    masked_max(n)
                counted(0)
                rows = [(z_2[:, i], gains[:, G2["pool"][0]:G2["pool"][1]], z_2[:, i], scr[:]) for i in range(NTOK)]
                for n in range(HEADS):
                    if n == 3:
                        squares = send(m, mean_squares(m, [(src, place) for src, _, _, place in rows]))
                    elif n == 5:
                        for ins in gain_rows(m, rows, *squares):
                            pass
                        ins.then_inc(s_mrg, 1)
                    if n + 1 < HEADS:
                        counted(n + 1)
                    turned_probs(m, m.start["p2"] + n, n)
                    if n + 3 < HEADS:
                        masked_max(n + 3)
                divide(m, 0, 0, lambda i: o_2[:, i])
                dve.wait_ge(s_y, YS + 1 if m is span2 else YS + 2)
                rows = [(o_2[:, i], gains[:, G2["attn"][0]:G2["attn"][1]], o_2[:, i], scr[:]) for i in range(NTOK)]
                squares = send(m, mean_squares(m, [(src, place) for src, _, _, place in rows]))
                half_low(m, "y2", 0)
                low(m, T_OUT2 + 1)
                for ins in gain_rows(m, rows, *squares):
                    pass
                ins.then_inc(s_mrg, 1)
                half_low(m, "y2", 1)
                for h in range(2):
                    if h:
                        ahead(m, T_OUT2 + 2 * h)
                    ahead(m, T_OUT2 + 2 * h + 1)
                    accumulate(m, "BA"[h], 2 + h, h, T_OUT2 + 2 * h + 1)

            YS = DEPTH * NBR
            mixer2(span2)
            dve.wait_ge(s_gain2, 48)
            scaled(span2, "ffn", G2["ffn"][0], T_FF2)
            ffn(span2, FF2_STEPS, T_FF2 + 1, D_FF2, 4)
            accumulate(span2, "B", 3, 0, len(tiles2) - 2)
            accumulate(span2, "C", 0, 1, len(tiles2) - 1)
            powers[0] = split_turns[0] = 0
            low(span3, 0)
            dve.wait_ge(s_gain2, 64)
            scaled(span3, "mix", G2["mix"][0], 0)
            mixer2(span3)
            norm_residual(span3, G2["ffn"][0])
            quarter_low(span3, "ffn")

            m = span3
            nc.vector.memset(give, 0.0)
            link(m, nc.vector.memset(psum[:, 2:4], 0.0))
            b = m.bank(m.start["rt"])
            dve.wait_ge(s_tp, m.at("tp", m.start["rt"] + 1))
            logits = route[:, 0:16].rearrange("p (i e) -> p i e", i=NTOK)
            ins = nc.vector.tensor_copy(logits, psum[:, TB[b], 0:16].rearrange("p (i e) -> p i e", i=NTOK))
            ins.then_inc(s_tf[b], 1)
            dve.wait_ge(s_tf[b], m.turned(m.start["rt"]))
            best, place = (route[:, 32 + 16 * k:48 + 16 * k].rearrange("p (i e) -> p i e", i=NTOK) for k in range(2))
            for i in range(NTOK):
                link(m, nc.vector.max(best[:, i], logits[:, i]))
                link(m, nc.vector.max_index(route_i[:], best[:, i], logits[:, i]))
                link(m, nc.vector.tensor_copy(place[:, i], route_i[:]))
                ins = nc.vector.tensor_tensor(route[:, 16 + i:17 + i], best[:, i, 1:2], best[:, i, 0:1], ALU.subtract)
                if i == 0:
                    link(m, ins)
            ins.then_inc(s_rt, 1)
            dve.wait_ge(s_rte, 1)
            e_, w1, w2, tmp = (route[:, k:k + w] for k, w in ((24, 2), (64, 2), (66, 2), (72, 16)))
            link(m, nc.vector.tensor_scalar(w1, e_, 1.0, None, ALU.add))
            link(m, nc.vector.reciprocal(w1, w1))
            link(m, nc.vector.tensor_tensor(w2, e_, w1, ALU.mult))
            names = iota[:, 0:NEXP]
            for i in range(NTOK):
                nc.vector.tensor_scalar(tmp[:, 0:8], names, place[:, i, 0:1], w1[:, i:i + 1], ALU.is_equal, ALU.mult)
                link(m, nc.vector.tensor_scalar(tmp[:, 8:16], names, place[:, i, 1:2], w2[:, i:i + 1],
                                                ALU.is_equal, ALU.mult))
                link(m, nc.vector.tensor_tensor(gate_e[:, :, i], tmp[:, 0:8], tmp[:, 8:16], ALU.add))
                nc.vector.tensor_scalar(tmp[:, 0:8], names, place[:, i, 0:1], None, ALU.is_equal)
                link(m, nc.vector.tensor_scalar(tmp[:, 8:16], names, place[:, i, 1:2], None, ALU.is_equal))
                ins = nc.vector.tensor_tensor(member[:, i], tmp[:, 0:8], tmp[:, 8:16], ALU.add)
                if i == 0:
                    link(m, ins)
            ins.then_inc(s_member, 1)
            b = m.bank(m.start["place"])
            dve.wait_ge(s_tp, m.at("tp", m.start["place"] + 1))
            before = route[:, 0:24]
            nc.vector.tensor_copy(before, psum[:, TB[b], 0:24]).then_inc(s_tf[b], 1)
            dve.wait_ge(s_tf[b], m.turned(m.start["place"]))
            own, prior = route[:, 24:32], route[:, 80:81 + NEXP]
            nc.vector.tensor_scalar(own, before[:, 16:24], float(P), 1.0, ALU.is_gt, ALU.add)
            link(m, nc.vector.memset(prior, 0.0))
            for n in range(1, NEXP + 1):
                link(m, nc.vector.tensor_tensor(prior[:, n:n + 1], prior[:, n - 1:n], own[:, n - 1:n], ALU.add))
            nc.vector.tensor_copy(rounds_i[:, 0, 0:NEXP], own)
            nc.vector.tensor_copy(rounds_i[:, 1], prior).then_inc(s_rounds, 1)
            for i in range(NTOK):
                link(m, nc.vector.scalar_tensor_tensor(out=tmp[:, 0:8], in0=before[:, 8 * i:8 * i + 8], scalar=1.0,
                                                       in1=member[:, i], op0=ALU.add, op1=ALU.mult))
                link(m, nc.vector.tensor_scalar(place_e[:, :, i], tmp[:, 0:8], P - 1.0, None, ALU.add))

            def finish(m, half):
                dve.wait_ge(s_given, m.at("fG", 0))
                dve.wait_ge(s_back, m.turn * 2 + (half + 1))
                for i in range(NTOK):
                    xs = x_sb[:, i, half * W:(half + 1) * W]
                    nc.vector.tensor_tensor(xs, psum[:, SETS["C"][i]], xs, ALU.add).then_inc(s_given, 1)

            def expert(m, e):
                chain["n"] = split_turns[0] = 0
                column = lambda v: v[:, bass.ds(e, 1), :].rearrange("p a i -> p (a i)")
                nc.vector.tensor_copy(gate_c[:], column(gate_e))
                link(m, nc.vector.tensor_copy(place_c[:], column(place_e)))
                link(m, nc.vector.tensor_scalar(place_c[:], place_c[:], -float(P), None, ALU.add))
                for i in range(NTOK):
                    ins = nc.vector.tensor_scalar(sel[:, i], iota, place_c[:, i:i + 1], None, ALU.is_equal)
                ins.then_inc(s_sel, 1)
                for i in range(NTOK):
                    ins = nc.vector.tensor_scalar(sel_w[:, i], iota, place_c[:, i:i + 1], gate_c[:, i:i + 1],
                                                  ALU.is_equal, ALU.mult)
                ins.then_inc(s_sel, 1)
                link(m, nc.vector.tensor_copy(column(place_e), place_c[:]))
                low(m, 0)
                for n in range(2):
                    turned_low(m, m.start["take"] + n, slice(4 * n, 4 * n + 4), slice(0, P), 4, P)
                j, turn = 0, m.start["ff"]
                for kind, g, k in FFE_STEPS:
                    if kind in TILE_STEPS:
                        ahead(m, j)
                        if j < 2:
                            finish(m, j)
                        j += 1
                    elif kind == "act_up":
                        dve.wait_ge(s_used, m.at("used", j))
                        nc.vector.tensor_tensor(ff_a[:, 0], psum[:, 1], ff_s[:, 0], ALU.mult)\
                          .then_inc(s_free["B"], 1)
                    elif kind == "turn":
                        c = 8 + 4 * (g % 2)
                        turned_low(m, turn, slice(c, c + 4), slice(0, P), 4, P)
                        turn += 1
                assert chain["n"] == STEP_EXPERT, chain

            chain.update(base=chain["base"] + chain["n"], rise=STEP_EXPERT)
            def finish_all(m):
                for half in range(2):
                    finish(m, half)
                dve.wait_ge(s_given, m.at("fG", 4))

            rounds(dve, expert, finish_all)
            powers[0] = 0
            dve.wait_ge(s_gain2, 80)
            norm_residual(spang, 0)

        @block.tensor
        def _(pe):
            for key in "ABC":
                pe.sem_inc(s_free[key], NTOK)
            for b in range(2):
                pe.sem_inc(s_tf[b], 1)
            pe.sem_inc(s_given, 1)
            pe.wait_ge(s_in, 32)

            def turn(m, k, blocks):
                b = m.bank(k)
                pe.wait_ge(s_tf[b], m.empty(k))
                for n, src in enumerate(blocks):
                    c = src.shape[-1]
                    ins = nc.tensor.transpose(psum[0:c, TB[b], n * P:(n + 1) * P], src, ident)
                ins.then_inc(s_tp, 1)

            def turned(m, k0, n):
                for k in range(max(k0, k0 + n - 2), k0 + n):
                    pe.wait_ge(s_tf[m.bank(k)], m.turned(k))

            def parts(v, n, w=P):
                return [v[:, k * w:(k + 1) * w] for k in range(n)]

            def free(m, key, use):
                pe.wait_ge(s_free[key], m.at("f" + key, NTOK * use))

            def group(m, j, ntiles, key, use, chunk=0, per=4):
                free(m, key, use)
                for k in range(ntiles):
                    product(m, j + k, key, chunk + per * k, k == 0, k == ntiles - 1)

            def product(m, j, key, chunk, first, last):
                t, (_, n, w) = m.tile(j) % SPLIT, m.tiles[j]
                for half, c0, c1, count in halves(n):
                    pe.wait_ge(s_lo, m.at("lo", j, half + count))
                    for i in range(NTOK):
                        o = psum[:, SETS[key][i], 0:w]
                        for c in range(c0, c1):
                            hh, hl = (hT[:, k, chunk + c, i * P:(i + 1) * P] for k in range(2))
                            wh, wl = (t_[:, t, half, (c - c0) * w:(c - c0 + 1) * w] for t_ in (whi, wlo))
                            nc.tensor.matmul(o, hh, wh, start=first and c == 0, stop=False)
                            nc.tensor.matmul(o, hh, wl, start=False, stop=False)
                            ins = nc.tensor.matmul(o, hl, wh, start=False, stop=last and c == n - 1)
                    ins.then_inc(s_used, count)

            def scaled_turns(m, stage, j, key, use):
                k = 4 * int(stage in ("ln2", "ffn"))
                for c in range(2):
                    for i in range(NTOK):
                        pe.wait_ge(s_xn, m.at("xn", k + 2 * c + i + 1))
                        turn(m, m.start[stage] + 2 * c + i, parts(xn[:, i, c * W:(c + 1) * W], 4))
                    turned(m, m.start[stage] + 2 * c, 2)
                    if c == 0:
                        free(m, key, use)
                        product(m, j, key, 0, True, False)

            def halves_turns(m, stage, before, source, j, key, use):
                for c in range(2):
                    pe.wait_ge(s_mrg, before + (c + 1))
                    for i in range(NTOK):
                        turn(m, m.start[stage] + 2 * c + i, parts(source(i, c), 4))
                    turned(m, m.start[stage] + 2 * c, 2)
                    if c == 0:
                        free(m, key, use)
                    product(m, j + c, key, 4 * c, c == 0, c == 1)

            def norm_turns(m, stage):
                for i in range(NTOK):
                    pe.wait_ge(s_xn, m.at("xn", 4 + i + 1))
                    for c in range(2):
                        turn(m, m.start[stage] + 2 * i + c, parts(xn[:, i, c * W:(c + 1) * W], 4))
                turned(m, m.start[stage], 4)

            def scores(m, n, q, k):
                if n >= 4:
                    pe.wait_ge(s_pr, m.at("sb", n - 3))
                for i in range(NTOK):
                    ins = nc.tensor.matmul(psum[:, n % 4, i * S:(i + 1) * S], q[:, i * P:(i + 1) * P], k,
                                           start=True, stop=True)
                ins.then_inc(s_sc, 1)

            def probs_turn(m, k, n):
                turn(m, k, [probs[:, n % 4, i, kb * P:(kb + 1) * P] for kb in range(2) for i in range(NTOK)])

            def values(m, k, h, v, done):
                pe.wait_ge(s_tf[m.bank(k)], m.turned(k))
                for i in range(NTOK):
                    for kb in range(2):
                        ins = nc.tensor.matmul(psum[:, SETS["C"][i], h * HV:(h + 1) * HV],
                                               probsT[:, h % 2, kb, i * P:(i + 1) * P], v(kb),
                                               start=kb == 0, stop=kb == 1)
                if done:
                    ins.then_inc(s_o, 1)

            def attend(m, n0, stage, q, k, v, per, ready):
                lead = 3 if per == 1 else 2
                for h in range(lead):
                    for b in range(per):
                        scores(m, n0 + per * h + b, q(h, b), k(h, b))
                for h in range(HEADS):
                    pe.wait_ge(*ready(h))
                    probs_turn(m, m.start[stage] + h, n0 + per * h)
                    if h + lead < HEADS:
                        for b in range(per):
                            scores(m, n0 + per * (h + lead) + b, q(h + lead, b), k(h + lead, b))
                    if h:
                        values(m, m.start[stage] + h - 1, h - 1, v(h - 1), False)
                values(m, m.start[stage] + HEADS - 1, HEADS - 1, v(HEADS - 1), True)

            def ffn(m, steps, j, hidden, a0, b0, c0):
                use, turns = a0, m.start["ff"]
                last = -(-hidden // W) - 1
                for kind, g, k in steps[1:]:
                    w = min(W, hidden - g * W)
                    if kind in ("gate", "up"):
                        if k == 0:
                            free(m, "A", use)
                        product(m, j, "A", 4 * k, k == 0, k == 1)
                        j += 1
                    elif kind in ("act_gate", "act_up"):
                        use += 1
                    elif kind == "turn":
                        pe.wait_ge(s_free["A"], m.at("fA", NTOK * use))
                        for i in range(NTOK):
                            turn(m, turns, parts(ff_a[:, i], w // P))
                            turns += 1
                    elif kind == "down":
                        key = "BC"[k]
                        if g == 0:
                            free(m, key, (b0, c0)[k])
                        if k == 0:
                            turned(m, turns - 2, 2)
                        product(m, j, key, 8 + 4 * (g % 2), g == 0, g == last)
                        j += 1

            with pe.Fori(0, DEPTH) as r:
                m = span1(r)
                scaled_turns(m, "ln1", 0, "A", 0)
                product(m, 1, "A", 4, False, True)
                for g in range(1, 12):
                    group(m, 2 * g, 2, "AB"[g % 2], g // 2)
                pe.wait_ge(s_prep, m.at("prep", 1))
                for i in range(NTOK):
                    turn(m, m.start["cc"] + 2 * i, parts(mix[:, i, OC_Q:], 3))
                    turn(m, m.start["cc"] + 2 * i + 1, parts(mix[:, i, OC_KV:], 2))
                turned(m, m.start["cc"], 4)
                for g in range(2):
                    group(m, T_UQ + g, 1, "AB"[g], 6)
                for g in range(2):
                    group(m, T_UKV + 2 * g, 2, "AB"[g], 7, chunk=3, per=1)
                pe.wait_ge(s_prep, m.at("prep", 2))
                for i in range(NTOK):
                    turn(m, m.start["qa"] + i, parts(mix[:, i, 0:], 4))
                for i in range(NTOK):
                    turn(m, m.start["ka"] + i, parts(mix[:, i, OA_K:], 1))
                pe.wait_ge(s_prep, m.at("prep", 3))
                for i in range(NTOK):
                    turn(m, m.start["qb"] + i, parts(mix[:, i, OB_Q:], 4))
                for i in range(NTOK):
                    turn(m, m.start["kb"] + i, parts(mix[:, i, OB_K:], 4))
                for key, use in (("A", 8), ("B", 8), ("C", 0)):
                    free(m, key, use)
                turned(m, m.start["qa"], 8)
                hp = lambda h: slice(64 * (h // 4), 64 * (h // 4) + 64)
                attend(m, 0, "pa", lambda h, b: qT_a[hp(h), h % 4], lambda h, b: kT_a[hp(h), 0],
                       lambda h: lambda kb: mix[:, kb, OA_V + HV * (h // 4):OA_V + HV * (h // 4) + HV],
                       1, lambda h: (s_pr, m.at("sb", h + 1)))
                pe.wait_ge(s_y, m.at("br", 1))
                cp = lambda h, b: slice(32 * ((2 * h + b) % 4), 32 * ((2 * h + b) % 4) + 32)
                attend(m, 8, "pb", lambda h, b: qT_b[cp(h, b), h // 2], lambda h, b: kT_b[cp(h, b), h // 2],
                       lambda h: lambda kb: mix[:, kb, OB_V + HV * h:OB_V + HV * (h + 1)],
                       2, lambda h: (s_pw, m.turn * B_HEADS + (h + 1)))
                pe.wait_ge(s_prep, m.at("prep", 4))
                for stage, v in (("qc", q_c), ("kc", k_c)):
                    for n in range(4):
                        i, c = n // 2, n % 2
                        turn(m, m.start[stage] + n, parts(v[:, i, 4 * c * C_DIM:], 4, C_DIM))
                turned(m, m.start["kc"], 4)
                pe.wait_ge(s_y, m.at("br", 2))
                attend(m, 24, "pc", lambda h, b: qT_c[0:C_DIM, h], lambda h, b: kT_c[0:C_DIM, h],
                       lambda h: lambda kb: v_c[:, kb, HV * h:HV * (h + 1)],
                       1, lambda h: (s_pr, m.at("sb", 24 + h + 1)))
                pe.wait_ge(s_y, m.at("br", 3))
                for n, o in enumerate((0, OB_Q, OB_K)):
                    for i in range(NTOK):
                        turn(m, m.start["y"] + 2 * n + i, parts(mix[:, i, o:], 4))
                turned(m, m.start["y"], 6)
                for n in range(NBR):
                    for h in range(2):
                        group(m, T_BR + 2 * n + h, 1, "AB"[h], 8 + n, chunk=4 * n)
                halves_turns(m, "mrg", m.turn * 2, lambda i, c: merged[:, i, c * W:], T_OUT, "A", 11)
                group(m, T_OUT + 2, 2, "B", 11)
                scaled_turns(m, "ln2", T_FF, "A", 12)
                ffn(m, FF1_STEPS, T_FF + 1, D_FF, 12, 12, 0)

            def mixer2(m, n):
                scaled_turns(m, "mix", 0, "A", 0)
                product(m, 1, "A", 4, False, True)
                for g in range(1, 4):
                    group(m, 2 * g, 2, "AB"[g % 2], g // 2)
                free(m, "A", 2)
                free(m, "B", 2)
                pe.wait_ge(s_big, 16)
                for t in range(2):
                    b = m.bank(m.start["dt"] + t)
                    pe.wait_ge(s_tf[b], m.empty(m.start["dt"] + t))
                    for g in range(2):
                        for i in range(NTOK):
                            c = (2 * t + g) * P
                            ins = nc.tensor.matmul(psum[:, TB[b], g * S:(g + 1) * S], mix2[:, i, c:c + P],
                                                   poolT[:, i, 2 * t + g], start=i == 0, stop=i == 1)
                    ins.then_inc(s_tp, 1)
                turned(m, m.start["dt"], 2)
                pe.wait_ge(s_lo, m.at("lo", T_POOL + 1))
                w_buf = m.tile(T_POOL) % SPLIT
                for i in range(NTOK):
                    for g in range(4):
                        o = psum[:, SETS["A"][i], g * P:(g + 1) * P]
                        hh, hl = (hT[:, k, 8 + g, i * P:(i + 1) * P] for k in range(2))
                        wh, wl = (t_[:, w_buf, g // 2, g % 2 * P:(g % 2 + 1) * P] for t_ in (whi, wlo))
                        nc.tensor.matmul(o, hh, wh, start=True, stop=False)
                        nc.tensor.matmul(o, hh, wl, start=False, stop=False)
                        ins = nc.tensor.matmul(o, hl, wh, start=False, stop=True)
                ins.then_inc(s_used, 2)
                for stage, o in (("q2", W), ("k2", 2 * W)):
                    for i in range(NTOK):
                        turn(m, m.start[stage] + i, parts(mix2[:, i, o:], 4))
                turned(m, m.start["q2"], 4)
                for key, use in (("A", 3), ("B", 2), ("C", 0)):
                    free(m, key, use)
                hp = lambda h: slice(64 * (h % 2), 64 * (h % 2) + 64)
                attend(m, 0, "p2", lambda h, b: qT_2[hp(h), h // 2], lambda h, b: kT_2[hp(h), h // 2],
                       lambda h: lambda kb: mix2[:, kb, 3 * W + HV * h:3 * W + HV * (h + 1)],
                       1, lambda h: (s_pw, DEPTH * B_HEADS + n * HEADS + h + 1))
                halves_turns(m, "y2", DEPTH * 2 + 2 * n, lambda i, c: (z_2, o_2)[c][:, i], T_OUT2, "B", 2)
                group(m, T_OUT2 + 2, 2, "A", 3)

            mixer2(span2, 0)
            scaled_turns(span2, "ffn", T_FF2, "A", 4)
            ffn(span2, FF2_STEPS, T_FF2 + 1, D_FF2, 4, 3, 0)
            mixer2(span3, 1)
            norm_turns(span3, "ffn")
            m = span3
            b = m.bank(m.start["rt"])
            pe.wait_ge(s_wr, 16)
            pe.wait_ge(s_tf[b], m.empty(m.start["rt"]))
            for i in range(NTOK):
                for c in range(KD):
                    for k in range(2):
                        ins = nc.tensor.matmul(psum[:, TB[b], i * NEXP:(i + 1) * NEXP],
                                               hT[:, k, c, i * P:(i + 1) * P].bitcast(F32), w_route[:, c],
                                               start=c == 0 and k == 0, stop=c == KD - 1 and k == 1)
            ins.then_inc(s_tp, 1)
            b = m.bank(m.start["place"])
            pe.wait_ge(s_member, 1)
            pe.wait_ge(s_tf[b], m.empty(m.start["place"]))
            for n, terms in enumerate((((earlier, 0),), ((ones, 0), (earlier, 1)), ((ones, 0), (ones, 1)))):
                for k, (before, i) in enumerate(terms):
                    ins = nc.tensor.matmul(psum[:, TB[b], n * NEXP:(n + 1) * NEXP], before, member[:, i],
                                           start=k == 0, stop=k == len(terms) - 1)
            ins.then_inc(s_tp, 1)

            def slots(m, j, bank, chunk, first, last):
                t, (_, n, w) = m.tile(j) % SPLIT, m.tiles[j]
                for half, c0, c1, count in halves(n):
                    pe.wait_ge(s_lo, m.at("lo", j, half + count))
                    for c in range(c0, c1):
                        hh, hl = (hT[:, k, chunk + c, 0:P] for k in range(2))
                        wh, wl = (t_[:, t, half, (c - c0) * w:(c - c0 + 1) * w] for t_ in (whi, wlo))
                        nc.tensor.matmul(psum[:, bank], hh, wh, start=first and c == 0, stop=False)
                        nc.tensor.matmul(psum[:, bank], hh, wl, start=False, stop=False)
                        ins = nc.tensor.matmul(psum[:, bank], hl, wh, start=False, stop=last and c == n - 1)
                    ins.then_inc(s_used, count)

            def finish(m, half):
                pe.wait_ge(s_free["C"], m.at("fC", half + 1))
                pe.wait_ge(s_given, m.at("fG", 2 * half))
                for i in range(NTOK):
                    ins = nc.tensor.matmul(psum[:, SETS["C"][i]], give[:, i], y_e[:, half * W:(half + 1) * W],
                                           start=True, stop=True)
                ins.then_inc(s_back, 1)

            def expert(m, e):
                pe.wait_ge(s_sel, m.turn * 2 + 1)
                for n in range(2):
                    b = m.bank(m.start["take"] + n)
                    pe.wait_ge(s_tf[b], m.empty(m.start["take"] + n))
                    for c in range(4):
                        f = (4 * n + c) * P
                        for i in range(NTOK):
                            ins = nc.tensor.matmul(psum[:, TB[b], c * P:(c + 1) * P], xn[:, i, f:f + P], sel[:, i],
                                                   start=i == 0, stop=i == NTOK - 1)
                    ins.then_inc(s_tp, 1)
                turned(m, m.start["take"], 2)
                j, turns, last = 0, m.start["ff"], D_FFE // W - 1
                for kind, g, k in FFE_STEPS:
                    if kind in ("gate", "up"):
                        if k == 0:
                            key = "AB"[kind == "up"]
                            pe.wait_ge(s_free[key], m.at("f" + key, g))
                        slots(m, j, int(kind == "up"), 4 * k, k == 0, k == 1)
                        if j < 2:
                            finish(m, j)
                        if j == 1:
                            pe.wait_ge(s_sel, m.turn * 2 + 2)
                            turn(m, m.start["give"], [sel_w[:, i] for i in range(NTOK)])
                        j += 1
                    elif kind == "turn":
                        pe.wait_ge(s_free["B"], m.at("fB", g + 1))
                        turn(m, turns, parts(ff_a[:, 0], 4))
                        turns += 1
                    elif kind == "down":
                        if k == 0:
                            pe.wait_ge(s_tf[m.bank(turns - 1)], m.turned(turns - 1))
                        slots(m, j, 2 + k, 8 + 4 * (g % 2), g == 0, g == last)
                        j += 1

            rounds(pe, expert, lambda m: [finish(m, half) for half in range(2)])


DIRECT = ["x", "w_in", "c_w_uq", "c_w_ukv", "w_branch", "w_out", "w_ff1", "w_ff2", "final_g", "w_in_2", "w_pool_2",
          "w_out_2", "ffn_wg_2", "ffn_wu_2", "ffn_wd_2", "w_router_2", "moe_wg_2", "moe_wu_2", "moe_wd_2",
          "final_norm_2"]


def kernel(**inputs):
    import concourse.bacc as bacc
    from concourse.bass_utils import run_bass_kernel_spmd

    nc = bacc.Bacc("TRN2", target_bir_lowering=False, num_devices=1)
    arrays = {n: np.ascontiguousarray(inputs[n]) for n in DIRECT}
    init = [0.8 - 0.6 * math.exp(-0.3 * l) for l in range(DEPTH)]
    rows = [inputs[n].reshape(DEPTH, -1) for n in ("ln1_g", "ln2_g", "a_q_norm", "a_k_norm", "b_subln", "c_q_norm",
                                                   "c_kv_norm", "b_lambda")]
    rows.append(np.array([[v, 1.0 - v] for v in init], np.float32))
    arrays["gains1"] = np.ascontiguousarray(np.concatenate(rows, 1))
    arrays["gains2"] = np.ascontiguousarray(np.concatenate(
        [inputs[n] for n in ("norm_mix_2", "pool_scale_2", "attn_gain_2", "norm_ffn_2")], 1))
    arrays["tables"], arrays["big"] = make_tables()
    args = {n: nc.dram_tensor(f"in_{n}", v.shape, mybir.dt.from_np(v.dtype), kind="ExternalInput").ap()
            for n, v in arrays.items()}
    out = nc.dram_tensor("out_0", (1, S, D), F32, kind="ExternalOutput").ap()
    build(nc, args, out)
    r = run_bass_kernel_spmd(nc, [{f"in_{n}": v for n, v in arrays.items()}], core_ids=[0])
    return r.results[0]["out_0"]
```
